# Optimizing a Trainium2 kernel written in Bass

```python
import math
import jax, jax.numpy as jnp
from jax import lax
import numpy as np

D_MODEL = 1024
BATCH = 1
SEQ = 2048
DEPTH = 1
DEC_BATCH = 1
DEC_SEQ = 32
PAST_LEN = 256

CHUNK = 64
N_META = 16
META_PAD = (-N_META) % CHUNK
HEAD_DIM = 64
A_HEADS = D_MODEL // 128
A_KV_HEADS = A_HEADS // 4
A_GROUP = A_HEADS // A_KV_HEADS
WINDOW = 128
WIN_CHUNKS = WINDOW // CHUNK
B_HEADS = D_MODEL // 256
SB_BLOCK = 128
C_HEADS = D_MODEL // 256
C_DK = HEAD_DIM
C_DV = HEAD_DIM
CONV_W = 4
GDN_CHUNK = 64
D_A = A_HEADS * HEAD_DIM
D_KV_A = A_KV_HEADS * HEAD_DIM
D_B = B_HEADS * HEAD_DIM
D_C = C_HEADS * C_DV
D_MIX = D_A + D_B + D_C
C_CONV = C_HEADS * (2 * C_DK + C_DV)
N_IN = D_A + 2 * D_KV_A + 3 * D_B + C_CONV + 2 * C_HEADS + D_MIX
RMS_EPS = 1e-6
NEG = -1e30

kernel_name = "hybrid_stream_swa_sb_gdn_step"

def rmsnorm(x, gain):
    xf = x.astype(jnp.float32)
    y = xf * lax.rsqrt(jnp.mean(xf * xf, axis=-1, keepdims=True) + RMS_EPS)
    return (y * gain.astype(jnp.float32)).astype(x.dtype)

def l2norm(x):
    return x * lax.rsqrt(jnp.sum(x * x, axis=-1, keepdims=True) + 1e-6)

def mixer_inputs(h, g_pre, w_in):
    b, t = h.shape[:2]
    u = jnp.einsum('btd,dn->btn', rmsnorm(h, g_pre), w_in)
    sizes = (D_A, D_KV_A, D_KV_A, D_B, D_B, D_B, C_CONV, C_HEADS, C_HEADS, D_MIX)
    cuts = [sum(sizes[:i + 1]) for i in range(len(sizes) - 1)]
    qa, ka, va, qb, kb, vb, xc, ac, bc, z = jnp.split(u, cuts, axis=-1)
    heads = lambda a, n: a.reshape(b, t, n, HEAD_DIM)
    return (heads(qa, A_HEADS), heads(ka, A_KV_HEADS), heads(va, A_KV_HEADS),
            heads(qb, B_HEADS), heads(kb, B_HEADS), heads(vb, B_HEADS), xc, ac, bc, z)

def mixer_output(h, o_a, o_b, o_c, z, g_post, w_out):
    o = jnp.concatenate([o_a, o_b, o_c], axis=-1) * jax.nn.silu(z)
    return h + rmsnorm(jnp.einsum('btm,md->btd', o, w_out), g_post)

def sink_attention(q, k, v, sinks, key_ok):
    s = jnp.einsum('bcqkgd,bcskd->bckgqs', q, k, preferred_element_type=jnp.float32) * (HEAD_DIM ** -0.5)
    s = jnp.where(key_ok[None, :, None, None, None, :], s, NEG)
    sink = jnp.broadcast_to(sinks.astype(jnp.float32).reshape(A_KV_HEADS, A_GROUP)[None, None, :, :, None, None],
                            s.shape[:-1] + (1,))
    p = jax.nn.softmax(jnp.concatenate([s, sink], axis=-1), axis=-1)[..., :-1]
    return jnp.einsum('bckgqs,bcskd->bcqkgd', p.astype(v.dtype), v)

def swa_prompt(q, k, v, sinks):
    b, t = q.shape[:2]
    n_c = (t + META_PAD) // CHUNK
    qc = jnp.pad(q, ((0, 0), (META_PAD, 0), (0, 0), (0, 0))).reshape(b, n_c, CHUNK, A_KV_HEADS, A_GROUP, HEAD_DIM)
    lead = META_PAD + WIN_CHUNKS * CHUNK
    to_chunks = lambda a: jnp.pad(a, ((0, 0), (lead, 0), (0, 0), (0, 0))).reshape(
        b, n_c + WIN_CHUNKS, CHUNK, A_KV_HEADS, HEAD_DIM)
    band = lambda a: jnp.concatenate([a[:, j:j + n_c] for j in range(WIN_CHUNKS + 1)], axis=2)
    k_band = band(to_chunks(k))
    v_band = band(to_chunks(v))
    ok = (jnp.arange((n_c + WIN_CHUNKS) * CHUNK) >= lead).reshape(n_c + WIN_CHUNKS, CHUNK)
    ok = jnp.concatenate([ok[j:j + n_c] for j in range(WIN_CHUNKS + 1)], axis=1)
    o = sink_attention(qc, k_band, v_band, sinks, ok)
    return o.reshape(b, n_c * CHUNK, D_A)[:, META_PAD:]

def swa_sample(q, k, v, cache_k, cache_v, sinks):
    b, t = q.shape[:2]
    n_keep = cache_k.shape[1]
    k_all = jnp.concatenate([cache_k, k], axis=1)
    v_all = jnp.concatenate([cache_v, v], axis=1)
    ok = jnp.ones((1, k_all.shape[1]), dtype=bool)
    o = sink_attention(q.reshape(b, 1, t, A_KV_HEADS, A_GROUP, HEAD_DIM), k_all[:, None], v_all[:, None], sinks, ok)
    return o.reshape(b, t, D_A), k_all[:, -n_keep:], v_all[:, -n_keep:]

def stick_breaking(q, k, v, q_pos, k_pos):
    z = jnp.einsum('bqhd,bkhd->bhqk', q, k, preferred_element_type=jnp.float32) * (HEAD_DIM ** -0.5)
    visible = k_pos[None, :] < q_pos[:, None]
    log_beta = jax.nn.log_sigmoid(z)
    log_keep = jnp.where(visible, jax.nn.log_sigmoid(-z), 0.0)
    later = lax.cumsum(log_keep, axis=3, reverse=True) - log_keep
    w = jnp.where(visible, jnp.exp(log_beta + later), 0.0)
    return jnp.einsum('bhqk,bkhd->bqhd', w.astype(v.dtype), v)

def sb_prompt(q, k, v):
    b, t = q.shape[:2]
    n_blk = -(-t // SB_BLOCK)
    pad = n_blk * SB_BLOCK - t
    pz = lambda a: jnp.pad(a, ((0, 0), (0, pad), (0, 0), (0, 0)))
    qp, kp, vp = pz(q), pz(k), pz(v)
    pos = jnp.arange(n_blk * SB_BLOCK)
    q_blocks = qp.reshape(b, n_blk, SB_BLOCK, B_HEADS, HEAD_DIM).transpose(1, 0, 2, 3, 4)
    o = lax.map(lambda a: stick_breaking(a[0], kp, vp, a[1], pos), (q_blocks, pos.reshape(n_blk, SB_BLOCK)))
    return o.transpose(1, 0, 2, 3, 4).reshape(b, n_blk * SB_BLOCK, D_B)[:, :t]

def sb_sample(q, k, v, cache_k, cache_v):
    b, t = q.shape[:2]
    past = cache_k.shape[1]
    k_all = jnp.concatenate([cache_k, k], axis=1)
    v_all = jnp.concatenate([cache_v, v], axis=1)
    o = stick_breaking(q, k_all, v_all, past + jnp.arange(t), jnp.arange(past + t))
    return o.reshape(b, t, D_B)

def depthwise_causal_conv(x_hist, w):
    return lax.conv_general_dilated(x_hist, w.astype(x_hist.dtype)[:, None, :], window_strides=(1,),
                                    padding='VALID', dimension_numbers=('NWC', 'WIO', 'NWC'),
                                    feature_group_count=w.shape[1])

def gated_delta_chunked(q, k, v, g, beta, s0, blk):
    b, t, h, _ = q.shape
    n = t // blk
    to_blocks = lambda a: a.reshape(b, n, blk, h, -1).transpose(1, 0, 3, 2, 4)
    q, k, v = to_blocks(q), to_blocks(k), to_blocks(v)
    g = to_blocks(g[..., None])[..., 0]
    beta = to_blocks(beta[..., None])[..., 0]
    gc = jnp.cumsum(g, axis=-1)
    incl = jnp.tril(jnp.ones((blk, blk), dtype=bool))
    strict = jnp.tril(jnp.ones((blk, blk), dtype=bool), -1)
    decay = jnp.exp(jnp.where(incl, gc[..., :, None] - gc[..., None, :], NEG))
    kb = k * beta[..., None]
    a_mat = jnp.where(strict, jnp.einsum('nbhid,nbhjd->nbhij', kb, k) * decay, 0.0)
    rhs = jnp.concatenate([v * beta[..., None], kb * jnp.exp(gc)[..., None]], axis=-1)
    sol = lax.linalg.triangular_solve(a_mat + jnp.eye(blk, dtype=jnp.float32), rhs, left_side=True,
                                      lower=True, unit_diagonal=True)
    u, w = sol[..., :C_DV], sol[..., C_DV:]
    qk = jnp.einsum('nbhid,nbhjd->nbhij', q, k) * decay
    q_dec = q * jnp.exp(gc)[..., None]
    k_dec = k * jnp.exp(gc[..., -1:] - gc)[..., None]
    g_last = jnp.exp(gc[..., -1])

    def step(s, xs):
        u_i, w_i, qk_i, qd_i, kd_i, gl_i = xs
        v_new = u_i - jnp.einsum('bhik,bhkv->bhiv', w_i, s)
        o_i = jnp.einsum('bhik,bhkv->bhiv', qd_i, s) + jnp.einsum('bhij,bhjv->bhiv', qk_i, v_new)
        s = s * gl_i[..., None, None] + jnp.einsum('bhik,bhiv->bhkv', kd_i, v_new)
        return s, o_i

    s, o = lax.scan(step, s0, (u, w, qk, q_dec, k_dec, g_last))
    return o.transpose(1, 0, 3, 2, 4).reshape(b, t, h, C_DV), s

def gdn_mixer(x_raw, a_raw, b_raw, conv_hist, s0, conv_w, a_log, dt_bias, o_norm):
    b, t = x_raw.shape[:2]
    hist = jnp.concatenate([conv_hist.astype(x_raw.dtype), x_raw], axis=1)
    new_hist = hist[:, -(CONV_W - 1):]
    y = jax.nn.silu(depthwise_causal_conv(hist, conv_w)).astype(jnp.float32)
    q, k, v = jnp.split(y, [C_HEADS * C_DK, 2 * C_HEADS * C_DK], axis=-1)
    q = l2norm(q.reshape(b, t, C_HEADS, C_DK)) * (C_DK ** -0.5)
    k = l2norm(k.reshape(b, t, C_HEADS, C_DK))
    v = v.reshape(b, t, C_HEADS, C_DV)
    g = -jnp.exp(a_log.astype(jnp.float32)) * jax.nn.softplus(a_raw.astype(jnp.float32) + dt_bias.astype(jnp.float32))
    beta = jax.nn.sigmoid(b_raw.astype(jnp.float32))
    blk = min(GDN_CHUNK, t)
    pad = (-t) % blk
    padt = lambda a: jnp.pad(a, ((0, 0), (0, pad)) + ((0, 0),) * (a.ndim - 2))
    o, s = gated_delta_chunked(padt(q), padt(k), padt(v), padt(g), padt(beta), s0.astype(jnp.float32), blk)
    o = rmsnorm(o[:, :t], o_norm)
    return o.reshape(b, t, D_C).astype(x_raw.dtype), new_hist, s

def setup_inputs(seed: int = 0) -> dict:
    key = jax.random.key(seed)
    ks = jax.random.split(key, 20)
    f32 = jnp.float32
    win_rows = min(WINDOW, PAST_LEN)
    nrm = lambda k, shape, scale: scale * jax.random.normal(k, shape, f32)
    dt = jnp.exp(jax.random.uniform(ks[15], (DEPTH, C_HEADS), f32, math.log(1e-3), math.log(1e-1)))
    return {
        'x_prompt': nrm(ks[0], (BATCH, SEQ, D_MODEL), 1.0),
        'x_sample': nrm(ks[1], (DEC_BATCH, DEC_SEQ, D_MODEL), 1.0),
        'cache_a_k': nrm(ks[2], (DEPTH, DEC_BATCH, win_rows, A_KV_HEADS, HEAD_DIM), 1.0),
        'cache_a_v': nrm(ks[3], (DEPTH, DEC_BATCH, win_rows, A_KV_HEADS, HEAD_DIM), 1.0),
        'cache_b_k': nrm(ks[4], (DEPTH, DEC_BATCH, PAST_LEN, B_HEADS, HEAD_DIM), 1.0),
        'cache_b_v': nrm(ks[5], (DEPTH, DEC_BATCH, PAST_LEN, B_HEADS, HEAD_DIM), 1.0),
        'state_c_conv': nrm(ks[6], (DEPTH, DEC_BATCH, CONV_W - 1, C_CONV), 1.0),
        'state_c_ssm': nrm(ks[7], (DEPTH, DEC_BATCH, C_HEADS, C_DK, C_DV), 0.1),
        'meta_tokens': nrm(ks[8], (N_META, D_MODEL), 1.0),
        'norm_pre': 1.0 + nrm(ks[9], (DEPTH, D_MODEL), 0.02),
        'norm_post': 1.0 + nrm(ks[10], (DEPTH, D_MODEL), 0.02),
        'w_in': nrm(ks[11], (DEPTH, D_MODEL, N_IN), D_MODEL ** -0.5),
        'w_out': nrm(ks[12], (DEPTH, D_MIX, D_MODEL), D_MIX ** -0.5),
        'sinks_a': nrm(ks[13], (DEPTH, A_HEADS), 0.5),
        'conv_c': nrm(ks[14], (DEPTH, CONV_W, C_CONV), CONV_W ** -0.5),
        'a_log_c': jnp.log(jax.random.uniform(ks[16], (DEPTH, C_HEADS), f32, 1.0, 16.0)),
        'dt_bias_c': dt + jnp.log(-jnp.expm1(-dt)),
        'onorm_c': 1.0 + nrm(ks[17], (DEPTH, C_DV), 0.02),
    }

def reference(x_prompt, x_sample, cache_a_k, cache_a_v, cache_b_k, cache_b_v, state_c_conv, state_c_ssm,
              meta_tokens, norm_pre, norm_post, w_in, w_out, sinks_a, conv_c, a_log_c, dt_bias_c, onorm_c):
    bp = x_prompt.shape[0]
    win_rows = cache_a_k.shape[2]
    hp = jnp.concatenate([jnp.broadcast_to(meta_tokens.astype(x_prompt.dtype)[None], (bp, N_META, D_MODEL)),
                          x_prompt], axis=1)
    hs = x_sample
    p_ak, p_av, p_bk, p_bv, p_cc, p_cs = [], [], [], [], [], []
    s_ak, s_av, s_bk, s_bv, s_cc, s_cs = [], [], [], [], [], []
    for l in range(DEPTH):
        qa, ka, va, qb, kb, vb, xc, ac, bc, z = mixer_inputs(hp, norm_pre[l], w_in[l])
        o_a = swa_prompt(qa, ka, va, sinks_a[l])
        o_b = sb_prompt(qb, kb, vb)
        o_c, conv_new, ssm_new = gdn_mixer(xc, ac, bc, jnp.zeros((bp, CONV_W - 1, C_CONV), xc.dtype),
                                           jnp.zeros((bp, C_HEADS, C_DK, C_DV), jnp.float32),
                                           conv_c[l], a_log_c[l], dt_bias_c[l], onorm_c[l])
        hp = mixer_output(hp, o_a, o_b, o_c, z, norm_post[l], w_out[l])
        p_ak.append(ka[:, -win_rows:])
        p_av.append(va[:, -win_rows:])
        p_bk.append(kb)
        p_bv.append(vb)
        p_cc.append(conv_new)
        p_cs.append(ssm_new)
        qa, ka, va, qb, kb, vb, xc, ac, bc, z = mixer_inputs(hs, norm_pre[l], w_in[l])
        o_a, ak_new, av_new = swa_sample(qa, ka, va, cache_a_k[l], cache_a_v[l], sinks_a[l])
        o_b = sb_sample(qb, kb, vb, cache_b_k[l], cache_b_v[l])
        o_c, conv_new, ssm_new = gdn_mixer(xc, ac, bc, state_c_conv[l], state_c_ssm[l],
                                           conv_c[l], a_log_c[l], dt_bias_c[l], onorm_c[l])
        hs = mixer_output(hs, o_a, o_b, o_c, z, norm_post[l], w_out[l])
        s_ak.append(ak_new)
        s_av.append(av_new)
        s_bk.append(kb)
        s_bv.append(vb)
        s_cc.append(conv_new)
        s_cs.append(ssm_new)
    y_prompt = hp[:, N_META:]
    y_sample = hs
    p_a_k, p_a_v = jnp.stack(p_ak), jnp.stack(p_av)
    p_b_k, p_b_v = jnp.stack(p_bk), jnp.stack(p_bv)
    p_c_conv, p_c_ssm = jnp.stack(p_cc), jnp.stack(p_cs)
    s_a_k, s_a_v = jnp.stack(s_ak), jnp.stack(s_av)
    s_b_k, s_b_v = jnp.stack(s_bk), jnp.stack(s_bv)
    s_c_conv, s_c_ssm = jnp.stack(s_cc), jnp.stack(s_cs)
    return (y_prompt, y_sample, p_a_k, p_a_v, p_b_k, p_b_v, p_c_conv, p_c_ssm,
            s_a_k, s_a_v, s_b_k, s_b_v, s_c_conv, s_c_ssm)


_drawn_inputs = setup_inputs


def setup_inputs(seed=0):
    import zlib

    import numpy as np

    out = dict(_drawn_inputs(seed))
    spreads = {}
    factors = {}
    for name, (base, spread) in spreads.items():
        noise = np.random.default_rng([zlib.crc32(name.encode()), seed]).standard_normal(out[name].shape)
        drawn = base * np.exp(spread * noise) if base else spread * noise
        out[name] = __import__('jax').numpy.asarray(drawn.astype(out[name].dtype))
    for name, factor in factors.items():
        out[name] = (out[name] * factor).astype(out[name].dtype)
    return out
```

```python
from contextlib import ExitStack

import numpy as np
import concourse.bass as bass
from concourse import mybir

F32 = mybir.dt.float32
BF16 = mybir.dt.bfloat16
ALU = mybir.AluOpType
ACT = mybir.ActivationFunctionType
AX = mybir.AxisListType

P = 128
D = 1024
KT = D // P
SEQ, NMETA, NSAMP, PAST, WIN = 2048, 16, 32, 256, 128
CH = 64
HD = 64
PAD = CH - NMETA
ROW0 = CH
SROW = ROW0 + SEQ
TILES = -(-(SROW + NSAMP) // P)
T = TILES * P
LAST = TILES - 1
SP0 = SROW - LAST * P
AH, AKV, BH, CHD = 8, 2, 4, 4
AG = AH // AKV
QA, KA, VA, QB, KB, VB, XC = 0, 512, 640, 768, 1024, 1280, 1536
AB, ZZ = 2304, 2312
NIN = 3336
VAW, VBW, ABW = 128, 256, 8
RV = VAW + VBW + ABW
SCALE = HD ** -0.5
NEG = -1e30
BLOCKS = [(512 * b, min(512, T - 512 * b)) for b in range(-(-T // 512))]
NBLK = len(BLOCKS)
LEVELS = 6
C_ID, C_TRI, C_BLK, C_LO, C_HI, C_LVL = 0, 128, 256, 384, 512, 640
C_EPS = C_LVL + LEVELS * P
C_ONE = C_EPS + 1
NCF = C_EPS + 2
M_ID, M_DT, M_A0, M_A1, M_A, M_B, M_PAD = 0, 128, 256, 384, 640, 896, 1024
NCB = M_PAD + 128


def shape_constants():
    r = np.arange(P)
    same = r[:, None] // CH == r[None, :] // CH
    cf = np.zeros((P, NCF), np.float32)
    cf[:, C_ID:C_ID + P] = np.eye(P)
    cf[:, C_TRI:C_TRI + P] = same & (r[:, None] <= r[None, :])
    cf[:, C_BLK:C_BLK + P] = same
    cf[:, C_LO:C_LO + P] = (r < CH)[:, None]
    cf[:, C_HI:C_HI + P] = (r >= CH)[:, None]
    for lv in range(LEVELS):
        s = 1 << lv
        j, i = r[:, None], r[None, :]
        cf[:, C_LVL + lv * P:C_LVL + (lv + 1) * P] = (j // (2 * s) == i // (2 * s)) & (j % (2 * s) < s) & (i % (2 * s) >= s)
    cf[:, C_EPS] = 1e-6
    cf[:, C_ONE] = 1.0
    cb = np.zeros((P, NCB), np.float32)
    cb[:, M_ID:M_ID + P] = np.eye(P)
    cb[:, M_DT:M_DT + P] = np.where(same & (r[:, None] <= r[None, :]), 0, NEG)
    q, k = r[:, None], np.arange(2 * P)[None, :]
    win = np.where(q < CH, k < 3 * CH, k >= CH)
    cb[:, M_A:M_A + 2 * P] = np.where(win, 0, NEG)
    cb[:, M_A1:M_A1 + 2 * P] = np.where(win & (k >= PAD), 0, NEG)
    cb[:, M_A0:M_A0 + P] = np.where(win[:, P:] & (k[:, :P] >= PAD), 0, NEG)
    cb[:, M_B:M_B + P] = np.where(r[None, :] < r[:, None], 0, NEG)
    cb[:, M_PAD:M_PAD + P] = np.where(r[None, :] >= PAD, 0, NEG)
    return cf, cb


def stream_layer(nc, io):
    top = ExitStack()
    with top:
        top.enter_context(nc.allow_non_contiguous_dma(reason="short vectors turned onto the partitions"))
        scope = [0]

        def fresh(name):
            scope[0] += 1
            return f"{name}_{scope[0]}"

        def sb(name, shape, dt=F32, st=top):
            return st.enter_context(nc.sbuf_tensor(fresh(name), shape, dt))

        def pb(name, shape, st):
            return st.enter_context(nc.psum_tensor(fresh(name), shape, F32))

        def sem(name, st):
            return nc.alloc_semaphore(name=fresh(name))

        cf = sb("cf", [P, NCF])
        cb = sb("cb", [P, NCB], BF16)
        hT = sb("hT", [P, KT, T])
        reg = sb("reg", [P, 6, T])
        vrow = sb("vrow", [P, TILES, RV])
        wslot = sb("wslot", [P, 2, KT, P])
        mix, uT, sz = io["mix"], io["uT"], io["sz"]
        ident = cf[:, C_ID:C_ID + P]
        identb = cb[:, M_ID:M_ID + P]
        eps = cf[:, C_EPS:C_EPS + 1]
        one = cf[:, C_ONE:C_ONE + 1]
        w_in = io["w_in"][0].rearrange("(k p) n -> p k n", p=P)

        def wide(ap, n, axis=1):
            a = ap.unsqueeze(axis)
            shape = list(a.shape)
            shape[axis] = n
            return a.to_broadcast(shape)


        def norm_and_transpose():
            with ExitStack() as st:
                xin = sb("xin", [P, 3, D], st=st)
                junk = sb("junk", [P, D], st=st)
                gpre = sb("gpre", [P, KT], st=st)
                ssq, lnv, rstd = (sb(n, [P, TILES], st=st) for n in ("ssq", "lnv", "rstd"))
                tp = pb("tp", [P, 3, KT, P], st)
                consts_in, zeroed, masks_cast = sem("consts_in", st), sem("zeroed", st), sem("masks_cast", st)
                x_in = [sem(f"x_in{i}", st) for i in range(3)]
                sq_done, ln_done, rstd_done = (sem(n, st) for n in ("sq_done", "ln_done", "rstd_done"))
                scaled, turned, kept = (sem(n, st) for n in ("scaled", "turned", "kept"))
                xp = io["x_prompt"][0]
                with nc.Block() as block:
                    @block.sync
                    def _(sp):
                        sp.wait_ge(zeroed, 2)
                        sp.dma_start(xin[PAD:CH, 0, :], io["meta_tokens"]).then_inc(x_in[0], 16)
                        sp.dma_start(xin[CH:P, 0, :], xp[0:CH, :]).then_inc(x_in[0], 16)
                        sp.dma_start(xin[0:SP0, 1, :], xp[SEQ - SP0:SEQ, :]).then_inc(x_in[1], 16)
                        sp.dma_start(xin[SP0:SP0 + NSAMP, 1, :], io["x_sample"][0]).then_inc(x_in[1], 16)
                        sp.dma_start(xin[:, 2, :], xp[CH:CH + P, :]).then_inc(x_in[2], 32)
                        sp.dma_start(cf[:, :], io["cf"]).then_inc(consts_in, 16)
                        sp.dma_start(gpre[:, :], io["norm_pre"][0].rearrange("(k p) -> p k", p=P)).then_inc(consts_in, 16)
                        sp.dma_start(reg[:, 0, 0:NCB], io["cb"]).then_inc(consts_in, 16)
                        for n in range(3, 5):
                            sp.wait_ge(turned, n - 2)
                            sp.dma_start(xin[:, n % 3, :], xp[CH + P * (n - 2):CH + P * (n - 1), :]).then_inc(x_in[n % 3], 32)
                        with sp.Fori(0, (TILES - 5) // 3) as i:
                            for u in range(3):
                                sp.wait_ge(turned, 3 * i + (u + 3))
                                sp.dma_start(xin[:, (u + 2) % 3, :],
                                             xp[bass.ds(i * (3 * P) + (CH + P * (u + 3)), P), :]).then_inc(x_in[(u + 2) % 3], 32)

                    @block.gpsimd
                    def _(pool):
                        pool.memset(xin[0:CH, 0, :], 0.0).then_inc(zeroed, 1)
                        pool.memset(xin[SP0 + NSAMP:P, 1, :], 0.0).then_inc(zeroed, 1)

                    @block.scalar
                    def _(act):
                        def step(n, slot, col, landed):
                            act.wait_ge(x_in[slot], landed)
                            act.activation(junk[:, :], xin[:, slot, :], ACT.Square, accum_out=ssq[:, col]).then_inc(sq_done, 1)
                            act.wait_ge(sq_done, n + 1)
                            act.activation(lnv[:, col], ssq[:, col], ACT.Ln, bias=eps, scale=1.0 / D).then_inc(ln_done, 1)
                            act.wait_ge(ln_done, n + 1)
                            act.activation(rstd[:, col], lnv[:, col], ACT.Exp, scale=-0.5).then_inc(rstd_done, 1)

                        act.wait_ge(consts_in, 48)
                        step(0, 0, slice(0, 1), 32)
                        step(1, 1, slice(LAST, TILES), 32)
                        with act.Fori(0, (TILES - 2) // 3) as i:
                            for u in range(3):
                                s = (u + 2) % 3
                                step(3 * i + (u + 2), s, bass.ds(3 * i + (u + 1), 1), 32 * i + (32 if s == 2 else 64))

                    @block.vector
                    def _(dve):
                        def scale(n, slot, col):
                            dve.wait_ge(rstd_done, n + 1)
                            dve.tensor_scalar(xin[:, slot, :], xin[:, slot, :], rstd[:, col], None, ALU.mult).then_inc(scaled, 1)

                        def keep(n, slot, cols):
                            dve.wait_ge(turned, n + 1)
                            for k in (0, KT // 2):
                                dve.tensor_tensor(hT[:, k:k + KT // 2, cols], tp[:, slot, k:k + KT // 2, :],
                                                  gpre[:, k:k + KT // 2].unsqueeze(2).to_broadcast([P, KT // 2, P]),
                                                  ALU.mult).then_inc(kept, 1)

                        dve.wait_ge(consts_in, 48)
                        dve.tensor_copy(cb[:, :], reg[:, 0, 0:NCB]).then_inc(masks_cast, 1)
                        scale(0, 0, slice(0, 1))
                        scale(1, 1, slice(LAST, TILES))
                        keep(0, 0, slice(0, P))
                        scale(2, 2, slice(1, 2))
                        keep(1, 1, slice(LAST * P, T))
                        with dve.Fori(0, (TILES - 2) // 3 - 1) as i:
                            for u in range(3):
                                scale(3 * i + (u + 3), u, bass.ds(3 * i + (u + 2), 1))
                                keep(3 * i + (u + 2), (u + 2) % 3, bass.ds(3 * P * i + P * (u + 1), P))
                        for n in (TILES - 2, TILES - 1):
                            scale(n, n % 3, slice(n - 1, n))
                            keep(n - 1, (n - 1) % 3, slice(P * (n - 2), P * (n - 1)))
                        keep(TILES - 1, (TILES - 1) % 3, slice(P * (TILES - 2), P * (TILES - 1)))

                    @block.tensor
                    def _(pe):
                        def step(n, slot, freed):
                            pe.wait_ge(scaled, n + 1)
                            if freed is not None:
                                pe.wait_ge(kept, freed)
                            for k in range(KT):
                                last = pe.transpose(tp[:, slot, k, :], xin[:, slot, k * P:(k + 1) * P], ident)
                            last.then_inc(turned, 1)

                        pe.wait_ge(consts_in, 48)
                        step(0, 0, None)
                        step(1, 1, None)
                        step(2, 2, None)
                        with pe.Fori(0, (TILES - 2) // 3 - 1) as i:
                            for u in range(3):
                                step(3 * i + (u + 3), u, 6 * i + 2 * (u + 1))
                        for n in (TILES - 2, TILES - 1):
                            step(n, n % 3, 2 * (n - 2))

        def project_rows():
            with ExitStack() as st:
                wv = sb("wv", [P, KT, RV], st=st)
                acc = pb("acc", [P, 4, 512], st)
                wv_in, row_ready, row_kept = (sem(n, st) for n in ("wv_in", "row_ready", "row_kept"))
                out_done = sem("out_done", st)
                with nc.Block() as block:
                    @block.sync
                    def _(sp):
                        sp.dma_start(wv[:, :, 0:VAW], w_in[:, :, VA:VA + VAW]).then_inc(wv_in, 16)
                        sp.dma_start(wv[:, :, VAW:VAW + VBW], w_in[:, :, VB:VB + VBW]).then_inc(wv_in, 16)
                        sp.dma_start(wv[:, :, VAW + VBW:RV], w_in[:, :, AB:AB + ABW]).then_inc(wv_in, 16)
                        sp.wait_ge(row_kept, TILES)
                        flat = lambda name: io[name][0, 0].rearrange("t h d -> t (h d)")
                        b0 = slice(VAW, VAW + VBW)
                        sp.dma_start(flat("p_b_v")[0:NMETA, :], vrow[PAD:CH, 0, b0]).then_inc(out_done, 16)
                        sp.dma_start(flat("p_b_v")[NMETA:NMETA + CH, :], vrow[CH:P, 0, b0]).then_inc(out_done, 16)
                        sp.dma_start(flat("p_b_v")[NMETA + CH:NMETA + SEQ - SP0, :].rearrange("(t p) n -> p t n", p=P),
                                     vrow[:, 1:LAST, b0]).then_inc(out_done, 16)
                        sp.dma_start(flat("p_b_v")[NMETA + SEQ - SP0:NMETA + SEQ, :], vrow[0:SP0, LAST, b0]).then_inc(out_done, 16)
                        sp.dma_start(flat("s_b_v"), vrow[SP0:SP0 + NSAMP, LAST, b0]).then_inc(out_done, 16)
                        sp.dma_start(flat("p_a_v")[0:WIN - SP0, :], vrow[SP0:P, LAST - 1, 0:VAW]).then_inc(out_done, 16)
                        sp.dma_start(flat("p_a_v")[WIN - SP0:WIN, :], vrow[0:SP0, LAST, 0:VAW]).then_inc(out_done, 16)
                        sp.dma_start(flat("s_a_v")[WIN - NSAMP:WIN, :], vrow[SP0:SP0 + NSAMP, LAST, 0:VAW]).then_inc(out_done, 16)
                        sp.dma_start(flat("s_a_v")[0:WIN - NSAMP, :], flat("cache_a_v")[NSAMP:WIN, :]).then_inc(out_done, 16)
                        sp.dma_start(flat("s_a_k")[0:WIN - NSAMP, :], flat("cache_a_k")[NSAMP:WIN, :]).then_inc(out_done, 16)
                        sp.wait_ge(out_done, 160)

                    @block.tensor
                    def _(pe):
                        pe.wait_ge(wv_in, 48)
                        for m in range(TILES):
                            if m >= 4:
                                pe.wait_ge(row_kept, m - 3)
                            for k in range(KT):
                                last = pe.matmul(acc[:, m % 4, 0:RV], hT[:, k, m * P:(m + 1) * P], wv[:, k, :],
                                                 start=(k == 0), stop=(k == KT - 1))
                            last.then_inc(row_ready, 1)

                    @block.vector
                    def _(dve):
                        for m in range(TILES):
                            dve.wait_ge(row_ready, m + 1)
                            dve.tensor_copy(vrow[:, m, :], acc[:, m % 4, 0:RV]).then_inc(row_kept, 1)

        def project(groups, spills=0):
            with ExitStack() as st:
                sg = sb("sg", [P, NBLK, 512], st=st)
                acc = pb("acc", [P, NBLK, 512], st)
                w_in_slot = [sem(f"w_in_slot{i}", st) for i in range(2)]
                acc_ready = sem("acc_ready", st)
                bank_free = [sem(f"bank_free{b}", st) for b in range(NBLK)]
                sig_ready, spilled = sem("sig_ready", st), sem("spilled", st)
                gated = [sem(f"gated{b}", st) for b in range(NBLK)]

                def tiles(eng, body):
                    base = 0
                    for g in groups:
                        pairs = g[3] // 2
                        peeled = 1 if base == 0 and pairs else 0
                        for u in range(2 * peeled):
                            body(base + u, (base + u) % 2, u, g)
                        if pairs > peeled:
                            with eng.Fori(peeled, pairs) as i:
                                for u in range(2):
                                    body(2 * i + (base + u), (base + u) % 2, 2 * i + u, g)
                        if g[3] % 2:
                            body(base + g[3] - 1, (base + g[3] - 1) % 2, g[3] - 1, g)
                        base += g[3]

                gates = sum(g[3] for g in groups if g[0] == "gate")
                with nc.Block() as block:
                    @block.sync
                    def _(sp):
                        def load(n, par, t, g):
                            if not isinstance(n, int) or n >= 2:
                                sp.wait_ge(bank_free[NBLK - 1], n - 1)
                            at = 0
                            for c0, width, step in g[1]:
                                src = w_in[:, :, c0 + t * step:c0 + t * step + width] if isinstance(t, int) else \
                                    w_in[:, :, bass.ds(t * step + c0, width)]
                                sp.dma_start(wslot[:, par, :, at:at + width], src).then_inc(w_in_slot[par], 32 // len(g[1]))
                                at += width
                        tiles(sp, load)

                    @block.gpsimd
                    def _(pool):
                        def spill(n, par, t, g):
                            if g[0] != "gate":
                                return
                            for b in range(NBLK):
                                pool.wait_ge(gated[b], t + 1)
                            k = g[2] + t
                            dst = mix[spills + t] if isinstance(t, int) else mix[bass.ds(t + spills, 1)].rearrange("o p t -> (o p) t")
                            pool.dma_start(dst, reg[:, k, :]).then_inc(spilled, 16)
                        tiles(pool, spill)
                        if gates:
                            pool.wait_ge(spilled, 16 * gates)

                    @block.tensor
                    def _(pe):
                        def tile(n, par, t, g):
                            pe.wait_ge(w_in_slot[par], (n - par) * 16 + 32)
                            for b, (c0, width) in enumerate(BLOCKS):
                                if not isinstance(n, int) or n > 0:
                                    pe.wait_ge(bank_free[b], n)
                                for k in range(KT):
                                    last = pe.matmul(acc[:, b, 0:width], wslot[:, par, k, :], hT[:, k, c0:c0 + width],
                                                     start=(k == 0), stop=(k == KT - 1))
                                last.then_inc(acc_ready, 1)
                        tiles(pe, tile)

                    @block.scalar
                    def _(act):
                        def tile(n, par, t, g):
                            for b, (c0, width) in enumerate(BLOCKS):
                                if g[0] == "gate":
                                    act.wait_ge(acc_ready, n * NBLK + (b + 1))
                                    if not isinstance(t, int) or t > 0:
                                        act.wait_ge(gated[b], t)
                                    act.activation(sg[:, b, 0:width], acc[:, b, 0:width], ACT.Sigmoid).then_inc(sig_ready, 1)
                                elif b % 2 == 0:
                                    act.wait_ge(acc_ready, n * NBLK + (b + 1))
                                    if len(g) > 4:
                                        act.wait_ge(spilled, 16 * gates)
                                    act.activation(reg[:, g[2] + t, c0:c0 + width], acc[:, b, 0:width], ACT.Copy).then_inc(bank_free[b], 1)
                        tiles(act, tile)

                    @block.vector
                    def _(dve):
                        def tile(n, par, t, g):
                            for b, (c0, width) in enumerate(BLOCKS):
                                if g[0] == "gate":
                                    dve.wait_ge(sig_ready, t * NBLK + (b + 1))
                                    dve.tensor_tensor(sg[:, b, 0:width], acc[:, b, 0:width], sg[:, b, 0:width], ALU.mult).then_inc(bank_free[b], 1)
                                    dve.wait_ge(bank_free[b], n + 1)
                                    r = reg[:, g[2] + t, c0:c0 + width]
                                    dve.tensor_tensor(r, r, sg[:, b, 0:width], ALU.mult).then_inc(gated[b], 1)
                                elif b % 2:
                                    dve.wait_ge(acc_ready, n * NBLK + (b + 1))
                                    if len(g) > 4:
                                        dve.wait_ge(spilled, 16 * gates)
                                    dve.tensor_copy(reg[:, g[2] + t, c0:c0 + width], acc[:, b, 0:width]).then_inc(bank_free[b], 1)
                        tiles(dve, tile)

        class SideProjection:

            def __init__(self, st, kind, tiles, scratch):
                self.kind, self.tiles, self.scratch = kind, tiles, scratch
                self.units = NBLK * len(tiles)
                self.pieces = KT * self.units
                self.stage = sb("side_stage", [P, 2, 512], st=st)
                self.acc = pb("side_acc", [P, 2, 512], st)
                self.w_in_slot = [sem(f"side_w_in{i}", st) for i in range(2)]
                self.acc_ready, self.sig_ready, self.staged = (sem(n, st) for n in ("side_acc_ready", "side_sig_ready", "side_staged"))
                self.stored = [sem(f"side_stored{i}", st) for i in range(2)]

            def products(self, pe, first, count):
                for p in range(first, min(first + count, self.pieces)):
                    n, k = divmod(p, KT)
                    t, b = divmod(n, NBLK)
                    c0, width = BLOCKS[b]
                    if k == 0:
                        if b == 0:
                            pe.wait_ge(self.w_in_slot[t % 2], 32 * (t // 2 + 1))
                        if n >= 2:
                            pe.wait_ge(self.staged, n - 1)
                    last = pe.matmul(self.acc[:, n % 2, 0:width], wslot[:, t % 2, k, :], hT[:, k, c0:c0 + width],
                                     start=(k == 0), stop=(k == KT - 1))
                    if k == KT - 1:
                        last.then_inc(self.acc_ready, 1)

            def keep(self, act, n):
                width = BLOCKS[n % NBLK][1]
                act.wait_ge(self.acc_ready, n + 1)
                if n >= 2:
                    act.wait_ge(self.stored[n % 2], 16 * (n // 2))
                if self.kind == "copy":
                    act.activation(self.stage[:, n % 2, 0:width], self.acc[:, n % 2, 0:width], ACT.Copy).then_inc(self.staged, 1)
                else:
                    act.activation(self.stage[:, n % 2, 0:width], self.acc[:, n % 2, 0:width], ACT.Sigmoid).then_inc(self.sig_ready, 1)

            def gate(self, dve, n):
                width = BLOCKS[n % NBLK][1]
                dve.wait_ge(self.sig_ready, n + 1)
                dve.tensor_tensor(self.stage[:, n % 2, 0:width], self.acc[:, n % 2, 0:width], self.stage[:, n % 2, 0:width],
                                  ALU.mult).then_inc(self.staged, 1)

            def transfers(self, sp):
                def load(t):
                    at, segs = 0, self.tiles[t]
                    if t >= 2:
                        sp.wait_ge(self.acc_ready, NBLK * (t - 1))
                    for c0, width in segs:
                        sp.dma_start(wslot[:, t % 2, :, at:at + width], w_in[:, :, c0:c0 + width]).then_inc(self.w_in_slot[t % 2], 32 // len(segs))
                        at += width

                load(0)
                load(1)
                for n in range(self.units):
                    t, b = divmod(n, NBLK)
                    c0, width = BLOCKS[b]
                    sp.wait_ge(self.staged, n + 1)
                    sp.dma_start(self.scratch[t][:, c0:c0 + width], self.stage[:, n % 2, 0:width]).then_inc(self.stored[n % 2], 16)
                    if b == NBLK - 1 and t + 2 < len(self.tiles):
                        load(t + 2)
                for i in range(2):
                    sp.wait_ge(self.stored[i], 16 * ((self.units + 1 - i) // 2))

        def move_blocks(sp, moves, done):
            for b, (c0, width) in enumerate(BLOCKS):
                for dst, src in moves:
                    sp.dma_start(dst(c0, width), src(c0, width)).then_inc(done[b], 16)

        def conv_and_gates(cx):
            with ExitStack() as st:
                y = sb("y", [P, 2, T], st=st)
                taps = sb("taps", [P, 6, 4], st=st)
                hist = sb("hist", [P, 6, 3 + NSAMP], st=st)
                tails = sb("tails", [P, 6, 2, 3], st=st)
                heads4 = sb("heads4", [P, 2, 4], st=st)
                ga = sb("ga", [P, 4, TILES, 4], st=st)
                ea = sb("ea", [P, 4], st=st)
                gsum = pb("gsum", [P, 4, 512], st)
                small_in, copied, tap, sample_tap = (sem(n, st) for n in ("small_in", "copied", "tap", "sample_tap"))
                scaled, conv_done, sig_done, silu_done = (sem(n, st) for n in ("scaled", "conv_done", "sig_done", "silu_done"))
                gate_v, gate_s, sums = sem("gate_v", st), sem("gate_s", st), sem("sums", st)
                out_done, s0_in = sem("out_done", st), sem("s0_in", st)
                W4 = 4 * TILES
                flat = lambda ap: ap.rearrange("p t h -> p (t h)")
                with nc.Block() as block:
                    @block.sync
                    def _(sp):
                        for w in range(4):
                            sp.dma_start(taps[:, :, w], io["conv_c"][0, w].rearrange("(t p) -> p t", p=P)).then_inc(small_in, 16)
                        for w in range(3):
                            sp.dma_start(hist[:, :, w], io["state_c_conv"][0, 0, w].rearrange("(t p) -> p t", p=P)).then_inc(small_in, 16)
                        sp.dma_start(heads4[:, 0, :], io["dt_bias_c"].to_broadcast([P, 4])).then_inc(small_in, 16)
                        sp.dma_start(heads4[:, 1, :], io["a_log_c"].to_broadcast([P, 4])).then_inc(small_in, 16)
                        for par in range(2):
                            sp.dma_start(cx["S"][par * CH:par * CH + CH, 1],
                                         io["state_c_ssm"][0, 0].rearrange("(a b) k v -> b k a v", b=2)[par]).then_inc(s0_in, 16)
                        sp.wait_ge(copied, 3)
                        for a, name in enumerate(("p_c_conv", "s_c_conv")):
                            for w in range(3):
                                sp.dma_start(io[name][0, 0, w].rearrange("(t p) -> p t", p=P), tails[:, :, a, w]).then_inc(out_done, 16)
                        sp.wait_ge(out_done, 96)
                        sp.wait_ge(s0_in, 32)

                    @block.vector
                    def _(dve):
                        for a, c0 in enumerate((SROW - 3, SROW + NSAMP - 3)):
                            dve.tensor_copy(tails[:, :, a, :], reg[:, :, c0:c0 + 3]).then_inc(copied, 1)
                        dve.tensor_copy(hist[:, :, 3:3 + NSAMP], reg[:, :, SROW:SROW + NSAMP]).then_inc(copied, 1)
                        dve.memset(cx["S"][:, 0], 0.0).then_inc(copied, 1)
                        dve.wait_ge(small_in, 144)
                        dve.wait_ge(copied, 4)
                        v = 0
                        x, t, u, g = (ga[:, n] for n in range(4))
                        raw = lambda at: vrow[:, :, VAW + VBW + at:VAW + VBW + at + 4]
                        dve.tensor_tensor(x, raw(0), wide(heads4[:, 0, :], TILES), ALU.add).then_inc(gate_v, 1)
                        dve.wait_ge(gate_v, 1)
                        dve.scalar_tensor_tensor(out=t, in0=x, scalar=-1.0, in1=x, op0=ALU.mult, op1=ALU.max).then_inc(gate_v, 1)
                        dve.wait_ge(gate_s, 4)
                        dve.scalar_tensor_tensor(out=u, in0=x, scalar=0.0, in1=t, op0=ALU.max, op1=ALU.add).then_inc(gate_v, 1)
                        dve.wait_ge(gate_v, 3)
                        dve.scalar_tensor_tensor(out=g, in0=u, scalar=-1.0, in1=wide(ea[:, :], TILES),
                                                 op0=ALU.mult, op1=ALU.mult).then_inc(gate_v, 1)
                        dve.tensor_scalar(cx["beta"][:, :, :], cx["beta"][:, :, :], 1.0, None, ALU.add).then_inc(gate_v, 1)
                        dve.wait_ge(gate_v, 5)
                        dve.reciprocal(cx["beta"][:, :, :], cx["beta"][:, :, :]).then_inc(gate_v, 1)
                        dve.memset(g[SP0 + NSAMP:P, LAST, :], 0.0).then_inc(gate_v, 1)
                        dve.wait_ge(gate_v, 7)
                        dve.tensor_copy(cx["g"][:, :, :], g).then_inc(gate_v, 1)
                        dve.wait_ge(sums, 1)
                        dve.tensor_scalar(flat(cx["ngc"]), gsum[:, 0, 0:W4], -1.0, None, ALU.mult).then_inc(gate_v, 1)
                        dve.wait_ge(gate_v, 9)
                        dve.tensor_tensor(flat(t), gsum[:, 1, 0:W4], flat(cx["ngc"]), ALU.add).then_inc(gate_v, 1)
                        dve.wait_ge(gate_s, 5)
                        dve.tensor_scalar(flat(cx["neg_eg"]), flat(cx["eg"]), -1.0, None, ALU.mult).then_inc(gate_v, 1)
                        for c in range(6):
                            yc = y[:, c % 2, :]
                            dve.wait_ge(scaled, c + 1)
                            for w in range(3):
                                if w:
                                    dve.wait_ge(tap, 3 * c + w)
                                dve.scalar_tensor_tensor(out=yc[:, 3:T], in0=reg[:, c, w:T - 3 + w], scalar=taps[:, c, w:w + 1],
                                                         in1=yc[:, 3:T], op0=ALU.mult, op1=ALU.add).then_inc(tap, 1)
                            dve.wait_ge(tap, 3 * c + 3)
                            ys = yc[:, SROW:SROW + NSAMP]
                            dve.tensor_scalar(ys, hist[:, c, 3:3 + NSAMP], taps[:, c, 3:4], None, ALU.mult).then_inc(sample_tap, 1)
                            for w in range(3):
                                dve.wait_ge(sample_tap, 4 * c + w + 1)
                                dve.scalar_tensor_tensor(out=ys, in0=hist[:, c, w:w + NSAMP], scalar=taps[:, c, w:w + 1],
                                                         in1=ys, op0=ALU.mult, op1=ALU.add).then_inc(sample_tap, 1)
                            dve.memset(yc[:, SROW + NSAMP:T], 0.0).then_inc(conv_done, 1)
                            dve.wait_ge(sample_tap, 4 * c + 4)

                    @block.scalar
                    def _(act):
                        act.wait_ge(small_in, 144)
                        act.activation(ea[:, :], heads4[:, 1, :], ACT.Exp).then_inc(gate_s, 1)
                        x, t, u, g = (ga[:, n] for n in range(4))
                        act.activation(cx["beta"][:, :, :], vrow[:, :, VAW + VBW + 4:RV], ACT.Exp, scale=-1.0).then_inc(gate_s, 1)
                        act.wait_ge(gate_v, 2)
                        act.activation(t, t, ACT.Exp, scale=-1.0).then_inc(gate_s, 1)
                        act.wait_ge(gate_s, 3)
                        act.activation(t, t, ACT.Ln, bias=one).then_inc(gate_s, 1)
                        act.wait_ge(gate_v, 9)
                        act.activation(flat(cx["eg"]), gsum[:, 0, 0:W4], ACT.Exp).then_inc(gate_s, 1)
                        act.wait_ge(gate_v, 10)
                        act.activation(flat(cx["ekd"]), flat(t), ACT.Exp).then_inc(gate_s, 1)
                        for c in range(2):
                            for par in range(2):
                                half = slice(par * CH, par * CH + CH)
                                act.activation(cx["gl"][half, :, c, :],
                                               gsum[half, 2 + c, 0:W4].rearrange("p (t a b) -> p t a b", a=2, b=2)[:, :, :, par],
                                               ACT.Exp).then_inc(gate_s, 1)
                        for c in range(6):
                            if c >= 2:
                                act.wait_ge(silu_done, c - 1)
                            if c == 0:
                                act.activation(y[:, 0, :], reg[:, 0, :], ACT.Copy, scale=taps[:, 0, 3:4]).then_inc(scaled, 1)
                            if c < 5:
                                if c >= 1:
                                    act.wait_ge(silu_done, c)
                                act.activation(y[:, (c + 1) % 2, :], reg[:, c + 1, :], ACT.Copy, scale=taps[:, c + 1, 3:4]).then_inc(scaled, 1)
                            act.wait_ge(conv_done, c + 1)
                            act.wait_ge(sample_tap, 4 * c + 4)
                            act.activation(reg[:, c, :], y[:, c % 2, :], ACT.Sigmoid).then_inc(sig_done, 1)

                    @block.gpsimd
                    def _(pool):
                        for c in range(6):
                            pool.wait_ge(sig_done, c + 1)
                            pool.tensor_tensor(reg[:, c, :], reg[:, c, :], y[:, c % 2, :], ALU.mult).then_inc(silu_done, 1)

                    @block.tensor
                    def _(pe):
                        pe.wait_ge(gate_v, 8)
                        gf = flat(cx["g"])
                        for n, c in enumerate((C_TRI, C_BLK, C_LO, C_HI)):
                            last = pe.matmul(gsum[:, n, 0:W4], cf[:, c:c + P], gf, start=True, stop=True)
                        last.then_inc(sums, 1)

            with ExitStack() as st:
                sq = sb("sq", [P, 4, 512], st=st)
                rn = sb("rn", [P, 4, 512], st=st)
                ss = pb("ss", [P, 4, 512], st)
                sq_done, ss_ready, ln_done, rn_done, normed = (sem(n, st) for n in ("sq_done", "ss_ready", "ln_done", "rn_done", "normed"))
                steps = [(c, c0, w) for c in range(4) for c0, w in BLOCKS]
                with nc.Block() as block:
                    @block.gpsimd
                    def _(pool):
                        for n, (c, c0, w) in enumerate(steps):
                            if n >= 4:
                                pool.wait_ge(ss_ready, n - 3)
                            r = reg[:, c, c0:c0 + w]
                            pool.tensor_tensor(sq[:, n % 4, 0:w], r, r, ALU.mult).then_inc(sq_done, 1)

                    @block.tensor
                    def _(pe):
                        for n, (c, c0, w) in enumerate(steps):
                            pe.wait_ge(sq_done, n + 1)
                            if n >= 4:
                                pe.wait_ge(ln_done, n - 3)
                            pe.matmul(ss[:, n % 4, 0:w], cf[:, C_BLK:C_BLK + P], sq[:, n % 4, 0:w], start=True, stop=True).then_inc(ss_ready, 1)

                    @block.scalar
                    def _(act):
                        for n, (c, c0, w) in enumerate(steps):
                            act.wait_ge(ss_ready, n + 1)
                            if n >= 4:
                                act.wait_ge(normed, n - 3)
                            act.activation(rn[:, n % 4, 0:w], ss[:, n % 4, 0:w], ACT.Ln, bias=eps).then_inc(ln_done, 1)
                            act.wait_ge(ln_done, n + 1)
                            act.activation(rn[:, n % 4, 0:w], rn[:, n % 4, 0:w], ACT.Exp, scale=-0.5).then_inc(rn_done, 1)

                    @block.vector
                    def _(dve):
                        for n, (c, c0, w) in enumerate(steps):
                            dve.wait_ge(rn_done, n + 1)
                            r = reg[:, c, c0:c0 + w]
                            dve.scalar_tensor_tensor(out=r, in0=r, scalar=SCALE if c < 2 else 1.0, in1=rn[:, n % 4, 0:w],
                                                     op0=ALU.mult, op1=ALU.mult).then_inc(normed, 1)

        def delta_net(cx, side_tiles):
            with ExitStack() as st:
                tg = sb("tg", [P, 4, P], st=st)
                dec = sb("dec", [P, 4, P], st=st)
                at = sb("at", [P, 4, P], st=st)
                atl = sb("atl", [P, LEVELS, 4, P], st=st)
                qk = sb("qk", [P, 2, 4, P], st=st)
                xm = sb("xm", [P, 4, P], st=st)
                xt = sb("xt", [P, 2, 4, P], st=st)
                ym = sb("ym", [P, 4, P], st=st)
                kd = sb("kd", [P, 2, 4, HD], st=st)
                vr = sb("vr", [P, 2, 4, HD], st=st)
                rr = sb("rr", [P, 4, HD], st=st)
                vn = sb("vn", [P, 4, HD], st=st)
                oo = sb("oo", [P, 4, HD], st=st)
                osq = sb("osq", [P, 4, HD], st=st)
                oss, oln, ors = (sb(n, [P, 4], st=st) for n in ("oss", "oln", "ors"))
                onorm = sb("onorm", [P, HD], st=st)
                b_dr = pb("b_dr", [P, 4, P], st)
                b_kq = pb("b_kq", [P, 2, 2, 2, P], st)
                b_lv = b_kq[:, 0].rearrange("p a q i -> p (a q) i")
                b_lt = b_kq[:, 1].rearrange("p a q i -> p (a q) i")
                b_s = pb("b_s", [P, 2, 512], st)
                b_ds = b_s[:, 0, 4 * HD:6 * HD]
                b_ot = b_s[:, 1, 4 * HD:8 * HD]
                b_vn = pb("b_vn", [P, 2, 4, HD], st)
                side = SideProjection(st, "copy", side_tiles, uT)
                names = ("tg_ready dec_ready dec_done rows_ready v_kept rows_kept kq_ready at_ready qk_ready kd_ready level "
                         "xt0_ready x0_ready x0_kept y_ready y_kept z_ready x_new ks_ready r_ready vn_ready vn_kept "
                         "ds_ready state_ready o_ready o_sum o_squared o_rss o_ln o_rstd o_scaled o_normed ot_ready ot_kept "
                         "onorm_in out_done o_part").split()
                (tg_ready, dec_ready, dec_done, rows_ready, v_kept, rows_kept, kq_ready, at_ready, qk_ready, kd_ready, level,
                 xt0_ready, x0_ready, x0_kept, y_ready, y_kept, z_ready, x_new, ks_ready, r_ready, vn_ready, vn_kept,
                 ds_ready, state_ready, o_ready, o_sum, o_squared, o_rss, o_ln, o_rstd, o_scaled, o_normed, ot_ready, ot_kept,
                 onorm_in, out_done, o_part) = (sem(n, st) for n in names)
                lvl = lambda l: cf[:, C_LVL + l * P:C_LVL + (l + 1) * P]
                cols = lambda m: slice(m * P, (m + 1) * P)
                NL = LEVELS - 1
                XN = 2 * NL - 1
                S = cx["S"]
                POINTS = [2, 1, 1, 3, 1, 3, 1, 3, 1, 3, 1, 2]
                FIRST = [[m * sum(POINTS) + sum(POINTS[:p]) for p in range(len(POINTS))] for m in range(TILES)]
                assert TILES * sum(POINTS) >= side.pieces

                def state(c):
                    return S[:, 1] if c == 2 * TILES - 1 else S[:, 0]

                with nc.Block() as block:
                    @block.sync
                    def _(sp):
                        side.transfers(sp)

                    @block.gpsimd
                    def _(pool):
                        def triangle_gates(m):
                            if m:
                                pool.wait_ge(dec_ready, m)
                            pool.tensor_tensor(tg[:, :, :], wide(cf[:, C_TRI:C_TRI + P], 4),
                                               cx["g"][:, m, :].unsqueeze(2).to_broadcast([P, 4, P]), ALU.mult).then_inc(tg_ready, 1)

                        pool.dma_start(onorm[:, :], io["onorm_c"].to_broadcast([P, HD])).then_inc(onorm_in, 16)
                        triangle_gates(0)
                        for m in range(TILES + 1):
                            if m < TILES:
                                pool.wait_ge(at_ready, 4 * m + 4)
                                for l in range(LEVELS):
                                    if m and l:
                                        pool.wait_ge(y_ready, NL * (m - 1) + l)
                                    elif m:
                                        pool.wait_ge(xt0_ready, m)
                                    pool.tensor_tensor(atl[:, l], at[:, :, :], wide(lvl(l), 4), ALU.mult).then_inc(level, 1)
                                if m + 1 < TILES:
                                    triangle_gates(m + 1)
                            if m:
                                pool.wait_ge(o_rstd, m)
                                pool.tensor_tensor(osq[:, :, :], oo[:, :, :], ors[:, :].unsqueeze(2).to_broadcast([P, 4, HD]),
                                                   ALU.mult).then_inc(o_scaled, 1)
                                if m == 1:
                                    pool.wait_ge(onorm_in, 16)
                                else:
                                    pool.wait_ge(ot_ready, m - 1)
                                pool.wait_ge(o_scaled, m)
                                pool.tensor_tensor(oo[:, :, :], osq[:, :, :], wide(onorm[:, :], 4), ALU.mult).then_inc(o_normed, 1)
                        for a, name in enumerate(("p_c_ssm", "s_c_ssm")):
                            pool.wait_ge(state_ready, 2 * (2 * TILES - 1) + 2 * a)
                            for par in range(2):
                                pool.dma_start(io[name][0, 0].rearrange("(a b) k v -> b k a v", b=2)[par],
                                               S[par * CH:par * CH + CH, a]).then_inc(out_done, 16)
                        pool.wait_ge(out_done, 64)

                    @block.tensor
                    def _(pe):
                        def decay(m):
                            pe.wait_ge(tg_ready, m + 1)
                            if m:
                                pe.wait_ge(rows_kept, m)
                            pe.matmul(b_dr[:, :, :], identb, wide(cb[:, M_DT:M_DT + P], 4), start=True, stop=False)
                            pe.matmul(b_dr[:, :, :], cf[:, C_BLK:C_BLK + P], tg[:, :, :], start=False, stop=True).then_inc(dec_ready, 1)

                        def rows(m):
                            pe.wait_ge(dec_done, 4 * m + 4)
                            for a in range(4):
                                last = pe.transpose(b_dr[:, a, :], reg[:, 2 + a, cols(m)], ident)
                            last.then_inc(rows_ready, 1)

                        def kq(m):
                            if m:
                                pe.wait_ge(x_new, XN * m)
                            for h in range(4):
                                half = slice((h % 2) * CH, (h % 2) * CH + CH)
                                last = pe.matmul(b_kq[:, h % 2, h // 2], reg[half, 2 + h // 2, cols(m)],
                                                 reg[half, h // 2:h // 2 + 3:2, cols(m)], start=True, stop=True)
                            last.then_inc(kq_ready, 1)

                        def x0(m):
                            pe.wait_ge(xt0_ready, m + 1)
                            pe.wait_ge(at_ready, 4 * m + 4)
                            pe.wait_ge(qk_ready, 2 * m + 2)
                            for h in range(4):
                                last = pe.transpose(b_lv[:, h, :], xt[:, m % 2, h], ident)
                            last.then_inc(x0_ready, 1)

                        def level_y(m, l):
                            if l == 1:
                                pe.wait_ge(x0_kept, m + 1)
                            else:
                                pe.wait_ge(x_new, XN * m + 2 * (l - 1))
                            pe.wait_ge(level, LEVELS * m + l + 1)
                            for h in range(4):
                                last = pe.matmul(b_lv[:, h, :], atl[:, l, h], xm[:, h], start=True, stop=True)
                            last.then_inc(y_ready, 1)

                        def level_z(m, l):
                            pe.wait_ge(y_kept, NL * m + l)
                            for h in range(4):
                                last = pe.matmul(b_lt[:, h, :], ym[:, h], xt[:, m % 2, h], start=True, stop=True)
                            if l < NL:
                                for h in range(4):
                                    last = pe.matmul(b_lv[:, h, :], xt[:, m % 2, h], ym[:, h], start=True, stop=True)
                            last.then_inc(z_ready, 1)

                        def read_state(c):
                            m, at0 = c // 2, (c % 2) * CH
                            if c:
                                pe.wait_ge(state_ready, 2 * c)
                            if c >= 2 and c % 2 == 0:
                                pe.wait_ge(o_part, 2 * m)
                                pe.wait_ge(ot_kept, m)
                            tok = slice(m * P + at0, m * P + at0 + CH)
                            for h in range(4):
                                half = slice((h % 2) * CH, (h % 2) * CH + CH)
                                for a in range(2):
                                    o = a * 2 * HD + (h // 2) * HD
                                    last = pe.matmul(b_s[at0:at0 + CH, h % 2, o:o + HD], reg[half, 2 * a + h // 2, tok],
                                                     state(c)[half, h // 2], start=True, stop=True)
                            last.then_inc(ks_ready, 1)

                        def new_values(c):
                            m, at0 = c // 2, (c % 2) * CH
                            pe.wait_ge(r_ready, 4 * c + 4)
                            if c:
                                pe.wait_ge(vn_kept, c)
                            if m and c == 2 * m:
                                pe.wait_ge(o_sum, m)
                            half = slice(at0, at0 + CH)
                            for h in range(4):
                                last = pe.matmul(b_vn[half, 0, h], xt[half, m % 2, h, half], rr[half, h], start=True, stop=True)
                            last.then_inc(vn_ready, 1)

                        def update_state(c):
                            m, at0 = c // 2, (c % 2) * CH
                            half = slice(at0, at0 + CH)
                            pe.wait_ge(vn_kept, c + 1)
                            for h in range(4):
                                o = (h // 2) * HD
                                last = pe.matmul(b_ds[(h % 2) * CH:(h % 2) * CH + CH, o:o + HD], kd[half, m % 2, h], vn[half, h],
                                                 start=True, stop=True)
                            last.then_inc(ds_ready, 1)

                        def outputs(m):
                            pe.wait_ge(vn_kept, 2 * m + 2)
                            for h in range(4):
                                last = pe.matmul(b_vn[:, 1, h], qk[:, m % 2, h], vn[:, h], start=True, stop=True)
                            last.then_inc(o_ready, 1)

                        def outputs_transposed(m):
                            pe.wait_ge(o_normed, m + 1)
                            for a in range(2):
                                last = pe.transpose(b_ot[:, a * P:(a + 1) * P],
                                                    oo[:, 2 * a:2 * a + 2, :].rearrange("p h v -> p (h v)"), ident)
                            last.then_inc(ot_ready, 1)

                        def beside(m, point):
                            side.products(pe, FIRST[m][point], POINTS[point])

                        for m in range(TILES + 1):
                            new, old = m < TILES, m > 0
                            c = 2 * (m - 1)
                            if new:
                                decay(m)
                                kq(m)
                                beside(m, 0)
                                rows(m)
                            if old:
                                read_state(c)
                            if new:
                                beside(m, 1)
                                x0(m)
                            if old:
                                new_values(c)
                            if new:
                                level_y(m, 1)
                                beside(m, 2)
                            if old:
                                update_state(c)
                            if new:
                                level_z(m, 1)
                                beside(m, 3)
                            if old:
                                read_state(c + 1)
                            if new:
                                level_y(m, 2)
                                beside(m, 4)
                            if old:
                                new_values(c + 1)
                            if new:
                                level_z(m, 2)
                                beside(m, 5)
                            if old:
                                update_state(c + 1)
                            if new:
                                level_y(m, 3)
                                beside(m, 6)
                            if old:
                                outputs(m - 1)
                            if new:
                                level_z(m, 3)
                                beside(m, 7)
                                level_y(m, 4)
                                beside(m, 8)
                                level_z(m, 4)
                                beside(m, 9)
                            if old:
                                outputs_transposed(m - 1)
                            if new:
                                level_y(m, 5)
                                beside(m, 10)
                                level_z(m, 5)
                                beside(m, 11)

                    @block.scalar
                    def _(act):
                        def keep_y(m, l):
                            act.wait_ge(y_ready, NL * m + l)
                            act.activation(ym[:, :, :], b_lv[:, :, :], ACT.Copy).then_inc(y_kept, 1)
                            keep_beside(m, (0, 1, 2) if l == 1 else (2 * l - 1, 2 * l))

                        def keep_beside(m, points):
                            for p in points:
                                for n in range(FIRST[m][p] // KT, min((FIRST[m][p] + POINTS[p]) // KT, side.units)):
                                    side.keep(act, n)

                        for m in range(TILES + 1):
                            if m < TILES:
                                act.wait_ge(dec_ready, m + 1)
                                if m:
                                    act.wait_ge(at_ready, 4 * m)
                                    act.wait_ge(qk_ready, 2 * m)
                                for h in range(4):
                                    act.activation(dec[:, h, :], b_dr[:, h, :], ACT.Exp, bias=cx["ngc"][:, m, h:h + 1]).then_inc(dec_done, 1)
                                act.wait_ge(rows_ready, m + 1)
                                if m >= 2:
                                    act.wait_ge(r_ready, 8 * (m - 1))
                                act.activation(vr[:, m % 2], b_dr[:, 2:4, :].rearrange("p a (b v) -> p (a b) v", b=2), ACT.Copy).then_inc(v_kept, 1)
                                act.wait_ge(x0_ready, m + 1)
                                act.activation(xm[:, :, :], b_lv[:, :, :], ACT.Copy).then_inc(x0_kept, 1)
                                for l in range(1, 5):
                                    keep_y(m, l)
                            if m:
                                act.wait_ge(o_rss, m)
                                act.activation(oln[:, :], oss[:, :], ACT.Ln, bias=eps, scale=1.0 / HD).then_inc(o_ln, 1)
                                act.wait_ge(o_ln, m)
                                act.activation(ors[:, :], oln[:, :], ACT.Exp, scale=-0.5).then_inc(o_rstd, 1)
                            if m < TILES:
                                keep_y(m, 5)
                            if m:
                                act.wait_ge(ot_ready, m)
                                act.activation(reg[:, 0:2, cols(m - 1)], b_ot.rearrange("p (a t) -> p a t", a=2),
                                               ACT.Copy).then_inc(ot_kept, 1)
                            if m < TILES:
                                keep_beside(m, (11,))

                    @block.vector
                    def _(dve):
                        def products(m):
                            dve.wait_ge(kq_ready, m + 1)
                            dve.wait_ge(dec_done, 4 * m + 4)
                            if m:
                                dve.wait_ge(level, LEVELS * m)
                            for h in range(4):
                                dve.scalar_tensor_tensor(out=at[:, h, :], in0=b_kq[:, h % 2, h // 2, 1], scalar=cx["beta"][:, m, h:h + 1],
                                                         in1=dec[:, h, :], op0=ALU.mult, op1=ALU.mult).then_inc(at_ready, 1)
                            if m >= 2:
                                dve.wait_ge(o_ready, m - 1)
                            for b in range(2):
                                dve.tensor_tensor(qk[:, m % 2, b::2, :], b_kq[:, b, :, 0, :], dec[:, b::2, :], ALU.mult).then_inc(qk_ready, 1)
                            dve.wait_ge(v_kept, m + 1)
                            if m >= 2:
                                dve.wait_ge(ds_ready, 2 * (m - 1))
                            dve.tensor_tensor(kd[:, m % 2], b_dr[:, 0:2, :].rearrange("p a (b v) -> p (a b) v", b=2),
                                              cx["ekd"][:, m, :].unsqueeze(2).to_broadcast([P, 4, HD]), ALU.mult).then_inc(rows_kept, 1)

                        def first_inverse(m):
                            dve.wait_ge(level, LEVELS * m + 1)
                            if m >= 2:
                                dve.wait_ge(vn_ready, 2 * (m - 1))
                            dve.tensor_tensor(xt[:, m % 2], wide(ident, 4), atl[:, 0], ALU.subtract).then_inc(xt0_ready, 1)

                        def level_sub(m, l):
                            dve.wait_ge(z_ready, NL * m + l)
                            dve.tensor_tensor(xt[:, m % 2], xt[:, m % 2], b_lt, ALU.subtract).then_inc(x_new, 1)
                            if l < NL:
                                dve.tensor_tensor(xm[:, :, :], xm[:, :, :], b_lv, ALU.subtract).then_inc(x_new, 1)

                        def residual(c):
                            m, at0 = c // 2, (c % 2) * CH
                            half = slice(at0, at0 + CH)
                            dve.wait_ge(ks_ready, c + 1)
                            dve.wait_ge(rows_kept, m + 1)
                            if c:
                                dve.wait_ge(vn_ready, c)
                            for h in range(4):
                                o = 2 * HD + (h // 2) * HD
                                dve.scalar_tensor_tensor(out=rr[half, h], in0=b_s[half, h % 2, o:o + HD], scalar=cx["neg_eg"][half, m, h:h + 1],
                                                         in1=vr[half, m % 2, h], op0=ALU.mult, op1=ALU.add).then_inc(r_ready, 1)

                        def values(c):
                            m, at0 = c // 2, (c % 2) * CH
                            half = slice(at0, at0 + CH)
                            dve.wait_ge(vn_ready, c + 1)
                            if c >= 2 and c % 2 == 0:
                                dve.wait_ge(o_ready, m)
                            dve.tensor_tensor(vn[half], b_vn[half, 0], cx["beta"][half, m, :].unsqueeze(2).to_broadcast([CH, 4, HD]),
                                              ALU.mult).then_inc(vn_kept, 1)

                        def new_state(c):
                            dve.wait_ge(ds_ready, c + 1)
                            for a in range(2):
                                s_ = state(c)[:, a]
                                dve.scalar_tensor_tensor(out=s_, in0=s_, scalar=cx["gl"][:, c // 2, c % 2, a:a + 1],
                                                         in1=b_ds[:, a * HD:(a + 1) * HD], op0=ALU.mult, op1=ALU.add).then_inc(state_ready, 1)

                        def finish(m):
                            dve.wait_ge(o_ready, m + 1)
                            if m:
                                dve.wait_ge(ot_ready, m)
                            for b in range(2):
                                dve.tensor_tensor(oo[:, b::2, :], b_s[:, b, 0:2 * HD].rearrange("p (a v) -> p a v", a=2),
                                                  cx["eg"][:, m, b::2].unsqueeze(2).to_broadcast([P, 2, HD]), ALU.mult).then_inc(o_part, 1)
                            dve.wait_ge(o_part, 2 * m + 2)
                            dve.tensor_tensor(oo[:, :, :], oo[:, :, :], b_vn[:, 1], ALU.add).then_inc(o_sum, 1)
                            dve.wait_ge(o_sum, m + 1)
                            dve.tensor_tensor(osq[:, :, :], oo[:, :, :], oo[:, :, :], ALU.mult).then_inc(o_squared, 1)
                            dve.wait_ge(o_squared, m + 1)
                            dve.tensor_reduce(oss[:, :], osq[:, :, :], AX.X, ALU.add).then_inc(o_rss, 1)

                        for m in range(TILES + 1):
                            new, old = m < TILES, m > 0
                            c = 2 * (m - 1)
                            if new:
                                products(m)
                            if old:
                                residual(c)
                            if new:
                                first_inverse(m)
                            if old:
                                values(c)
                                new_state(c)
                            if new:
                                level_sub(m, 1)
                            if old:
                                residual(c + 1)
                                values(c + 1)
                            if new:
                                level_sub(m, 2)
                            if old:
                                new_state(c + 1)
                            if new:
                                level_sub(m, 3)
                            if old:
                                finish(m - 1)
                            if new:
                                level_sub(m, 4)
                                level_sub(m, 5)

        def key_rows(dve_src, n_tiles, first_tile, outs):
            with ExitStack() as st:
                kr = sb("kr", [P, 4, len(dve_src) * P], st=st)
                bank = pb("bank", [P, 4, 512], st)
                turned, kept = sem("turned", st), sem("kept", st)
                stored = [sem(f"stored{i}", st) for i in range(4)]
                W = len(dve_src) * P
                total = [0, 0, 0, 0]
                with nc.Block() as block:
                    @block.tensor
                    def _(pe):
                        for n in range(n_tiles):
                            m = first_tile + n
                            if n >= 4:
                                pe.wait_ge(kept, n - 3)
                            for a, r in enumerate(dve_src):
                                last = pe.transpose(bank[:, n % 4, a * P:(a + 1) * P], reg[:, r, m * P:(m + 1) * P], ident)
                            last.then_inc(turned, 1)

                    def stores(n):
                        return outs(first_tile + n)

                    @block.vector
                    def _(dve):
                        done = [0, 0, 0, 0]
                        for n in range(n_tiles):
                            dve.wait_ge(turned, n + 1)
                            if n >= 4:
                                dve.wait_ge(stored[n % 4], done[n % 4])
                            dve.tensor_copy(kr[:, n % 4, :], bank[:, n % 4, 0:W]).then_inc(kept, 1)
                            done[n % 4] += 16 * len(stores(n))

                    @block.sync
                    def _(sp):
                        for n in range(n_tiles):
                            sp.wait_ge(kept, n + 1)
                            for dst, rows in stores(n):
                                sp.dma_start(dst, kr[rows, n % 4, :]).then_inc(stored[n % 4], 16)
                                total[n % 4] += 16
                        for i in range(4):
                            if total[i]:
                                sp.wait_ge(stored[i], total[i])

        def a_key_stores(m):
            pk = io["p_a_k"][0, 0].rearrange("t h d -> t (h d)")
            sk = io["s_a_k"][0, 0].rearrange("t h d -> t (h d)")
            if m == LAST - 1:
                return [(pk[0:WIN - SP0, :], slice(SP0, P))]
            return [(pk[WIN - SP0:WIN, :], slice(0, SP0)), (sk[WIN - NSAMP:WIN, :], slice(SP0, SP0 + NSAMP))]

        def b_key_stores(m):
            pk = io["p_b_k"][0, 0].rearrange("t h d -> t (h d)")
            sk = io["s_b_k"][0, 0].rearrange("t h d -> t (h d)")
            if m == 0:
                return [(pk[0:P - PAD, :], slice(PAD, P))]
            if m == LAST:
                return [(pk[m * P - PAD:m * P - PAD + SP0, :], slice(0, SP0)), (sk, slice(SP0, SP0 + NSAMP))]
            return [(pk[m * P - PAD:(m + 1) * P - PAD, :], slice(0, P))]

        def window_attention():
            with ExitStack() as st:
                kc = sb("kc", [P, P], st=st)
                vc = sb("vc", [P, P], st=st)
                kcT = sb("kcT", [P, P], st=st)
                nsink = sb("nsink", [P, AH], st=st)
                sink = sb("sink", [P, AH], st=st)
                pr = sb("pr", [P, 2, AG, 2 * P], st=st)
                pt = sb("pt", [P, 2, 2, AG, P], st=st)
                mx, nm, den, se, rd = (sb(n, [P, 2, AG], st=st) for n in ("mx", "nm", "den", "se", "rd"))
                b_sc = pb("b_sc", [P, 2, AG, 2 * P], st)
                b_pt = pb("b_pt", [P, 2, AG, P], st)
                b_o = pb("b_o", [P, 2, AG, P], st)
                names = ("cache_in sink_in turned kct_kept nsink_ready scores_ready max_ready bias_ready exp_done sink_biased sink_exp "
                         "den_ready recip_ready normed pt_ready pt_kept_act pt_kept_dve o_ready o_kept").split()
                (cache_in, sink_in, turned, kct_kept, nsink_ready, scores_ready, max_ready, bias_ready, exp_done, sink_biased, sink_exp,
                 den_ready, recip_ready, normed, pt_ready, pt_kept_act, pt_kept_dve, o_ready, o_kept) = (sem(n, st) for n in names)
                spilled = [sem(f"spilled{b}", st) for b in range(NBLK)]
                qk_in = [sem(f"qk_in{b}", st) for b in range(NBLK)]
                vA = vrow
                units = [(m, j) for m in range(TILES + 1) for j in range(AKV)]
                N = len(units)

                def keys(m):
                    return P if m == 0 else (WIN + NSAMP if m == TILES else 2 * P)

                def rows_of(m):
                    return NSAMP if m == TILES else P

                def key_tiles(m, j):
                    d = slice(j * HD, (j + 1) * HD)
                    if m == 0:
                        return [(vA[:, 0, d], slice(0, P), 0)]
                    if m == TILES:
                        new = slice(SP0, SP0 + NSAMP)
                        return [(vc[:, d], slice(0, P), 0), (vA[new, LAST, d], new, WIN)]
                    return [(vA[:, m - 1, d], slice(0, P), 0), (vA[:, m, d], slice(0, P), P)]

                with nc.Block() as block:
                    @block.sync
                    def _(sp):
                        sp.dma_start(kc[:, :], io["cache_a_k"][0, 0].rearrange("t h d -> t (h d)")).then_inc(cache_in, 16)
                        sp.dma_start(vc[:, :], io["cache_a_v"][0, 0].rearrange("t h d -> t (h d)")).then_inc(cache_in, 16)
                        sp.dma_start(sink[:, :], io["sinks_a"].to_broadcast([P, AH])).then_inc(sink_in, 16)
                        for b, (c0, w) in enumerate(BLOCKS):
                            sp.dma_start(mix[6:8, :, c0:c0 + w].rearrange("k p t -> p k t"), reg[:, 0:2, c0:c0 + w]).then_inc(spilled[b], 16)
                            sp.dma_start(reg[:, 2:5, c0:c0 + w], uT[2:5, :, c0:c0 + w].rearrange("k p t -> p k t")).then_inc(qk_in[b], 16)
                        for b, (c0, w) in enumerate(BLOCKS):
                            sp.wait_ge(spilled[b], 16)
                            sp.dma_start(reg[:, 0:2, c0:c0 + w], uT[0:2, :, c0:c0 + w].rearrange("k p t -> p k t")).then_inc(qk_in[b], 16)

                    @block.tensor
                    def _(pe):
                        pe.wait_ge(cache_in, 32)
                        pe.transpose(b_pt[:, 0, 0, :], kc[:, :], ident).then_inc(turned, 1)
                        pe.wait_ge(kct_kept, 1)

                        def scores(n):
                            m, j = units[n]
                            R, K = rows_of(m), keys(m)
                            if j == 0 and m % 4 == 0 and m < TILES:
                                pe.wait_ge(qk_in[m // 4], 32)
                            if n:
                                pe.wait_ge(exp_done, AG * n)
                            half = slice(j * CH, (j + 1) * CH)
                            q0 = SROW if m == TILES else m * P
                            for a in range(0, AG, 2):
                                if m < TILES:
                                    at = M_A0 if m == 0 else (M_A1 if m == 1 else M_A)
                                    pe.matmul(b_sc[:, n % 2, a:a + 2, 0:K], identb, wide(cb[:, at:at + K], 2), start=True, stop=False,
                                              skip_group_check=True)
                            for g in range(AG):
                                qh = reg[half, g, q0:q0 + R]
                                if m < TILES:
                                    k0 = max(m - 1, 0) * P
                                    last = pe.matmul(b_sc[0:R, n % 2, g, 0:K], qh, reg[half, 4, k0:k0 + K], start=False, stop=True,
                                                     skip_group_check=True)
                                else:
                                    pe.matmul(b_sc[0:R, n % 2, g, 0:WIN], qh, kcT[half, :], start=True, stop=True)
                                    last = pe.matmul(b_sc[0:R, n % 2, g, WIN:K], qh, reg[half, 4, SROW:SROW + NSAMP], start=True, stop=True)
                            last.then_inc(scores_ready, 1)

                        def turn(n):
                            m, j = units[n]
                            R = rows_of(m)
                            pe.wait_ge(normed, AG * (n + 1))
                            if n:
                                pe.wait_ge(pt_kept_act, n)
                                pe.wait_ge(pt_kept_dve, n)
                            for t, (_, part, k0) in enumerate(key_tiles(m, j)):
                                kn = part.stop - part.start
                                for g in range(AG):
                                    last = pe.transpose(b_pt[0:kn, t, g, 0:R], pr[0:R, n % 2, g, k0:k0 + kn], ident[0:R, 0:R])
                            last.then_inc(pt_ready, 1)

                        def values(n):
                            m, j = units[n]
                            R = rows_of(m)
                            pe.wait_ge(pt_kept_act, n + 1)
                            pe.wait_ge(pt_kept_dve, n + 1)
                            if n >= 4 and j == 0:
                                pe.wait_ge(o_kept, n // 2 - 1)
                            tiles_ = key_tiles(m, j)
                            for t, (v, part, k0) in enumerate(tiles_):
                                last = pe.matmul(b_o[j * CH:(j + 1) * CH, m % 2, :, 0:R], v, pt[part, n % 2, t, :, 0:R],
                                                 start=(t == 0), stop=(t == len(tiles_) - 1))
                            last.then_inc(o_ready, 1)

                        for n in range(N + 2):
                            if n < N:
                                scores(n)
                            if 1 <= n <= N:
                                turn(n - 1)
                            if n >= 2:
                                values(n - 2)

                    @block.scalar
                    def _(act):
                        def exps(n):
                            m, j = units[n]
                            R, K = rows_of(m), keys(m)
                            act.wait_ge(bias_ready, n + 1)
                            if n >= 2:
                                act.wait_ge(pt_ready, n - 1)
                            for g in range(AG):
                                act.activation(pr[0:R, n % 2, g, 0:K], b_sc[0:R, n % 2, g, 0:K], ACT.Exp, bias=nm[0:R, n % 2, g:g + 1],
                                               scale=SCALE, accum_out=den[0:R, n % 2, g:g + 1]).then_inc(exp_done, 1)
                            act.wait_ge(sink_biased, n + 1)
                            act.activation(se[0:R, n % 2, :], se[0:R, n % 2, :], ACT.Exp).then_inc(sink_exp, 1)

                        def keep(n):
                            m, j = units[n]
                            R = rows_of(m)
                            act.wait_ge(pt_ready, n + 1)
                            if n >= 2:
                                act.wait_ge(o_ready, n - 1)
                            act.activation(pt[:, n % 2, 0, :, 0:R], b_pt[:, 0, :, 0:R], ACT.Copy).then_inc(pt_kept_act, 1)

                        for n in range(N + 1):
                            if n < N:
                                exps(n)
                            if n >= 1:
                                keep(n - 1)

                    @block.vector
                    def _(dve):
                        dve.wait_ge(turned, 1)
                        dve.tensor_copy(kcT[:, :], b_pt[:, 0, 0, :]).then_inc(kct_kept, 1)
                        dve.wait_ge(sink_in, 16)
                        dve.tensor_scalar(nsink[:, :], sink[:, :], -1.0, None, ALU.mult).then_inc(nsink_ready, 1)
                        dve.wait_ge(nsink_ready, 1)

                        def bias(n):
                            m, j = units[n]
                            R, K = rows_of(m), keys(m)
                            hs = slice(j * AG, (j + 1) * AG)
                            dve.wait_ge(scores_ready, n + 1)
                            dve.tensor_reduce(mx[0:R, n % 2, :], b_sc[0:R, n % 2, :, 0:K], AX.X, ALU.max).then_inc(max_ready, 1)
                            dve.wait_ge(max_ready, n + 1)
                            if n >= 2:
                                dve.wait_ge(exp_done, AG * (n - 1))
                            dve.scalar_tensor_tensor(out=nm[0:R, n % 2, :], in0=mx[0:R, n % 2, :], scalar=-SCALE, in1=nsink[0:R, hs],
                                                     op0=ALU.mult, op1=ALU.min).then_inc(bias_ready, 1)
                            dve.wait_ge(bias_ready, n + 1)
                            dve.tensor_tensor(se[0:R, n % 2, :], sink[0:R, hs], nm[0:R, n % 2, :], ALU.add).then_inc(sink_biased, 1)

                        def norm(n):
                            m, j = units[n]
                            R, K = rows_of(m), keys(m)
                            dve.wait_ge(sink_exp, n + 1)
                            dve.wait_ge(exp_done, AG * (n + 1))
                            dve.tensor_tensor(den[0:R, n % 2, :], den[0:R, n % 2, :], se[0:R, n % 2, :], ALU.add).then_inc(den_ready, 1)
                            dve.wait_ge(den_ready, n + 1)
                            dve.reciprocal(rd[0:R, n % 2, :], den[0:R, n % 2, :]).then_inc(recip_ready, 1)
                            dve.wait_ge(recip_ready, n + 1)
                            for g in range(AG):
                                x = pr[0:R, n % 2, g, 0:K]
                                dve.tensor_scalar(x, x, rd[0:R, n % 2, g:g + 1], None, ALU.mult).then_inc(normed, 1)

                        def keep(n):
                            m, j = units[n]
                            R = rows_of(m)
                            dve.wait_ge(pt_ready, n + 1)
                            if n >= 2:
                                dve.wait_ge(o_ready, n - 1)
                            part = key_tiles(m, j)[-1][1]
                            if m == 0:
                                dve.memset(pt[:, n % 2, 1, :, :], 0.0).then_inc(pt_kept_dve, 1)
                            else:
                                dve.tensor_copy(pt[part, n % 2, 1, :, 0:R], b_pt[0:part.stop - part.start, 1, :, 0:R]).then_inc(pt_kept_dve, 1)

                        def keep_out(m):
                            dve.wait_ge(o_ready, 2 * m + 2)
                            q0, cnt = (SROW, NSAMP) if m == TILES else (m * P, SP0 if m == LAST else P)
                            dve.tensor_copy(reg[:, 0:AG, q0:q0 + cnt], b_o[:, m % 2, :, 0:cnt]).then_inc(o_kept, 1)

                        for n in range(N + 3):
                            if n < N:
                                bias(n)
                            if n < N:
                                norm(n)
                            if 1 <= n <= N:
                                keep(n - 1)
                            if n >= 3 and (n - 3) % 2:
                                keep_out((n - 3) // 2)

        def stick_breaking(side_tiles):
            KC = 512
            QS, KS = 0, 4
            with ExitStack() as st:
                kc = sb("kc", [P, 2, VBW], st=st)
                vc = sb("vc", [P, 2, VBW], st=st)
                kcT = sb("kcT", [P, 2, PAST], st=st)
                keepb = sb("keepb", [P, 2, KC], st=st)
                beta = sb("beta", [P, 2, KC], st=st)
                prod = sb("prod", [P, T + 1], st=st)
                w = sb("w", [P, 2, KC], st=st)
                wt = sb("wt", [P, 2, 4, P], st=st)
                b_z = pb("b_z", [P, 2, KC], st)
                b_w = pb("b_w", [P, 2, 4, P], st)
                b_o = pb("b_o", [P, 2, 512], st)
                side = SideProjection(st, "silu", side_tiles, sz)
                spilled = [sem(f"spilled{b}", st) for b in range(NBLK)]
                qk_in = [sem(f"qk_in{b}", st) for b in range(NBLK)]
                names = ("cache_in turned kct_kept z_ready keep_ready beta_ready one_ready prod_ready w_ready wt_ready wt_kept o_ready o_kept part_kept").split()
                (cache_in, turned, kct_kept, z_ready, keep_ready, beta_ready, one_ready, prod_ready, w_ready, wt_ready, wt_kept, o_ready,
                 o_kept, part_kept) = (sem(n, st) for n in names)
                new = slice(SP0, SP0 + NSAMP)

                def side_piece(s):
                    return side.pieces * s // (N - 1)

                def side_units(s):
                    return range(side_piece(s) // KT, min(side_piece(s + 1) // KT, side.units))
                steps = []
                for m in range(TILES + 1):
                    for h in range(BH):
                        if m == TILES:
                            steps.append((m, h, 0, PAST + NSAMP, True, True))
                            continue
                        L = (m + 1) * P
                        for k0 in range((L - 1) // KC * KC, -1, -KC):
                            steps.append((m, h, k0, min(KC, L - k0), k0 + KC >= L, k0 == 0))
                N = len(steps)
                rowno = []
                for s_ in steps:
                    rowno.append((rowno[-1] if rowno else -1) + s_[4])

                def rows_of(m):
                    return NSAMP if m == TILES else P

                def end(m):
                    return PAST + NSAMP if m == TILES else (m + 1) * P

                def key_tiles(s):
                    m, h, k0, nk = steps[s][:4]
                    d = slice(VAW + h * HD, VAW + (h + 1) * HD)
                    if m == TILES:
                        dc = slice(h * HD, (h + 1) * HD)
                        return [(vc[:, 0, dc], slice(0, P), 0), (vc[:, 1, dc], slice(0, P), P), (vrow[new, LAST, d], new, PAST)]
                    return [(vrow[:, k0 // P + t, d], slice(0, P), t * P) for t in range(nk // P)]

                def keep_weights(eng, s, copy):
                    eng.wait_ge(wt_ready, s + 1)
                    if s >= 2:
                        eng.wait_ge(o_ready, s - 1)
                    if s >= 1:
                        eng.wait_ge(wt_kept, s)
                    R = rows_of(steps[s][0])
                    tiles_ = key_tiles(s)
                    full = [t for t, x in enumerate(tiles_) if x[1].stop - x[1].start == P]
                    if len(full) == len(tiles_):
                        copy(wt[:, s % 2, 0:len(full), 0:R], b_w[:, s % 2, 0:len(full), 0:R]).then_inc(wt_kept, 1)
                    else:
                        copy(wt[:, s % 2, 0:len(full), 0:R], b_w[:, s % 2, 0:len(full), 0:R]).then_inc(part_kept, 1)
                        eng.wait_ge(part_kept, steps[s][1] + 1)
                        copy(wt[new, s % 2, len(full), 0:R], b_w[0:NSAMP, s % 2, len(full), 0:R]).then_inc(wt_kept, 1)

                with nc.Block() as block:
                    @block.sync
                    def _(sp):
                        for name, dst in (("cache_b_k", kc), ("cache_b_v", vc)):
                            sp.dma_start(dst[:, :, :], io[name][0, 0].rearrange("(t p) h d -> p t (h d)", p=P)).then_inc(cache_in, 16)
                        for b, (c0, w) in enumerate(BLOCKS):
                            sp.dma_start(mix[0:4, :, c0:c0 + w].rearrange("k p t -> p k t"), reg[:, 0:4, c0:c0 + w]).then_inc(spilled[b], 16)
                            sp.dma_start(reg[:, KS:KS + 2, c0:c0 + w], uT[7:9, :, c0:c0 + w].rearrange("k p t -> p k t")).then_inc(qk_in[b], 16)
                            sp.wait_ge(spilled[b], 16)
                            sp.dma_start(reg[:, QS:QS + 2, c0:c0 + w], uT[5:7, :, c0:c0 + w].rearrange("k p t -> p k t")).then_inc(qk_in[b], 16)
                        side.transfers(sp)

                    @block.tensor
                    def _(pe):
                        pe.wait_ge(cache_in, 32)
                        for a in range(2):
                            for t in range(2):
                                last = pe.transpose(b_w[:, 0, 2 * a + t, :], kc[:, t, a * P:(a + 1) * P], ident)
                        last.then_inc(turned, 1)
                        pe.wait_ge(kct_kept, 1)

                        def scores(s):
                            m, h, k0, nk, first, last_ = steps[s]
                            R = rows_of(m)
                            half = slice((h % 2) * CH, (h % 2) * CH + CH)
                            if first and h == 0 and m % 4 == 0 and m < TILES:
                                pe.wait_ge(qk_in[m // 4], 32)
                            if s >= 2:
                                pe.wait_ge(keep_ready, s - 1)
                                pe.wait_ge(beta_ready, s - 1)
                            bank = b_z[0:R, s % 2]
                            q0 = SROW if m == TILES else m * P
                            q = reg[half, QS + h // 2, q0:q0 + R]
                            if m == TILES:
                                pe.matmul(bank[:, 0:PAST], q, kcT[half, h // 2, :], start=True, stop=True)
                                last = pe.matmul(bank[:, PAST:nk], q, reg[half, KS + h // 2, SROW:SROW + NSAMP], start=True, stop=False,
                                                 skip_group_check=True)
                                last = pe.matmul(bank[:, PAST:nk], identb[0:R, 0:R], cb[0:R, M_B:M_B + NSAMP], start=False, stop=True,
                                                 skip_group_check=True)
                            else:
                                masks = ([(nk - P, M_B)] if first else []) + ([(0, M_PAD)] if last_ else [])
                                last = pe.matmul(bank[:, 0:nk], q, reg[half, KS + h // 2, k0:k0 + nk], start=True, stop=not masks,
                                                 skip_group_check=True)
                                for n, (at, mask) in enumerate(masks):
                                    last = pe.matmul(bank[:, at:at + P], identb, cb[:, mask:mask + P], start=False,
                                                     stop=(n == len(masks) - 1), skip_group_check=True)
                            last.then_inc(z_ready, 1)

                        def turn(s):
                            R = rows_of(steps[s][0])
                            pe.wait_ge(w_ready, s + 1)
                            if s >= 2:
                                pe.wait_ge(wt_kept, s - 1)
                            for t, (_, part, at) in enumerate(key_tiles(s)):
                                kn = part.stop - part.start
                                last = pe.transpose(b_w[0:kn, s % 2, t, 0:R], w[0:R, s % 2, at:at + kn], ident[0:R, 0:R])
                            last.then_inc(wt_ready, 1)

                        def values(s):
                            m, h, k0, nk, first, last_ = steps[s]
                            R = rows_of(m)
                            pe.wait_ge(wt_kept, s + 1)
                            row = rowno[s]
                            pair = row // 2
                            if first and h % 2 == 0 and pair >= 2:
                                pe.wait_ge(o_kept, pair - 1)
                            tiles_ = key_tiles(s)
                            for t, (v, part, at) in enumerate(tiles_):
                                last = pe.matmul(b_o[(h % 2) * CH:(h % 2) * CH + CH, pair % 2, 0:R], v, wt[part, s % 2, t, 0:R],
                                                 start=(first and t == 0), stop=(last_ and t == len(tiles_) - 1))
                            last.then_inc(o_ready, 1)

                        for s in range(N + 3):
                            if s < N:
                                scores(s)
                                side.products(pe, side_piece(s), side_piece(s + 1) - side_piece(s))
                            if 2 <= s < N + 2:
                                turn(s - 2)
                            if s >= 3:
                                values(s - 3)

                    @block.scalar
                    def _(act):
                        def sigmoids(s):
                            m, h, k0, nk, first, last_ = steps[s]
                            R = rows_of(m)
                            act.wait_ge(z_ready, s + 1)
                            if s >= 2:
                                act.wait_ge(prod_ready, s - 1)
                            act.activation(keepb[0:R, s % 2, 0:nk], b_z[0:R, s % 2, 0:nk], ACT.Sigmoid, scale=-SCALE).then_inc(keep_ready, 1)
                            if s >= 2:
                                act.wait_ge(w_ready, s - 1)
                            act.activation(beta[0:R, s % 2, 0:nk], b_z[0:R, s % 2, 0:nk], ACT.Sigmoid, scale=SCALE).then_inc(beta_ready, 1)

                        def keep(s):
                            keep_weights(act, s, lambda o, i: act.activation(o, i, ACT.Copy))

                        for s in range(N + 3):
                            if s < N:
                                sigmoids(s)
                                for n in side_units(s):
                                    side.keep(act, n)
                            if s >= 3 and (s - 3) % 2:
                                keep(s - 3)

                    @block.gpsimd
                    def _(pool):
                        for s, (m, h, k0, nk, first, last_) in enumerate(steps):
                            R = rows_of(m)
                            pool.wait_ge(prod_ready, s + 1)
                            pool.wait_ge(beta_ready, s + 1)
                            if s >= 2:
                                pool.wait_ge(wt_ready, s - 1)
                            pool.tensor_tensor(w[0:R, s % 2, 0:nk], beta[0:R, s % 2, 0:nk], prod[0:R, k0 + 1:k0 + nk + 1],
                                               ALU.mult).then_inc(w_ready, 1)

                    @block.vector
                    def _(dve):
                        dve.wait_ge(turned, 1)
                        dve.tensor_copy(kcT[:, :, :], b_w[:, 0, :, :].rearrange("p (a t) k -> p a (t k)", a=2)).then_inc(kct_kept, 1)

                        def scan(s):
                            m, h, k0, nk, first, last_ = steps[s]
                            R = rows_of(m)
                            if first:
                                if s:
                                    dve.wait_ge(w_ready, s)
                                dve.memset(prod[0:R, k0 + nk:k0 + nk + 1], 1.0).then_inc(one_ready, 1)
                                dve.wait_ge(one_ready, rowno[s] + 1)
                            else:
                                dve.wait_ge(prod_ready, s)
                            dve.wait_ge(keep_ready, s + 1)
                            kv = keepb[0:R, s % 2, 0:nk][:, ::-1]
                            dve.tensor_tensor_scan(prod[0:R, k0:k0 + nk][:, ::-1], kv, kv, prod[0:R, k0 + nk:k0 + nk + 1],
                                                   ALU.mult, ALU.bypass).then_inc(prod_ready, 1)

                        def keep_out(pair):
                            m, a = pair // 2, pair % 2
                            q0, cnt = (SROW, NSAMP) if m == TILES else (m * P, SP0 if m == LAST else P)
                            dve.tensor_copy(reg[:, QS + a, q0:q0 + cnt], b_o[:, pair % 2, 0:cnt]).then_inc(o_kept, 1)

                        for s in range(N + 4):
                            if s < N:
                                scan(s)
                                for n in side_units(s):
                                    side.gate(dve, n)
                            if s >= 3 and s - 3 < N and (s - 3) % 2 == 0:
                                keep_weights(dve, s - 3, lambda o, i: dve.tensor_copy(o, i))
                            if s >= 4:
                                e = s - 4
                                if steps[e][5] and steps[e][1] % 2:
                                    dve.wait_ge(o_ready, e + 1)
                                    keep_out(rowno[e] // 2)

        def output():
            with ExitStack() as st:
                MIX0 = D
                gpost = sb("gpost", [P, D], st=st)
                xres = sb("xres", [P, 3, D], st=st)
                ssq, lnv, rstd = (sb(n, [P, 3], st=st) for n in ("ssq", "lnv", "rstd"))
                yy = sb("yy", [P, 3, D], st=st)
                b_y = pb("b_y", [P, 3, D], st)
                wo_in = sem("wo_in", st)
                mix_in = [sem(f"mix_in{i}", st) for i in range(3)]
                spilled, gated = sem("spilled", st), sem("gated", st)
                zin = sb("zin", [P, 3, KT, P], st=st)
                x_in = [sem(f"x_in{i}", st) for i in range(3)]
                y_out = [sem(f"y_out{i}", st) for i in range(3)]
                y_ready, sq_done, ln_done, rstd_done, normed, summed = (sem(n, st) for n in
                                                                      ("y_ready", "sq_done", "ln_done", "rstd_done", "normed", "summed"))
                xp, wo = io["x_prompt"][0], io["w_out"][0]
                yp = io["y_prompt"][0]
                with nc.Block() as block:
                    def rows(ap, n, base):
                        return ap[bass.ds(n * P + base, P), :]

                    @block.sync
                    def _(sp):
                        for b, (c0, w) in enumerate(BLOCKS):
                            sp.dma_start(mix[4:6, :, c0:c0 + w].rearrange("k p t -> p k t"), reg[:, 0:2, c0:c0 + w]).then_inc(spilled, 16)
                        for g in range(AG):
                            for j in range(AKV):
                                sp.dma_start(hT[j * CH:(j + 1) * CH, g, 0:D], wo[(j * AG + g) * HD:(j * AG + g + 1) * HD, :]).then_inc(wo_in, 16)
                        sp.dma_start(hT[:, AG:KT, 0:D], wo[AH * HD:D, :].rearrange("(k p) n -> p k n", p=P)).then_inc(wo_in, 16)
                        sp.dma_start(gpost[:, :], io["norm_post"].to_broadcast([P, D])).then_inc(wo_in, 16)

                        def load(n, s):
                            if not isinstance(n, int) or n >= 3:
                                sp.wait_ge(y_ready, n - 2)
                            c = slice(n * P, (n + 1) * P) if isinstance(n, int) else bass.ds(n * P, P)
                            sp.dma_start(hT[:, :, MIX0 + s * P:MIX0 + (s + 1) * P], mix[:, :, c].rearrange("k p t -> p k t")).then_inc(mix_in[s], 16)
                            sp.dma_start(zin[:, s], sz[:, :, c].rearrange("k p t -> p k t")).then_inc(mix_in[s], 16)
                            if not isinstance(n, int) or n >= 3:
                                sp.wait_ge(summed, n - 2)
                            if isinstance(n, int) and n == 0:
                                sp.dma_start(xres[CH:P, s, :], xp[0:CH, :]).then_inc(x_in[s], 32)
                            elif isinstance(n, int) and n == LAST:
                                sp.dma_start(xres[0:SP0, s, :], xp[SEQ - SP0:SEQ, :]).then_inc(x_in[s], 16)
                                sp.dma_start(xres[SP0:SP0 + NSAMP, s, :], io["x_sample"][0]).then_inc(x_in[s], 16)
                            else:
                                sp.dma_start(xres[:, s, :], rows(xp, n, -CH)).then_inc(x_in[s], 32)

                        sp.wait_ge(spilled, 16 * NBLK)
                        load(0, 0)
                        load(1, 1)
                        load(2, 2)
                        with sp.Fori(0, (TILES - 5) // 3) as i:
                            for u in range(3):
                                load(3 * i + (u + 3), u)
                        for n in range(LAST - 1, TILES):
                            load(n, n % 3)

                    @block.tensor
                    def _(pe):
                        pe.wait_ge(wo_in, 160)

                        def step(n, s):
                            pe.wait_ge(gated, n + 1)
                            if not isinstance(n, int) or n >= 3:
                                pe.wait_ge(normed, n - 2)
                            for c in range(2):
                                for k in range(KT):
                                    last = pe.matmul(b_y[:, s, c * 512:(c + 1) * 512], hT[:, k, MIX0 + s * P:MIX0 + (s + 1) * P],
                                                     hT[:, k, c * 512:(c + 1) * 512], start=(k == 0), stop=(k == KT - 1))
                            last.then_inc(y_ready, 1)
                        for n in range(3):
                            step(n, n)
                        with pe.Fori(0, (TILES - 5) // 3) as i:
                            for u in range(3):
                                step(3 * i + (u + 3), u)
                        for n in range(LAST - 1, TILES):
                            step(n, n % 3)

                    @block.scalar
                    def _(act):
                        def step(n, s):
                            act.wait_ge(y_ready, n + 1)
                            if not isinstance(n, int) or n >= 3:
                                act.wait_ge(y_out[s], y_stored(n, s))
                            act.activation(yy[:, s], b_y[:, s, :], ACT.Square, accum_out=ssq[:, s:s + 1]).then_inc(sq_done, 1)
                            act.wait_ge(sq_done, n + 1)
                            act.activation(lnv[:, s:s + 1], ssq[:, s:s + 1], ACT.Ln, bias=eps, scale=1.0 / D).then_inc(ln_done, 1)
                            act.wait_ge(ln_done, n + 1)
                            act.activation(rstd[:, s:s + 1], lnv[:, s:s + 1], ACT.Exp, scale=-0.5).then_inc(rstd_done, 1)
                        it = {}

                        def y_stored(n, s):
                            return 32 * (n // 3) if isinstance(n, int) else it["i"] * 32 + 32

                        for n in range(3):
                            step(n, n)
                        with act.Fori(0, (TILES - 5) // 3) as i:
                            it["i"] = i
                            for u in range(3):
                                step(3 * i + (u + 3), u)
                        for n in range(LAST - 1, TILES):
                            step(n, n % 3)

                    @block.vector
                    def _(dve):
                        dve.wait_ge(wo_in, 160)

                        def gate(n, s, landed):
                            m_ = hT[:, :, MIX0 + s * P:MIX0 + (s + 1) * P]
                            dve.wait_ge(mix_in[s], landed)
                            dve.tensor_tensor(m_, m_, zin[:, s], ALU.mult).then_inc(gated, 1)

                        def norm(n, s):
                            dve.wait_ge(rstd_done, n + 1)
                            dve.scalar_tensor_tensor(out=yy[:, s], in0=b_y[:, s, :], scalar=rstd[:, s:s + 1], in1=gpost[:, :],
                                                     op0=ALU.mult, op1=ALU.mult).then_inc(normed, 1)

                        for n in range(3):
                            gate(n, n, 32)
                        norm(0, 0)
                        with dve.Fori(0, (TILES - 5) // 3) as i:
                            for u in range(3):
                                gate(3 * i + (u + 3), u, 32 * i + 64)
                                norm(3 * i + (u + 1), (u + 1) % 3)
                        for n in range(LAST - 1, TILES):
                            gate(n, n % 3, 32 * (n // 3 + 1))
                            norm(n - 2, (n - 2) % 3)
                        norm(LAST - 1, (LAST - 1) % 3)
                        norm(LAST, LAST % 3)

                    @block.gpsimd
                    def _(pool):
                        def step(n, s, landed, part):
                            pool.wait_ge(normed, n + 1)
                            pool.wait_ge(x_in[s], landed)
                            pool.tensor_tensor(yy[part, s], yy[part, s], xres[part, s, :], ALU.add).then_inc(summed, 1)
                            pool.wait_ge(summed, n + 1)

                        step(0, 0, 32, slice(CH, P))
                        pool.dma_start(yp[0:CH, :], yy[CH:P, 0]).then_inc(y_out[0], 32)
                        for n in (1, 2):
                            step(n, n, 32, slice(0, P))
                            pool.dma_start(yp[n * P - CH:(n + 1) * P - CH, :], yy[:, n]).then_inc(y_out[n], 32)
                        with pool.Fori(0, (TILES - 5) // 3) as i:
                            for u in range(3):
                                step(3 * i + (u + 3), u, 32 * i + 64, slice(0, P))
                                pool.dma_start(rows(yp, 3 * i + (u + 3), -CH), yy[:, u]).then_inc(y_out[u], 32)
                        n = LAST - 1
                        step(n, n % 3, 32 * (n // 3 + 1), slice(0, P))
                        pool.dma_start(yp[n * P - CH:(n + 1) * P - CH, :], yy[:, n % 3]).then_inc(y_out[n % 3], 32)
                        n = LAST
                        step(n, n % 3, 32 * (n // 3 + 1), slice(0, SP0 + NSAMP))
                        pool.dma_start(yp[SEQ - SP0:SEQ, :], yy[0:SP0, n % 3]).then_inc(y_out[n % 3], 16)
                        pool.dma_start(io["y_sample"][0], yy[SP0:SP0 + NSAMP, n % 3]).then_inc(y_out[n % 3], 16)
                        for s in range(3):
                            pool.wait_ge(y_out[s], 32 * len([n for n in range(TILES) if n % 3 == s]))

        def stage(work, *args, **kwargs):
            with nc.cleanup_on_exit():
                work(*args, **kwargs)

        stage(norm_and_transpose)
        stage(project_rows)
        stage(project, [("copy", [(XC, P, P)], 0, 6)])
        with ExitStack() as st:
            cx = {n: sb("cx_" + n, [P, TILES, 4], st=st) for n in ("g", "ngc", "beta", "eg", "neg_eg", "ekd")}
            cx["gl"] = sb("cx_gl", [P, TILES, 2, 2], st=st)
            cx["S"] = sb("cx_S", [P, 2, 2, HD], st=st)
            stage(conv_and_gates, cx)
            pair = lambda c0, g: [(c0 + g * HD, HD), (c0 + (AG + g) * HD, HD)]
            tile = lambda c0: [(c0, P)]
            stage(delta_net, cx, [pair(QA, g) for g in range(AG)] + [tile(c) for c in (KA, QB, QB + P, KB, KB + P)])
        stage(window_attention)
        stage(key_rows, [4], 2, LAST - 1, a_key_stores)
        stage(stick_breaking, [pair(ZZ, g) for g in range(AG)] + [tile(ZZ + AH * HD + i * P) for i in range(4)])
        stage(key_rows, [4, 5], TILES, 0, b_key_stores)
        stage(output)


_INS = ["x_prompt", "x_sample", "cache_a_k", "cache_a_v", "cache_b_k", "cache_b_v", "state_c_conv", "state_c_ssm", "meta_tokens",
        "norm_pre", "norm_post", "w_in", "w_out", "sinks_a", "conv_c", "a_log_c", "dt_bias_c", "onorm_c"]
_OUTS = [("y_prompt", (1, SEQ, D)), ("y_sample", (1, NSAMP, D)),
         ("p_a_k", (1, 1, WIN, AKV, HD)), ("p_a_v", (1, 1, WIN, AKV, HD)),
         ("p_b_k", (1, 1, NMETA + SEQ, BH, HD)), ("p_b_v", (1, 1, NMETA + SEQ, BH, HD)),
         ("p_c_conv", (1, 1, 3, 768)), ("p_c_ssm", (1, 1, CHD, HD, HD)),
         ("s_a_k", (1, 1, WIN, AKV, HD)), ("s_a_v", (1, 1, WIN, AKV, HD)),
         ("s_b_k", (1, 1, NSAMP, BH, HD)), ("s_b_v", (1, 1, NSAMP, BH, HD)),
         ("s_c_conv", (1, 1, 3, 768)), ("s_c_ssm", (1, 1, CHD, HD, HD))]


def build(nc, arrays):
    io = {}
    for name, a in arrays.items():
        io[name] = nc.dram_tensor("in_" + name, a.shape, mybir.dt.from_np(a.dtype), kind="ExternalInput").ap()
    for name, shape in _OUTS:
        io[name] = nc.dram_tensor("out_" + name, shape, F32, kind="ExternalOutput").ap()
    for name, tiles in (("mix", KT), ("uT", 9), ("sz", KT)):
        io[name] = nc.dram_tensor(name + "_scratch", (tiles, P, T), F32, kind="Internal").ap()
    stream_layer(nc, io)


def kernel(**inputs):
    import concourse.bacc as bacc
    from concourse.bass_utils import run_bass_kernel_spmd as run
    arrays = {name: np.ascontiguousarray(inputs[name]) for name in _INS}
    arrays["cf"], arrays["cb"] = shape_constants()
    nc = bacc.Bacc("TRN2", target_bir_lowering=False, num_devices=1)
    build(nc, arrays)
    r = run(nc, [{"in_" + n: a for n, a in arrays.items()}], core_ids=[0])
    return tuple(r.results[0]["out_" + name] for name, _ in _OUTS)
```

```python
from contextlib import ExitStack

import numpy as np
import concourse.bass as bass
from concourse import mybir

F32 = mybir.dt.float32
BF16 = mybir.dt.bfloat16
ALU = mybir.AluOpType
ACT = mybir.ActivationFunctionType
AX = mybir.AxisListType

P = 128
D = 1024
KT = D // P
SEQ, NMETA, NSAMP, PAST, WIN = 2048, 16, 32, 256, 128
CH = 64
HD = 64
PAD = CH - NMETA
ROW0 = CH
SROW = ROW0 + SEQ
TILES = -(-(SROW + NSAMP) // P)
T = TILES * P
LAST = TILES - 1
SP0 = SROW - LAST * P
AH, AKV, BH, CHD = 8, 2, 4, 4
AG = AH // AKV
QA, KA, VA, QB, KB, VB, XC = 0, 512, 640, 768, 1024, 1280, 1536
AB, ZZ = 2304, 2312
NIN = 3336
VAW, VBW, ABW = 128, 256, 8
RV = VAW + VBW + ABW
SCALE = HD ** -0.5
NEG = -1e30
LN_EXP = "natural_log_exp_and_others"
BLOCKS = [(512 * b, min(512, T - 512 * b)) for b in range(-(-T // 512))]
NBLK = len(BLOCKS)
LEVELS = 6
C_ID, C_TRI, C_BLK, C_LO, C_HI, C_LVL = 0, 128, 256, 384, 512, 640
C_EPS = C_LVL + LEVELS * P
C_ONE = C_EPS + 1
NCF = C_EPS + 2
M_ID, M_DT, M_A0, M_A1, M_A, M_B, M_PAD = 0, 128, 256, 384, 640, 896, 1024
NCB = M_PAD + 128


def shape_constants():
    r = np.arange(P)
    same = r[:, None] // CH == r[None, :] // CH
    cf = np.zeros((P, NCF), np.float32)
    cf[:, C_ID:C_ID + P] = np.eye(P)
    cf[:, C_TRI:C_TRI + P] = same & (r[:, None] <= r[None, :])
    cf[:, C_BLK:C_BLK + P] = same
    cf[:, C_LO:C_LO + P] = (r < CH)[:, None]
    cf[:, C_HI:C_HI + P] = (r >= CH)[:, None]
    for lv in range(LEVELS):
        s = 1 << lv
        j, i = r[:, None], r[None, :]
        cf[:, C_LVL + lv * P:C_LVL + (lv + 1) * P] = (j // (2 * s) == i // (2 * s)) & (j % (2 * s) < s) & (i % (2 * s) >= s)
    cf[:, C_EPS] = 1e-6
    cf[:, C_ONE] = 1.0
    cb = np.zeros((P, NCB), np.float32)
    cb[:, M_ID:M_ID + P] = np.eye(P)
    cb[:, M_DT:M_DT + P] = np.where(same & (r[:, None] <= r[None, :]), 0, NEG)
    q, k = r[:, None], np.arange(2 * P)[None, :]
    win = np.where(q < CH, k < 3 * CH, k >= CH)
    cb[:, M_A:M_A + 2 * P] = np.where(win, 0, NEG)
    cb[:, M_A1:M_A1 + 2 * P] = np.where(win & (k >= PAD), 0, NEG)
    cb[:, M_A0:M_A0 + P] = np.where(win[:, P:] & (k[:, :P] >= PAD), 0, NEG)
    cb[:, M_B:M_B + P] = np.where(r[None, :] < r[:, None], 0, NEG)
    cb[:, M_PAD:M_PAD + P] = np.where(r[None, :] >= PAD, 0, NEG)
    return cf, cb


def stream_layer(nc, io):
    top = ExitStack()
    with top:
        top.enter_context(nc.allow_non_contiguous_dma(reason="short vectors turned onto the partitions"))
        scope = [0]

        def fresh(name):
            scope[0] += 1
            return f"{name}_{scope[0]}"

        def sb(name, shape, dt=F32, st=top):
            return st.enter_context(nc.sbuf_tensor(fresh(name), shape, dt))

        def pb(name, shape, st):
            return st.enter_context(nc.psum_tensor(fresh(name), shape, F32))

        def sem(name, st):
            return nc.alloc_semaphore(name=fresh(name))

        cf = sb("cf", [P, NCF])
        cb = sb("cb", [P, NCB], BF16)
        hT = sb("hT", [P, KT, T])
        reg = sb("reg", [P, 6, T])
        vrow = sb("vrow", [P, TILES, RV])
        wslot = sb("wslot", [P, 2, KT, P])
        mix, uT, sz = io["mix"], io["uT"], io["sz"]
        ident = cf[:, C_ID:C_ID + P]
        identb = cb[:, M_ID:M_ID + P]
        eps = cf[:, C_EPS:C_EPS + 1]
        one = cf[:, C_ONE:C_ONE + 1]
        w_in = io["w_in"][0].rearrange("(k p) n -> p k n", p=P)

        def wide(ap, n, axis=1):
            a = ap.unsqueeze(axis)
            shape = list(a.shape)
            shape[axis] = n
            return a.to_broadcast(shape)


        def norm_and_transpose():
            with ExitStack() as st:
                xin = sb("xin", [P, 3, D], st=st)
                junk = sb("junk", [P, D], st=st)
                gpre = sb("gpre", [P, KT], st=st)
                ssq, lnv, rstd = (sb(n, [P, TILES], st=st) for n in ("ssq", "lnv", "rstd"))
                wv = sb("wv", [P, KT, RV], st=st)
                tp = pb("tp", [P, 3, KT, P], st)
                acc = pb("acc", [P, 2, 512], st)
                wv_in, row_ready, row_kept = (sem(n, st) for n in ("wv_in", "row_ready", "row_kept"))
                consts_in, zeroed, masks_cast = sem("consts_in", st), sem("zeroed", st), sem("masks_cast", st)
                x_in = [sem(f"x_in{i}", st) for i in range(3)]
                sq_done, ln_done, rstd_done = (sem(n, st) for n in ("sq_done", "ln_done", "rstd_done"))
                scaled, turned, kept = (sem(n, st) for n in ("scaled", "turned", "kept"))
                xp = io["x_prompt"][0]
                tile_of = lambda n: (0, LAST)[n] if n < 2 else n - 1
                with nc.Block() as block:
                    @block.sync
                    def _(sp):
                        sp.wait_ge(zeroed, 2)
                        sp.dma_start(xin[PAD:CH, 0, :], io["meta_tokens"]).then_inc(x_in[0], 16)
                        sp.dma_start(xin[CH:P, 0, :], xp[0:CH, :]).then_inc(x_in[0], 16)
                        sp.dma_start(xin[0:SP0, 1, :], xp[SEQ - SP0:SEQ, :]).then_inc(x_in[1], 16)
                        sp.dma_start(xin[SP0:SP0 + NSAMP, 1, :], io["x_sample"][0]).then_inc(x_in[1], 16)
                        sp.dma_start(xin[:, 2, :], xp[CH:CH + P, :]).then_inc(x_in[2], 32)
                        sp.dma_start(cf[:, :], io["cf"]).then_inc(consts_in, 16)
                        sp.dma_start(gpre[:, :], io["norm_pre"][0].rearrange("(k p) -> p k", p=P)).then_inc(consts_in, 16)
                        sp.dma_start(reg[:, 0, 0:NCB], io["cb"]).then_inc(consts_in, 16)
                        sp.dma_start(wv[:, :, 0:VAW], w_in[:, :, VA:VA + VAW]).then_inc(wv_in, 16)
                        sp.dma_start(wv[:, :, VAW:VAW + VBW], w_in[:, :, VB:VB + VBW]).then_inc(wv_in, 16)
                        sp.dma_start(wv[:, :, VAW + VBW:RV], w_in[:, :, AB:AB + ABW]).then_inc(wv_in, 16)
                        for n in range(3, 5):
                            sp.wait_ge(turned, n - 2)
                            sp.dma_start(xin[:, n % 3, :], xp[CH + P * (n - 2):CH + P * (n - 1), :]).then_inc(x_in[n % 3], 32)
                        with sp.Fori(0, (TILES - 5) // 3) as i:
                            for u in range(3):
                                sp.wait_ge(turned, 3 * i + (u + 3))
                                sp.dma_start(xin[:, (u + 2) % 3, :],
                                             xp[bass.ds(i * (3 * P) + (CH + P * (u + 3)), P), :]).then_inc(x_in[(u + 2) % 3], 32)

                    @block.gpsimd
                    def _(pool):
                        pool.memset(xin[0:CH, 0, :], 0.0).then_inc(zeroed, 1)
                        pool.memset(xin[SP0 + NSAMP:P, 1, :], 0.0).then_inc(zeroed, 1)

                    @block.scalar
                    def _(act):
                        def step(n, slot, col, landed):
                            act.wait_ge(x_in[slot], landed)
                            act.activation(junk[:, :], xin[:, slot, :], ACT.Square, accum_out=ssq[:, col]).then_inc(sq_done, 1)
                            act.wait_ge(sq_done, n + 1)
                            act.activation(lnv[:, col], ssq[:, col], ACT.Ln, bias=eps, scale=1.0 / D).then_inc(ln_done, 1)
                            act.wait_ge(ln_done, n + 1)
                            act.activation(rstd[:, col], lnv[:, col], ACT.Exp, scale=-0.5).then_inc(rstd_done, 1)

                        act.preload_act_table_set(LN_EXP)
                        act.wait_ge(consts_in, 48)
                        step(0, 0, slice(0, 1), 32)
                        step(1, 1, slice(LAST, TILES), 32)
                        with act.Fori(0, (TILES - 2) // 3) as i:
                            for u in range(3):
                                s = (u + 2) % 3
                                step(3 * i + (u + 2), s, bass.ds(3 * i + (u + 1), 1), 32 * i + (32 if s == 2 else 64))

                    @block.vector
                    def _(dve):
                        def scale(n, slot, col):
                            dve.wait_ge(rstd_done, n + 1)
                            dve.tensor_scalar(xin[:, slot, :], xin[:, slot, :], rstd[:, col], None, ALU.mult).then_inc(scaled, 1)

                        def keep(n, slot, cols):
                            dve.wait_ge(turned, n + 1)
                            for k in (0, KT // 2):
                                dve.tensor_tensor(hT[:, k:k + KT // 2, cols], tp[:, slot, k:k + KT // 2, :],
                                                  gpre[:, k:k + KT // 2].unsqueeze(2).to_broadcast([P, KT // 2, P]),
                                                  ALU.mult).then_inc(kept, 1)

                        def keep_row(n, tile):
                            dve.wait_ge(row_ready, n + 1)
                            dve.tensor_copy(vrow[:, tile, :], acc[:, n % 2, 0:RV]).then_inc(row_kept, 1)

                        dve.wait_ge(consts_in, 48)
                        dve.tensor_copy(cb[:, :], reg[:, 0, 0:NCB]).then_inc(masks_cast, 1)
                        scale(0, 0, slice(0, 1))
                        for n in range(TILES):
                            if n + 1 < TILES:
                                scale(n + 1, (n + 1) % 3, slice(tile_of(n + 1), tile_of(n + 1) + 1))
                            keep(n, n % 3, slice(P * tile_of(n), P * tile_of(n) + P))
                            if n:
                                keep_row(n - 1, tile_of(n - 1))
                        keep_row(TILES - 1, tile_of(TILES - 1))

                    @block.tensor
                    def _(pe):
                        def turn(n):
                            pe.wait_ge(scaled, n + 1)
                            if n >= 3:
                                pe.wait_ge(kept, 2 * (n - 2))
                            for k in range(KT):
                                last = pe.transpose(tp[:, n % 3, k, :], xin[:, n % 3, k * P:(k + 1) * P], ident)
                            last.then_inc(turned, 1)

                        def row(n):
                            m = tile_of(n)
                            pe.wait_ge(kept, 2 * (n + 1))
                            if n >= 2:
                                pe.wait_ge(row_kept, n - 1)
                            for k in range(KT):
                                last = pe.matmul(acc[:, n % 2, 0:RV], hT[:, k, m * P:(m + 1) * P], wv[:, k, :],
                                                 start=(k == 0), stop=(k == KT - 1))
                            last.then_inc(row_ready, 1)

                        pe.wait_ge(consts_in, 48)
                        turn(0)
                        for n in range(TILES):
                            if n + 1 < TILES:
                                turn(n + 1)
                            if n == 0:
                                pe.wait_ge(wv_in, 48)
                            row(n)

        class SideProjection:

            def __init__(self, st, kind, tiles, scratch):
                self.kind, self.tiles, self.scratch = kind, tiles, scratch
                self.units = NBLK * len(tiles)
                self.pieces = KT * self.units
                self.stage = sb("side_stage", [P, 2, 512], st=st)
                self.acc = pb("side_acc", [P, 2, 512], st)
                self.w_in_slot = [sem(f"side_w_in{i}", st) for i in range(2)]
                self.acc_ready, self.sig_ready, self.staged = (sem(n, st) for n in ("side_acc_ready", "side_sig_ready", "side_staged"))
                self.stored = [sem(f"side_stored{i}", st) for i in range(2)]

            def products(self, pe, first, count):
                for p in range(first, min(first + count, self.pieces)):
                    n, k = divmod(p, KT)
                    t, b = divmod(n, NBLK)
                    c0, width = BLOCKS[b]
                    if k == 0:
                        if b == 0:
                            pe.wait_ge(self.w_in_slot[t % 2], 32 * (t // 2 + 1))
                        if n >= 2:
                            pe.wait_ge(self.staged, n - 1)
                    last = pe.matmul(self.acc[:, n % 2, 0:width], wslot[:, t % 2, k, :], hT[:, k, c0:c0 + width],
                                     start=(k == 0), stop=(k == KT - 1))
                    if k == KT - 1:
                        last.then_inc(self.acc_ready, 1)

            def keep(self, act, n):
                width = BLOCKS[n % NBLK][1]
                act.wait_ge(self.acc_ready, n + 1)
                if n >= 2:
                    act.wait_ge(self.stored[n % 2], 16 * (n // 2))
                if self.kind == "copy":
                    act.activation(self.stage[:, n % 2, 0:width], self.acc[:, n % 2, 0:width], ACT.Copy).then_inc(self.staged, 1)
                else:
                    act.activation(self.stage[:, n % 2, 0:width], self.acc[:, n % 2, 0:width], ACT.Sigmoid).then_inc(self.sig_ready, 1)

            def gate(self, dve, n):
                width = BLOCKS[n % NBLK][1]
                dve.wait_ge(self.sig_ready, n + 1)
                dve.tensor_tensor(self.stage[:, n % 2, 0:width], self.acc[:, n % 2, 0:width], self.stage[:, n % 2, 0:width],
                                  ALU.mult).then_inc(self.staged, 1)

            def transfers(self, sp):
                def load(t):
                    at, segs = 0, self.tiles[t]
                    if t >= 2:
                        sp.wait_ge(self.acc_ready, NBLK * (t - 1))
                    for c0, width in segs:
                        sp.dma_start(wslot[:, t % 2, :, at:at + width], w_in[:, :, c0:c0 + width]).then_inc(self.w_in_slot[t % 2], 32 // len(segs))
                        at += width

                load(0)
                load(1)
                for n in range(self.units):
                    t, b = divmod(n, NBLK)
                    c0, width = BLOCKS[b]
                    sp.wait_ge(self.staged, n + 1)
                    sp.dma_start(self.scratch[t][:, c0:c0 + width], self.stage[:, n % 2, 0:width]).then_inc(self.stored[n % 2], 16)
                    if b == NBLK - 1 and t + 2 < len(self.tiles):
                        load(t + 2)
                for i in range(2):
                    sp.wait_ge(self.stored[i], 16 * ((self.units + 1 - i) // 2))

        def conv_and_gates(cx):
            NC = 6
            with ExitStack() as st:
                y = sb("y", [P, 2, T], st=st)
                sq = sb("sq", [P, NBLK, 512], st=st)
                rn = sb("rn", [P, NBLK, 512], st=st)
                taps = sb("taps", [P, NC, 4], st=st)
                hist = sb("hist", [P, NC, 3 + NSAMP], st=st)
                tails = sb("tails", [P, NC, 2, 3], st=st)
                heads4 = sb("heads4", [P, 2, 4], st=st)
                ga = sb("ga", [P, 4, TILES, 4], st=st)
                ea = sb("ea", [P, 4], st=st)
                acc = pb("acc", [P, NBLK, 512], st)
                ss = pb("ss", [P, 2, 512], st)
                W4 = 4 * TILES
                gsum = pb("gsum", [P, 4, P], st)
                names = ("small_in copied tap sample_tap scaled conv_done sig_done silu_done gate_v gate_s sums out_done s0_in "
                         "acc_ready raw_kept sq_done ss_ready ln_done rn_done normed tail_kept").split()
                (small_in, copied, tap, sample_tap, scaled, conv_done, sig_done, silu_done, gate_v, gate_s, sums, out_done, s0_in,
                 acc_ready, raw_kept, sq_done, ss_ready, ln_done, rn_done, normed, tail_kept) = (sem(n, st) for n in names)
                w_in_slot = [sem(f"w_in_slot{i}", st) for i in range(2)]
                flat = lambda ap: ap.rearrange("p t h -> p (t h)")
                with nc.Block() as block:
                    @block.sync
                    def _(sp):
                        def load(c):
                            if c >= 2:
                                sp.wait_ge(acc_ready, NBLK * (c - 1))
                            sp.dma_start(wslot[:, c % 2], w_in[:, :, XC + c * P:XC + (c + 1) * P]).then_inc(w_in_slot[c % 2], 16)

                        load(0)
                        load(1)
                        for w in range(4):
                            sp.dma_start(taps[:, :, w], io["conv_c"][0, w].rearrange("(t p) -> p t", p=P)).then_inc(small_in, 16)
                        for w in range(3):
                            sp.dma_start(hist[:, :, w], io["state_c_conv"][0, 0, w].rearrange("(t p) -> p t", p=P)).then_inc(small_in, 16)
                        sp.dma_start(heads4[:, 0, :], io["dt_bias_c"].to_broadcast([P, 4])).then_inc(small_in, 16)
                        sp.dma_start(heads4[:, 1, :], io["a_log_c"].to_broadcast([P, 4])).then_inc(small_in, 16)
                        for par in range(2):
                            sp.dma_start(cx["S"][par * CH:par * CH + CH, 1],
                                         io["state_c_ssm"][0, 0].rearrange("(a b) k v -> b k a v", b=2)[par]).then_inc(s0_in, 16)
                        for c in range(2, NC):
                            load(c)
                        rows = lambda name: io[name][0, 0].rearrange("t h d -> t (h d)")
                        b0 = slice(VAW, VAW + VBW)
                        stores = [(rows("p_b_v")[0:NMETA, :], vrow[PAD:CH, 0, b0]),
                                  (rows("p_b_v")[NMETA:NMETA + CH, :], vrow[CH:P, 0, b0]),
                                  (rows("p_b_v")[NMETA + CH:NMETA + SEQ - SP0, :].rearrange("(t p) n -> p t n", p=P), vrow[:, 1:LAST, b0]),
                                  (rows("p_b_v")[NMETA + SEQ - SP0:NMETA + SEQ, :], vrow[0:SP0, LAST, b0]),
                                  (rows("s_b_v"), vrow[SP0:SP0 + NSAMP, LAST, b0]),
                                  (rows("p_a_v")[0:WIN - SP0, :], vrow[SP0:P, LAST - 1, 0:VAW]),
                                  (rows("p_a_v")[WIN - SP0:WIN, :], vrow[0:SP0, LAST, 0:VAW]),
                                  (rows("s_a_v")[WIN - NSAMP:WIN, :], vrow[SP0:SP0 + NSAMP, LAST, 0:VAW]),
                                  (rows("s_a_v")[0:WIN - NSAMP, :], rows("cache_a_v")[NSAMP:WIN, :]),
                                  (rows("s_a_k")[0:WIN - NSAMP, :], rows("cache_a_k")[NSAMP:WIN, :])]
                        for dst, src in stores:
                            sp.dma_start(dst, src).then_inc(out_done, 16)
                        sp.wait_ge(tail_kept, 2 * NC)
                        for a, name in enumerate(("p_c_conv", "s_c_conv")):
                            for w in range(3):
                                sp.dma_start(io[name][0, 0, w].rearrange("(t p) -> p t", p=P), tails[:, :, a, w]).then_inc(out_done, 16)
                        sp.wait_ge(out_done, 16 * (len(stores) + 6))
                        sp.wait_ge(s0_in, 32)

                    @block.tensor
                    def _(pe):
                        for c in range(NC):
                            pe.wait_ge(w_in_slot[c % 2], 16 * (c // 2 + 1))
                            for b, (c0, w) in enumerate(BLOCKS):
                                if c:
                                    pe.wait_ge(raw_kept, NBLK * (c - 1) + b + 1)
                                for k in range(KT):
                                    last = pe.matmul(acc[:, b, 0:w], wslot[:, c % 2, k, :], hT[:, k, c0:c0 + w],
                                                     start=(k == 0), stop=(k == KT - 1))
                                last.then_inc(acc_ready, 1)
                                if c >= 2:
                                    n = NBLK * (c - 2) + b
                                    pe.wait_ge(sq_done, n + 1)
                                    if n >= 2:
                                        pe.wait_ge(ln_done, n - 1)
                                    pe.matmul(ss[:, n % 2, 0:w], cf[:, C_BLK:C_BLK + P], sq[:, b, 0:w], start=True, stop=True).then_inc(ss_ready, 1)
                            if c == 0:
                                pe.wait_ge(gate_v, 8)
                                for n, c_ in enumerate((C_TRI, C_BLK, C_LO, C_HI)):
                                    last = pe.matmul(gsum[:, n, 0:W4], cf[:, c_:c_ + P], flat(cx["g"]), start=True, stop=True)
                                last.then_inc(sums, 1)

                    @block.scalar
                    def _(act):
                        act.preload_act_table_set(LN_EXP)
                        act.wait_ge(small_in, 144)
                        x, t, u, g = (ga[:, n] for n in range(4))
                        act.activation(ea[:, :], heads4[:, 1, :], ACT.Exp).then_inc(gate_s, 1)
                        act.activation(cx["beta"][:, :, :], vrow[:, :, VAW + VBW + 4:RV], ACT.Exp, scale=-1.0).then_inc(gate_s, 1)
                        act.wait_ge(gate_v, 2)
                        act.activation(t, t, ACT.Exp, scale=-1.0).then_inc(gate_s, 1)
                        act.wait_ge(gate_s, 3)
                        act.activation(t, t, ACT.Ln, bias=one).then_inc(gate_s, 1)

                        def gate_sums():
                            act.wait_ge(gate_v, 10)
                            act.activation(flat(cx["eg"]), gsum[:, 0, 0:W4], ACT.Exp).then_inc(gate_s, 1)
                            act.activation(flat(cx["ekd"]), flat(t), ACT.Exp).then_inc(gate_s, 1)
                            for c in range(2):
                                for par in range(2):
                                    half = slice(par * CH, par * CH + CH)
                                    act.activation(cx["gl"][half, :, c, :],
                                                   gsum[half, 2 + c, 0:W4].rearrange("p (t a b) -> p t a b", a=2, b=2)[:, :, :, par],
                                                   ACT.Exp).then_inc(gate_s, 1)

                        def last_tap(c):
                            act.wait_ge(raw_kept, NBLK * (c + 1))
                            if c >= 2:
                                act.wait_ge(silu_done, c - 1)
                            act.activation(y[:, c % 2, :], reg[:, c, :], ACT.Copy, scale=taps[:, c, 3:4]).then_inc(scaled, 1)

                        def sigmoid(c):
                            act.wait_ge(conv_done, c + 1)
                            act.activation(reg[:, c, :], y[:, c % 2, :], ACT.Sigmoid).then_inc(sig_done, 1)

                        for c in range(NC):
                            for b, (c0, w) in enumerate(BLOCKS):
                                act.wait_ge(acc_ready, NBLK * c + b + 1)
                                act.activation(reg[:, c, c0:c0 + w], acc[:, b, 0:w], ACT.Copy).then_inc(raw_kept, 1)
                                if c and b == 0:
                                    sigmoid(c - 1)
                                if c >= 2:
                                    n = NBLK * (c - 2) + b
                                    act.wait_ge(ss_ready, n + 1)
                                    if n >= NBLK:
                                        act.wait_ge(normed, n - NBLK + 1)
                                    act.activation(rn[:, b, 0:w], ss[:, n % 2, 0:w], ACT.Ln, bias=eps).then_inc(ln_done, 1)
                            last_tap(c)
                            if c == 0:
                                gate_sums()
                            if c >= 2:
                                for b, (c0, w) in enumerate(BLOCKS):
                                    act.wait_ge(ln_done, NBLK * (c - 2) + b + 1)
                                    act.activation(rn[:, b, 0:w], rn[:, b, 0:w], ACT.Exp, scale=-0.5).then_inc(rn_done, 1)
                        sigmoid(NC - 1)

                    @block.gpsimd
                    def _(pool):
                        for c in range(NC):
                            pool.wait_ge(sig_done, c + 1)
                            pool.tensor_tensor(reg[:, c, :], reg[:, c, :], y[:, c % 2, :], ALU.mult).then_inc(silu_done, 1)
                            if c < 4:
                                pool.wait_ge(silu_done, c + 1)
                                for b, (c0, w) in enumerate(BLOCKS):
                                    if c:
                                        pool.wait_ge(ss_ready, NBLK * (c - 1) + b + 1)
                                    r = reg[:, c, c0:c0 + w]
                                    pool.tensor_tensor(sq[:, b, 0:w], r, r, ALU.mult).then_inc(sq_done, 1)

                    @block.vector
                    def _(dve):
                        dve.memset(cx["S"][:, 0], 0.0).then_inc(copied, 1)
                        dve.wait_ge(small_in, 144)
                        x, t, u, g = (ga[:, n] for n in range(4))
                        dve.tensor_tensor(x, vrow[:, :, VAW + VBW:VAW + VBW + 4], wide(heads4[:, 0, :], TILES), ALU.add).then_inc(gate_v, 1)
                        dve.wait_ge(gate_v, 1)
                        dve.scalar_tensor_tensor(out=t, in0=x, scalar=-1.0, in1=x, op0=ALU.mult, op1=ALU.max).then_inc(gate_v, 1)
                        dve.wait_ge(gate_s, 4)
                        dve.scalar_tensor_tensor(out=u, in0=x, scalar=0.0, in1=t, op0=ALU.max, op1=ALU.add).then_inc(gate_v, 1)
                        dve.wait_ge(gate_v, 3)
                        dve.scalar_tensor_tensor(out=g, in0=u, scalar=-1.0, in1=wide(ea[:, :], TILES),
                                                 op0=ALU.mult, op1=ALU.mult).then_inc(gate_v, 1)
                        dve.tensor_scalar(cx["beta"][:, :, :], cx["beta"][:, :, :], 1.0, None, ALU.add).then_inc(gate_v, 1)
                        dve.wait_ge(gate_v, 5)
                        dve.reciprocal(cx["beta"][:, :, :], cx["beta"][:, :, :]).then_inc(gate_v, 1)
                        dve.memset(g[SP0 + NSAMP:P, LAST, :], 0.0).then_inc(gate_v, 1)
                        dve.wait_ge(gate_v, 7)
                        dve.tensor_copy(cx["g"][:, :, :], g).then_inc(gate_v, 1)
                        dve.wait_ge(sums, 1)
                        dve.tensor_scalar(flat(cx["ngc"]), gsum[:, 0, 0:W4], -1.0, None, ALU.mult).then_inc(gate_v, 1)
                        dve.wait_ge(gate_v, 9)
                        dve.tensor_tensor(flat(t), gsum[:, 1, 0:W4], flat(cx["ngc"]), ALU.add).then_inc(gate_v, 1)
                        dve.wait_ge(gate_s, 6)
                        dve.tensor_scalar(flat(cx["neg_eg"]), flat(cx["eg"]), -1.0, None, ALU.mult).then_inc(gate_v, 1)

                        def conv(c):
                            yc = y[:, c % 2, :]
                            dve.wait_ge(raw_kept, NBLK * (c + 1))
                            for a, c0 in enumerate((SROW - 3, SROW + NSAMP - 3)):
                                dve.tensor_copy(tails[:, c, a, :], reg[:, c, c0:c0 + 3]).then_inc(tail_kept, 1)
                            dve.tensor_copy(hist[:, c, 3:3 + NSAMP], reg[:, c, SROW:SROW + NSAMP]).then_inc(copied, 1)
                            dve.wait_ge(scaled, c + 1)
                            for w in range(3):
                                if w:
                                    dve.wait_ge(tap, 3 * c + w)
                                dve.scalar_tensor_tensor(out=yc[:, 3:T], in0=reg[:, c, w:T - 3 + w], scalar=taps[:, c, w:w + 1],
                                                         in1=yc[:, 3:T], op0=ALU.mult, op1=ALU.add).then_inc(tap, 1)
                            dve.wait_ge(tap, 3 * c + 3)
                            dve.wait_ge(copied, c + 2)
                            ys = yc[:, SROW:SROW + NSAMP]
                            dve.tensor_scalar(ys, hist[:, c, 3:3 + NSAMP], taps[:, c, 3:4], None, ALU.mult).then_inc(sample_tap, 1)
                            for w in range(3):
                                dve.wait_ge(sample_tap, 4 * c + w + 1)
                                dve.scalar_tensor_tensor(out=ys, in0=hist[:, c, w:w + NSAMP], scalar=taps[:, c, w:w + 1],
                                                         in1=ys, op0=ALU.mult, op1=ALU.add).then_inc(sample_tap, 1)
                            dve.wait_ge(sample_tap, 4 * c + 4)
                            dve.memset(yc[:, SROW + NSAMP:T], 0.0).then_inc(conv_done, 1)

                        def norm(c):
                            for b, (c0, w) in enumerate(BLOCKS):
                                n = NBLK * c + b
                                dve.wait_ge(rn_done, n + 1)
                                r = reg[:, c, c0:c0 + w]
                                dve.scalar_tensor_tensor(out=r, in0=r, scalar=SCALE if c < 2 else 1.0, in1=rn[:, b, 0:w],
                                                         op0=ALU.mult, op1=ALU.mult).then_inc(normed, 1)

                        for c in range(NC):
                            conv(c)
                            if c >= 2:
                                norm(c - 2)

        def delta_net(cx, side_tiles):
            with ExitStack() as st:
                tg = sb("tg", [P, 4, P], st=st)
                dec = sb("dec", [P, 4, P], st=st)
                at = sb("at", [P, 4, P], st=st)
                atl = sb("atl", [P, LEVELS, 4, P], st=st)
                qk = sb("qk", [P, 2, 4, P], st=st)
                xm = sb("xm", [P, 4, P], st=st)
                xt = sb("xt", [P, 2, 4, P], st=st)
                ym = sb("ym", [P, 4, P], st=st)
                kd = sb("kd", [P, 2, 4, HD], st=st)
                vr = sb("vr", [P, 2, 4, HD], st=st)
                rr = sb("rr", [P, 4, HD], st=st)
                vn = sb("vn", [P, 4, HD], st=st)
                oo = sb("oo", [P, 4, HD], st=st)
                osq = sb("osq", [P, 4, HD], st=st)
                oss, oln, ors = (sb(n, [P, 4], st=st) for n in ("oss", "oln", "ors"))
                onorm = sb("onorm", [P, HD], st=st)
                b_dr = pb("b_dr", [P, 4, P], st)
                b_kq = pb("b_kq", [P, 2, 2, 2, P], st)
                b_lv = b_kq[:, 0].rearrange("p a q i -> p (a q) i")
                b_lt = b_kq[:, 1].rearrange("p a q i -> p (a q) i")
                b_s = pb("b_s", [P, 2, 512], st)
                b_ds = b_s[:, 0, 4 * HD:6 * HD]
                b_ot = b_s[:, 1, 4 * HD:8 * HD]
                b_vn = pb("b_vn", [P, 2, 4, HD], st)
                side = SideProjection(st, "copy", side_tiles, uT)
                names = ("tg_ready dec_ready dec_done rows_ready v_kept rows_kept kq_ready at_ready qk_ready kd_ready level "
                         "xt0_ready x_turned x_kept y_ready y_kept z_ready x_new ks_ready r_ready vn_ready vn_kept "
                         "ds_ready state_ready o_ready o_sum o_squared o_rss o_ln o_rstd o_scaled o_normed ot_ready ot_kept "
                         "onorm_in out_done o_part").split()
                (tg_ready, dec_ready, dec_done, rows_ready, v_kept, rows_kept, kq_ready, at_ready, qk_ready, kd_ready, level,
                 xt0_ready, x_turned, x_kept, y_ready, y_kept, z_ready, x_new, ks_ready, r_ready, vn_ready, vn_kept,
                 ds_ready, state_ready, o_ready, o_sum, o_squared, o_rss, o_ln, o_rstd, o_scaled, o_normed, ot_ready, ot_kept,
                 onorm_in, out_done, o_part) = (sem(n, st) for n in names)
                lvl = lambda l: cf[:, C_LVL + l * P:C_LVL + (l + 1) * P]
                cols = lambda m: slice(m * P, (m + 1) * P)
                NL = LEVELS - 1
                
                S = cx["S"]
                POINTS = [3, 1, 1, 1] + [2, 1, 1] * 4 + [1]
                FIRST = [[m * sum(POINTS) + sum(POINTS[:p]) for p in range(len(POINTS))] for m in range(TILES)]
                assert TILES * sum(POINTS) >= side.pieces

                def state(c):
                    return S[:, 1] if c == 2 * TILES - 1 else S[:, 0]

                with nc.Block() as block:
                    @block.sync
                    def _(sp):
                        side.transfers(sp)

                    @block.gpsimd
                    def _(pool):
                        def triangle_gates(m):
                            if m:
                                pool.wait_ge(dec_ready, m)
                            pool.tensor_tensor(tg[:, :, :], wide(cf[:, C_TRI:C_TRI + P], 4),
                                               cx["g"][:, m, :].unsqueeze(2).to_broadcast([P, 4, P]), ALU.mult).then_inc(tg_ready, 1)

                        pool.dma_start(onorm[:, :], io["onorm_c"].to_broadcast([P, HD])).then_inc(onorm_in, 16)
                        triangle_gates(0)
                        for m in range(TILES + 1):
                            if m < TILES:
                                pool.wait_ge(at_ready, 4 * m + 4)
                                for l in range(LEVELS):
                                    if m and l:
                                        pool.wait_ge(y_ready, NL * (m - 1) + l)
                                    elif m:
                                        pool.wait_ge(xt0_ready, m)
                                    pool.tensor_tensor(atl[:, l], at[:, :, :], wide(lvl(l), 4), ALU.mult).then_inc(level, 1)
                                if m + 1 < TILES:
                                    triangle_gates(m + 1)
                            if m:
                                pool.wait_ge(o_rstd, m)
                                pool.tensor_tensor(osq[:, :, :], oo[:, :, :], ors[:, :].unsqueeze(2).to_broadcast([P, 4, HD]),
                                                   ALU.mult).then_inc(o_scaled, 1)
                                if m == 1:
                                    pool.wait_ge(onorm_in, 16)
                                else:
                                    pool.wait_ge(ot_ready, m - 1)
                                pool.wait_ge(o_scaled, m)
                                pool.tensor_tensor(oo[:, :, :], osq[:, :, :], wide(onorm[:, :], 4), ALU.mult).then_inc(o_normed, 1)
                        for a, name in enumerate(("p_c_ssm", "s_c_ssm")):
                            pool.wait_ge(state_ready, 2 * (2 * TILES - 1) + 2 * a)
                            for par in range(2):
                                pool.dma_start(io[name][0, 0].rearrange("(a b) k v -> b k a v", b=2)[par],
                                               S[par * CH:par * CH + CH, a]).then_inc(out_done, 16)
                        pool.wait_ge(out_done, 64)

                    @block.tensor
                    def _(pe):
                        def decay(m):
                            pe.wait_ge(tg_ready, m + 1)
                            if m:
                                pe.wait_ge(rows_kept, m)
                            pe.matmul(b_dr[:, :, :], identb, wide(cb[:, M_DT:M_DT + P], 4), start=True, stop=False)
                            pe.matmul(b_dr[:, :, :], cf[:, C_BLK:C_BLK + P], tg[:, :, :], start=False, stop=True).then_inc(dec_ready, 1)

                        def rows(m):
                            pe.wait_ge(dec_done, 4 * m + 4)
                            for a in range(4):
                                last = pe.transpose(b_dr[:, a, :], reg[:, 2 + a, cols(m)], ident)
                            last.then_inc(rows_ready, 1)

                        def kq(m):
                            if m:
                                pe.wait_ge(x_new, NL * m)
                            for h in range(4):
                                half = slice((h % 2) * CH, (h % 2) * CH + CH)
                                last = pe.matmul(b_kq[:, h % 2, h // 2], reg[half, 2 + h // 2, cols(m)],
                                                 reg[half, h // 2:h // 2 + 3:2, cols(m)], start=True, stop=True)
                            last.then_inc(kq_ready, 1)

                        def turn_x(m, l):
                            if l == 1:
                                pe.wait_ge(xt0_ready, m + 1)
                                pe.wait_ge(at_ready, 4 * m + 4)
                                pe.wait_ge(qk_ready, 2 * m + 2)
                            else:
                                pe.wait_ge(x_new, NL * m + l - 1)
                            for h in range(4):
                                last = pe.transpose(b_lv[:, h, :], xt[:, m % 2, h], ident)
                            last.then_inc(x_turned, 1)

                        def level_y(m, l):
                            pe.wait_ge(x_kept, NL * m + l)
                            pe.wait_ge(level, LEVELS * m + l + 1)
                            for h in range(4):
                                last = pe.matmul(b_lv[:, h, :], atl[:, l, h], xm[:, h], start=True, stop=True)
                            last.then_inc(y_ready, 1)

                        def level_z(m, l):
                            pe.wait_ge(y_kept, NL * m + l)
                            for h in range(4):
                                last = pe.matmul(b_lt[:, h, :], ym[:, h], xt[:, m % 2, h], start=True, stop=True)
                            last.then_inc(z_ready, 1)

                        def read_state(c):
                            m, at0 = c // 2, (c % 2) * CH
                            if c:
                                pe.wait_ge(state_ready, 2 * c)
                            if c >= 2 and c % 2 == 0:
                                pe.wait_ge(o_part, 2 * m)
                                pe.wait_ge(ot_kept, m)
                            tok = slice(m * P + at0, m * P + at0 + CH)
                            for h in range(4):
                                half = slice((h % 2) * CH, (h % 2) * CH + CH)
                                for a in range(2):
                                    o = a * 2 * HD + (h // 2) * HD
                                    last = pe.matmul(b_s[at0:at0 + CH, h % 2, o:o + HD], reg[half, 2 * a + h // 2, tok],
                                                     state(c)[half, h // 2], start=True, stop=True)
                            last.then_inc(ks_ready, 1)

                        def new_values(c):
                            m, at0 = c // 2, (c % 2) * CH
                            pe.wait_ge(r_ready, 4 * c + 4)
                            if c:
                                pe.wait_ge(vn_kept, c)
                            if m and c == 2 * m:
                                pe.wait_ge(o_sum, m)
                            half = slice(at0, at0 + CH)
                            for h in range(4):
                                last = pe.matmul(b_vn[half, 0, h], xt[half, m % 2, h, half], rr[half, h], start=True, stop=True)
                            last.then_inc(vn_ready, 1)

                        def update_state(c):
                            m, at0 = c // 2, (c % 2) * CH
                            half = slice(at0, at0 + CH)
                            pe.wait_ge(vn_kept, c + 1)
                            for h in range(4):
                                o = (h // 2) * HD
                                last = pe.matmul(b_ds[(h % 2) * CH:(h % 2) * CH + CH, o:o + HD], kd[half, m % 2, h], vn[half, h],
                                                 start=True, stop=True)
                            last.then_inc(ds_ready, 1)

                        def outputs(m):
                            pe.wait_ge(vn_kept, 2 * m + 2)
                            for h in range(4):
                                last = pe.matmul(b_vn[:, 1, h], qk[:, m % 2, h], vn[:, h], start=True, stop=True)
                            last.then_inc(o_ready, 1)

                        def outputs_transposed(m):
                            pe.wait_ge(o_normed, m + 1)
                            for a in range(2):
                                last = pe.transpose(b_ot[:, a * P:(a + 1) * P],
                                                    oo[:, 2 * a:2 * a + 2, :].rearrange("p h v -> p (h v)"), ident)
                            last.then_inc(ot_ready, 1)

                        def beside(m, point):
                            side.products(pe, FIRST[m][point], POINTS[point])

                        for m in range(TILES + 1):
                            new, old = m < TILES, m > 0
                            c = 2 * (m - 1)

                            def invert(l, after_turn=None, after_y=None, after_z=None):
                                if new:
                                    beside(m, 3 * l - 2)
                                    turn_x(m, l)
                                if old and after_turn:
                                    after_turn()
                                if new:
                                    beside(m, 3 * l - 1)
                                    level_y(m, l)
                                    beside(m, 3 * l)
                                if old and after_y:
                                    after_y()
                                if new:
                                    level_z(m, l)
                                if old and after_z:
                                    after_z()

                            if new:
                                decay(m)
                                kq(m)
                                beside(m, 0)
                                rows(m)
                            if old:
                                read_state(c)
                            invert(1, lambda: new_values(c), lambda: update_state(c), lambda: read_state(c + 1))
                            invert(2, None, lambda: new_values(c + 1), lambda: update_state(c + 1))
                            invert(3, None, lambda: outputs(m - 1))
                            invert(4, None, None, lambda: outputs_transposed(m - 1))
                            invert(5)
                            if new:
                                beside(m, 16)

                    @block.scalar
                    def _(act):
                        def keep_y(m, l):
                            keep_beside(m, (3 * l - 2,))
                            act.wait_ge(x_turned, NL * m + l)
                            act.activation(xm[:, :, :], b_lv, ACT.Copy).then_inc(x_kept, 1)
                            keep_beside(m, (3 * l - 1,))
                            act.wait_ge(y_ready, NL * m + l)
                            act.activation(ym[:, :, :], b_lv[:, :, :], ACT.Copy).then_inc(y_kept, 1)
                            keep_beside(m, (3 * l,))

                        def keep_beside(m, points):
                            for p in points:
                                for n in range(FIRST[m][p] // KT, min((FIRST[m][p] + POINTS[p]) // KT, side.units)):
                                    side.keep(act, n)

                        act.preload_act_table_set(LN_EXP)
                        for m in range(TILES + 1):
                            if m < TILES:
                                act.wait_ge(dec_ready, m + 1)
                                if m:
                                    act.wait_ge(at_ready, 4 * m)
                                    act.wait_ge(qk_ready, 2 * m)
                                for h in range(4):
                                    act.activation(dec[:, h, :], b_dr[:, h, :], ACT.Exp, bias=cx["ngc"][:, m, h:h + 1]).then_inc(dec_done, 1)
                                act.wait_ge(rows_ready, m + 1)
                                if m >= 2:
                                    act.wait_ge(r_ready, 8 * (m - 1))
                                act.activation(vr[:, m % 2], b_dr[:, 2:4, :].rearrange("p a (b v) -> p (a b) v", b=2), ACT.Copy).then_inc(v_kept, 1)
                                keep_beside(m, (0,))
                                for l in range(1, 5):
                                    keep_y(m, l)
                            if m:
                                act.wait_ge(o_rss, m)
                                act.activation(oln[:, :], oss[:, :], ACT.Ln, bias=eps, scale=1.0 / HD).then_inc(o_ln, 1)
                                act.wait_ge(o_ln, m)
                                act.activation(ors[:, :], oln[:, :], ACT.Exp, scale=-0.5).then_inc(o_rstd, 1)
                            if m < TILES:
                                keep_y(m, 5)
                            if m:
                                act.wait_ge(ot_ready, m)
                                act.activation(reg[:, 0:2, cols(m - 1)], b_ot.rearrange("p (a t) -> p a t", a=2),
                                               ACT.Copy).then_inc(ot_kept, 1)
                            if m < TILES:
                                keep_beside(m, (16,))

                    @block.vector
                    def _(dve):
                        def products(m):
                            dve.wait_ge(kq_ready, m + 1)
                            dve.wait_ge(dec_done, 4 * m + 4)
                            if m:
                                dve.wait_ge(level, LEVELS * m)
                            for h in range(4):
                                dve.scalar_tensor_tensor(out=at[:, h, :], in0=b_kq[:, h % 2, h // 2, 1], scalar=cx["beta"][:, m, h:h + 1],
                                                         in1=dec[:, h, :], op0=ALU.mult, op1=ALU.mult).then_inc(at_ready, 1)
                            if m >= 2:
                                dve.wait_ge(o_ready, m - 1)
                            for b in range(2):
                                dve.tensor_tensor(qk[:, m % 2, b::2, :], b_kq[:, b, :, 0, :], dec[:, b::2, :], ALU.mult).then_inc(qk_ready, 1)
                            dve.wait_ge(v_kept, m + 1)
                            if m >= 2:
                                dve.wait_ge(ds_ready, 2 * (m - 1))
                            dve.tensor_tensor(kd[:, m % 2], b_dr[:, 0:2, :].rearrange("p a (b v) -> p (a b) v", b=2),
                                              cx["ekd"][:, m, :].unsqueeze(2).to_broadcast([P, 4, HD]), ALU.mult).then_inc(rows_kept, 1)

                        def first_inverse(m):
                            dve.wait_ge(level, LEVELS * m + 1)
                            if m >= 2:
                                dve.wait_ge(vn_ready, 2 * (m - 1))
                            dve.tensor_tensor(xt[:, m % 2], wide(ident, 4), atl[:, 0], ALU.subtract).then_inc(xt0_ready, 1)

                        def level_sub(m, l):
                            dve.wait_ge(z_ready, NL * m + l)
                            dve.tensor_tensor(xt[:, m % 2], xt[:, m % 2], b_lt, ALU.subtract).then_inc(x_new, 1)

                        def residual(c):
                            m, at0 = c // 2, (c % 2) * CH
                            half = slice(at0, at0 + CH)
                            dve.wait_ge(ks_ready, c + 1)
                            dve.wait_ge(rows_kept, m + 1)
                            if c:
                                dve.wait_ge(vn_ready, c)
                            for h in range(4):
                                o = 2 * HD + (h // 2) * HD
                                dve.scalar_tensor_tensor(out=rr[half, h], in0=b_s[half, h % 2, o:o + HD], scalar=cx["neg_eg"][half, m, h:h + 1],
                                                         in1=vr[half, m % 2, h], op0=ALU.mult, op1=ALU.add).then_inc(r_ready, 1)

                        def values(c):
                            m, at0 = c // 2, (c % 2) * CH
                            half = slice(at0, at0 + CH)
                            dve.wait_ge(vn_ready, c + 1)
                            if c >= 2 and c % 2 == 0:
                                dve.wait_ge(o_ready, m)
                            dve.tensor_tensor(vn[half], b_vn[half, 0], cx["beta"][half, m, :].unsqueeze(2).to_broadcast([CH, 4, HD]),
                                              ALU.mult).then_inc(vn_kept, 1)

                        def new_state(c):
                            dve.wait_ge(ds_ready, c + 1)
                            for a in range(2):
                                s_ = state(c)[:, a]
                                dve.scalar_tensor_tensor(out=s_, in0=s_, scalar=cx["gl"][:, c // 2, c % 2, a:a + 1],
                                                         in1=b_ds[:, a * HD:(a + 1) * HD], op0=ALU.mult, op1=ALU.add).then_inc(state_ready, 1)

                        def finish(m):
                            dve.wait_ge(o_ready, m + 1)
                            if m:
                                dve.wait_ge(ot_ready, m)
                            for b in range(2):
                                dve.tensor_tensor(oo[:, b::2, :], b_s[:, b, 0:2 * HD].rearrange("p (a v) -> p a v", a=2),
                                                  cx["eg"][:, m, b::2].unsqueeze(2).to_broadcast([P, 2, HD]), ALU.mult).then_inc(o_part, 1)
                            dve.wait_ge(o_part, 2 * m + 2)
                            dve.tensor_tensor(oo[:, :, :], oo[:, :, :], b_vn[:, 1], ALU.add).then_inc(o_sum, 1)
                            dve.wait_ge(o_sum, m + 1)
                            dve.tensor_tensor(osq[:, :, :], oo[:, :, :], oo[:, :, :], ALU.mult).then_inc(o_squared, 1)
                            dve.wait_ge(o_squared, m + 1)
                            dve.tensor_reduce(oss[:, :], osq[:, :, :], AX.X, ALU.add).then_inc(o_rss, 1)

                        for m in range(TILES + 1):
                            new, old = m < TILES, m > 0
                            c = 2 * (m - 1)
                            if new:
                                products(m)
                            if old:
                                residual(c)
                            if new:
                                first_inverse(m)
                            if old:
                                values(c)
                                new_state(c)
                            if new:
                                level_sub(m, 1)
                            if old:
                                residual(c + 1)
                                values(c + 1)
                            if new:
                                level_sub(m, 2)
                            if old:
                                new_state(c + 1)
                            if new:
                                level_sub(m, 3)
                            if old:
                                finish(m - 1)
                            if new:
                                level_sub(m, 4)
                                level_sub(m, 5)

        def key_rows(dve_src, n_tiles, first_tile, outs):
            with ExitStack() as st:
                kr = sb("kr", [P, 4, len(dve_src) * P], st=st)
                bank = pb("bank", [P, 4, 512], st)
                turned, kept = sem("turned", st), sem("kept", st)
                stored = [sem(f"stored{i}", st) for i in range(4)]
                W = len(dve_src) * P
                total = [0, 0, 0, 0]
                with nc.Block() as block:
                    @block.tensor
                    def _(pe):
                        for n in range(n_tiles):
                            m = first_tile + n
                            if n >= 4:
                                pe.wait_ge(kept, n - 3)
                            for a, r in enumerate(dve_src):
                                last = pe.transpose(bank[:, n % 4, a * P:(a + 1) * P], reg[:, r, m * P:(m + 1) * P], ident)
                            last.then_inc(turned, 1)

                    def stores(n):
                        return outs(first_tile + n)

                    @block.vector
                    def _(dve):
                        done = [0, 0, 0, 0]
                        for n in range(n_tiles):
                            dve.wait_ge(turned, n + 1)
                            if n >= 4:
                                dve.wait_ge(stored[n % 4], done[n % 4])
                            dve.tensor_copy(kr[:, n % 4, :], bank[:, n % 4, 0:W]).then_inc(kept, 1)
                            done[n % 4] += 16 * len(stores(n))

                    @block.sync
                    def _(sp):
                        for n in range(n_tiles):
                            sp.wait_ge(kept, n + 1)
                            for dst, rows in stores(n):
                                sp.dma_start(dst, kr[rows, n % 4, :]).then_inc(stored[n % 4], 16)
                                total[n % 4] += 16
                        for i in range(4):
                            if total[i]:
                                sp.wait_ge(stored[i], total[i])

        def a_key_stores(m):
            pk = io["p_a_k"][0, 0].rearrange("t h d -> t (h d)")
            sk = io["s_a_k"][0, 0].rearrange("t h d -> t (h d)")
            if m == LAST - 1:
                return [(pk[0:WIN - SP0, :], slice(SP0, P))]
            return [(pk[WIN - SP0:WIN, :], slice(0, SP0)), (sk[WIN - NSAMP:WIN, :], slice(SP0, SP0 + NSAMP))]

        def b_key_stores(m):
            pk = io["p_b_k"][0, 0].rearrange("t h d -> t (h d)")
            sk = io["s_b_k"][0, 0].rearrange("t h d -> t (h d)")
            if m == 0:
                return [(pk[0:P - PAD, :], slice(PAD, P))]
            if m == LAST:
                return [(pk[m * P - PAD:m * P - PAD + SP0, :], slice(0, SP0)), (sk, slice(SP0, SP0 + NSAMP))]
            return [(pk[m * P - PAD:(m + 1) * P - PAD, :], slice(0, P))]

        def window_attention():
            with ExitStack() as st:
                kc = sb("kc", [P, P], st=st)
                vc = sb("vc", [P, P], st=st)
                kcT = sb("kcT", [P, P], st=st)
                nsink = sb("nsink", [P, AH], st=st)
                sink = sb("sink", [P, AH], st=st)
                pr = sb("pr", [P, 2, AG, 2 * P], st=st)
                pt = sb("pt", [P, 2, 2, AG, P], st=st)
                mx, nm, den, se, rd = (sb(n, [P, 2, AG], st=st) for n in ("mx", "nm", "den", "se", "rd"))
                b_sc = pb("b_sc", [P, 2, AG, 2 * P], st)
                b_pt = pb("b_pt", [P, 2, AG, P], st)
                b_o = pb("b_o", [P, 2, AG, P], st)
                names = ("cache_in sink_in turned kct_kept nsink_ready scores_ready max_ready bias_ready exp_done sink_biased sink_exp "
                         "den_ready recip_ready normed pt_ready pt_kept_act pt_kept_dve o_ready o_kept").split()
                (cache_in, sink_in, turned, kct_kept, nsink_ready, scores_ready, max_ready, bias_ready, exp_done, sink_biased, sink_exp,
                 den_ready, recip_ready, normed, pt_ready, pt_kept_act, pt_kept_dve, o_ready, o_kept) = (sem(n, st) for n in names)
                spilled = [sem(f"spilled{b}", st) for b in range(NBLK)]
                qk_in = [sem(f"qk_in{b}", st) for b in range(NBLK)]
                vA = vrow
                units = [(m, j) for m in range(TILES + 1) for j in range(AKV)]
                N = len(units)

                def keys(m):
                    return P if m == 0 else (WIN + NSAMP if m == TILES else 2 * P)

                def rows_of(m):
                    return NSAMP if m == TILES else P

                def key_tiles(m, j):
                    d = slice(j * HD, (j + 1) * HD)
                    if m == 0:
                        return [(vA[:, 0, d], slice(0, P), 0)]
                    if m == TILES:
                        new = slice(SP0, SP0 + NSAMP)
                        return [(vc[:, d], slice(0, P), 0), (vA[new, LAST, d], new, WIN)]
                    return [(vA[:, m - 1, d], slice(0, P), 0), (vA[:, m, d], slice(0, P), P)]

                with nc.Block() as block:
                    @block.sync
                    def _(sp):
                        sp.dma_start(kc[:, :], io["cache_a_k"][0, 0].rearrange("t h d -> t (h d)")).then_inc(cache_in, 16)
                        sp.dma_start(vc[:, :], io["cache_a_v"][0, 0].rearrange("t h d -> t (h d)")).then_inc(cache_in, 16)
                        sp.dma_start(sink[:, :], io["sinks_a"].to_broadcast([P, AH])).then_inc(sink_in, 16)
                        for b, (c0, w) in enumerate(BLOCKS):
                            sp.dma_start(mix[6:8, :, c0:c0 + w].rearrange("k p t -> p k t"), reg[:, 0:2, c0:c0 + w]).then_inc(spilled[b], 16)
                            sp.dma_start(reg[:, 2:5, c0:c0 + w], uT[2:5, :, c0:c0 + w].rearrange("k p t -> p k t")).then_inc(qk_in[b], 16)
                        for b, (c0, w) in enumerate(BLOCKS):
                            sp.wait_ge(spilled[b], 16)
                            sp.dma_start(reg[:, 0:2, c0:c0 + w], uT[0:2, :, c0:c0 + w].rearrange("k p t -> p k t")).then_inc(qk_in[b], 16)

                    @block.tensor
                    def _(pe):
                        pe.wait_ge(cache_in, 32)
                        pe.transpose(b_pt[:, 0, 0, :], kc[:, :], ident).then_inc(turned, 1)
                        pe.wait_ge(kct_kept, 1)

                        def scores(n):
                            m, j = units[n]
                            R, K = rows_of(m), keys(m)
                            if j == 0 and m % 4 == 0 and m < TILES:
                                pe.wait_ge(qk_in[m // 4], 32)
                            if n:
                                pe.wait_ge(exp_done, AG * n)
                            half = slice(j * CH, (j + 1) * CH)
                            q0 = SROW if m == TILES else m * P
                            for a in range(0, AG, 2):
                                if m < TILES:
                                    at = M_A0 if m == 0 else (M_A1 if m == 1 else M_A)
                                    pe.matmul(b_sc[:, n % 2, a:a + 2, 0:K], identb, wide(cb[:, at:at + K], 2), start=True, stop=False,
                                              skip_group_check=True)
                            for g in range(AG):
                                qh = reg[half, g, q0:q0 + R]
                                if m < TILES:
                                    k0 = max(m - 1, 0) * P
                                    last = pe.matmul(b_sc[0:R, n % 2, g, 0:K], qh, reg[half, 4, k0:k0 + K], start=False, stop=True,
                                                     skip_group_check=True)
                                else:
                                    pe.matmul(b_sc[0:R, n % 2, g, 0:WIN], qh, kcT[half, :], start=True, stop=True)
                                    last = pe.matmul(b_sc[0:R, n % 2, g, WIN:K], qh, reg[half, 4, SROW:SROW + NSAMP], start=True, stop=True)
                            last.then_inc(scores_ready, 1)

                        def turn(n):
                            m, j = units[n]
                            R = rows_of(m)
                            pe.wait_ge(normed, AG * (n + 1))
                            if n:
                                pe.wait_ge(pt_kept_act, n)
                                pe.wait_ge(pt_kept_dve, n)
                            for t, (_, part, k0) in enumerate(key_tiles(m, j)):
                                kn = part.stop - part.start
                                for g in range(AG):
                                    last = pe.transpose(b_pt[0:kn, t, g, 0:R], pr[0:R, n % 2, g, k0:k0 + kn], ident[0:R, 0:R])
                            last.then_inc(pt_ready, 1)

                        def values(n):
                            m, j = units[n]
                            R = rows_of(m)
                            pe.wait_ge(pt_kept_act, n + 1)
                            pe.wait_ge(pt_kept_dve, n + 1)
                            if n >= 4 and j == 0:
                                pe.wait_ge(o_kept, n // 2 - 1)
                            tiles_ = key_tiles(m, j)
                            for t, (v, part, k0) in enumerate(tiles_):
                                last = pe.matmul(b_o[j * CH:(j + 1) * CH, m % 2, :, 0:R], v, pt[part, n % 2, t, :, 0:R],
                                                 start=(t == 0), stop=(t == len(tiles_) - 1))
                            last.then_inc(o_ready, 1)

                        for n in range(N + 2):
                            if n < N:
                                scores(n)
                            if 1 <= n <= N:
                                turn(n - 1)
                            if n >= 2:
                                values(n - 2)

                    @block.scalar
                    def _(act):
                        def exps(n):
                            m, j = units[n]
                            R, K = rows_of(m), keys(m)
                            act.wait_ge(bias_ready, n + 1)
                            if n >= 2:
                                act.wait_ge(pt_ready, n - 1)
                            for g in range(AG):
                                act.activation(pr[0:R, n % 2, g, 0:K], b_sc[0:R, n % 2, g, 0:K], ACT.Exp, bias=nm[0:R, n % 2, g:g + 1],
                                               scale=SCALE, accum_out=den[0:R, n % 2, g:g + 1]).then_inc(exp_done, 1)
                            act.wait_ge(sink_biased, n + 1)
                            act.activation(se[0:R, n % 2, :], se[0:R, n % 2, :], ACT.Exp).then_inc(sink_exp, 1)

                        def keep(n):
                            m, j = units[n]
                            R = rows_of(m)
                            act.wait_ge(pt_ready, n + 1)
                            if n >= 2:
                                act.wait_ge(o_ready, n - 1)
                            act.activation(pt[:, n % 2, 0, :, 0:R], b_pt[:, 0, :, 0:R], ACT.Copy).then_inc(pt_kept_act, 1)

                        for n in range(N + 1):
                            if n < N:
                                exps(n)
                            if n >= 1:
                                keep(n - 1)

                    @block.vector
                    def _(dve):
                        dve.wait_ge(turned, 1)
                        dve.tensor_copy(kcT[:, :], b_pt[:, 0, 0, :]).then_inc(kct_kept, 1)
                        dve.wait_ge(sink_in, 16)
                        dve.tensor_scalar(nsink[:, :], sink[:, :], -1.0, None, ALU.mult).then_inc(nsink_ready, 1)
                        dve.wait_ge(nsink_ready, 1)

                        def bias(n):
                            m, j = units[n]
                            R, K = rows_of(m), keys(m)
                            hs = slice(j * AG, (j + 1) * AG)
                            dve.wait_ge(scores_ready, n + 1)
                            dve.tensor_reduce(mx[0:R, n % 2, :], b_sc[0:R, n % 2, :, 0:K], AX.X, ALU.max).then_inc(max_ready, 1)
                            dve.wait_ge(max_ready, n + 1)
                            if n >= 2:
                                dve.wait_ge(exp_done, AG * (n - 1))
                            dve.scalar_tensor_tensor(out=nm[0:R, n % 2, :], in0=mx[0:R, n % 2, :], scalar=-SCALE, in1=nsink[0:R, hs],
                                                     op0=ALU.mult, op1=ALU.min).then_inc(bias_ready, 1)
                            dve.wait_ge(bias_ready, n + 1)
                            dve.tensor_tensor(se[0:R, n % 2, :], sink[0:R, hs], nm[0:R, n % 2, :], ALU.add).then_inc(sink_biased, 1)

                        def norm(n):
                            m, j = units[n]
                            R, K = rows_of(m), keys(m)
                            dve.wait_ge(sink_exp, n + 1)
                            dve.wait_ge(exp_done, AG * (n + 1))
                            dve.tensor_tensor(den[0:R, n % 2, :], den[0:R, n % 2, :], se[0:R, n % 2, :], ALU.add).then_inc(den_ready, 1)
                            dve.wait_ge(den_ready, n + 1)
                            dve.reciprocal(rd[0:R, n % 2, :], den[0:R, n % 2, :]).then_inc(recip_ready, 1)
                            dve.wait_ge(recip_ready, n + 1)
                            for g in range(AG):
                                x = pr[0:R, n % 2, g, 0:K]
                                dve.tensor_scalar(x, x, rd[0:R, n % 2, g:g + 1], None, ALU.mult).then_inc(normed, 1)

                        def keep(n):
                            m, j = units[n]
                            R = rows_of(m)
                            dve.wait_ge(pt_ready, n + 1)
                            if n >= 2:
                                dve.wait_ge(o_ready, n - 1)
                            part = key_tiles(m, j)[-1][1]
                            if m == 0:
                                dve.memset(pt[:, n % 2, 1, :, :], 0.0).then_inc(pt_kept_dve, 1)
                            else:
                                dve.tensor_copy(pt[part, n % 2, 1, :, 0:R], b_pt[0:part.stop - part.start, 1, :, 0:R]).then_inc(pt_kept_dve, 1)

                        def keep_out(m):
                            dve.wait_ge(o_ready, 2 * m + 2)
                            q0, cnt = (SROW, NSAMP) if m == TILES else (m * P, SP0 if m == LAST else P)
                            dve.tensor_copy(reg[:, 0:AG, q0:q0 + cnt], b_o[:, m % 2, :, 0:cnt]).then_inc(o_kept, 1)

                        for n in range(N + 3):
                            if n < N:
                                bias(n)
                            if n < N:
                                norm(n)
                            if 1 <= n <= N:
                                keep(n - 1)
                            if n >= 3 and (n - 3) % 2:
                                keep_out((n - 3) // 2)

        def stick_breaking(side_tiles):
            KC = 512
            QS, KS = 0, 4
            with ExitStack() as st:
                kc = sb("kc", [P, 2, VBW], st=st)
                vc = sb("vc", [P, 2, VBW], st=st)
                kcT = sb("kcT", [P, 2, PAST], st=st)
                keepb = sb("keepb", [P, 3, KC], st=st)
                beta = sb("beta", [P, 4, KC], st=st)
                prod = sb("prod", [P, 2, T + 1], st=st)
                wt = sb("wt", [P, 2, 4, P], st=st)
                b_z = pb("b_z", [P, 2, KC], st)
                b_w = pb("b_w", [P, 2, 4, P], st)
                b_o = pb("b_o", [P, 2, 512], st)
                side = SideProjection(st, "silu", side_tiles, sz)
                spilled = [sem(f"spilled{b}", st) for b in range(NBLK)]
                qk_in = [sem(f"qk_in{b}", st) for b in range(NBLK)]
                names = ("cache_in turned kct_kept z_ready keep_ready beta_ready one_ready prod_ready w_ready wt_ready wt_kept o_ready o_kept part_kept").split()
                (cache_in, turned, kct_kept, z_ready, keep_ready, beta_ready, one_ready, prod_ready, w_ready, wt_ready, wt_kept, o_ready,
                 o_kept, part_kept) = (sem(n, st) for n in names)
                new = slice(SP0, SP0 + NSAMP)

                def side_piece(s):
                    return side.pieces * s // (N - 1)

                def side_units(s):
                    return range(side_piece(s) // KT, min(side_piece(s + 1) // KT, side.units))
                steps = []
                for m in range(TILES + 1):
                    for h in range(BH):
                        if m == TILES:
                            steps.append((m, h, 0, PAST + NSAMP, True, True))
                            continue
                        L = (m + 1) * P
                        for k0 in range((L - 1) // KC * KC, -1, -KC):
                            steps.append((m, h, k0, min(KC, L - k0), k0 + KC >= L, k0 == 0))
                N = len(steps)
                rowno = []
                for s_ in steps:
                    rowno.append((rowno[-1] if rowno else -1) + s_[4])
                row_end = [s + 1 for s, s_ in enumerate(steps) if s_[5]]

                def rows_of(m):
                    return NSAMP if m == TILES else P

                def end(m):
                    return PAST + NSAMP if m == TILES else (m + 1) * P

                def key_tiles(s):
                    m, h, k0, nk = steps[s][:4]
                    d = slice(VAW + h * HD, VAW + (h + 1) * HD)
                    if m == TILES:
                        dc = slice(h * HD, (h + 1) * HD)
                        return [(vc[:, 0, dc], slice(0, P), 0), (vc[:, 1, dc], slice(0, P), P), (vrow[new, LAST, d], new, PAST)]
                    return [(vrow[:, k0 // P + t, d], slice(0, P), t * P) for t in range(nk // P)]

                def keep_weights(eng, s, copy):
                    eng.wait_ge(wt_ready, s + 1)
                    if s >= 2:
                        eng.wait_ge(o_ready, s - 1)
                    if s >= 1:
                        eng.wait_ge(wt_kept, s)
                    R = rows_of(steps[s][0])
                    tiles_ = key_tiles(s)
                    full = [t for t, x in enumerate(tiles_) if x[1].stop - x[1].start == P]
                    if len(full) == len(tiles_):
                        copy(wt[:, s % 2, 0:len(full), 0:R], b_w[:, s % 2, 0:len(full), 0:R]).then_inc(wt_kept, 1)
                    else:
                        copy(wt[:, s % 2, 0:len(full), 0:R], b_w[:, s % 2, 0:len(full), 0:R]).then_inc(part_kept, 1)
                        eng.wait_ge(part_kept, steps[s][1] + 1)
                        copy(wt[new, s % 2, len(full), 0:R], b_w[0:NSAMP, s % 2, len(full), 0:R]).then_inc(wt_kept, 1)

                with nc.Block() as block:
                    @block.sync
                    def _(sp):
                        for name, dst in (("cache_b_k", kc), ("cache_b_v", vc)):
                            sp.dma_start(dst[:, :, :], io[name][0, 0].rearrange("(t p) h d -> p t (h d)", p=P)).then_inc(cache_in, 16)
                        for b, (c0, w) in enumerate(BLOCKS):
                            sp.dma_start(mix[0:4, :, c0:c0 + w].rearrange("k p t -> p k t"), reg[:, 0:4, c0:c0 + w]).then_inc(spilled[b], 16)
                            sp.dma_start(reg[:, KS:KS + 2, c0:c0 + w], uT[7:9, :, c0:c0 + w].rearrange("k p t -> p k t")).then_inc(qk_in[b], 16)
                            sp.wait_ge(spilled[b], 16)
                            sp.dma_start(reg[:, QS:QS + 2, c0:c0 + w], uT[5:7, :, c0:c0 + w].rearrange("k p t -> p k t")).then_inc(qk_in[b], 16)
                        side.transfers(sp)

                    @block.tensor
                    def _(pe):
                        pe.wait_ge(cache_in, 32)
                        for a in range(2):
                            for t in range(2):
                                last = pe.transpose(b_w[:, 0, 2 * a + t, :], kc[:, t, a * P:(a + 1) * P], ident)
                        last.then_inc(turned, 1)
                        pe.wait_ge(kct_kept, 1)

                        def scores(s):
                            m, h, k0, nk, first, last_ = steps[s]
                            R = rows_of(m)
                            half = slice((h % 2) * CH, (h % 2) * CH + CH)
                            if first and h == 0 and m % 4 == 0 and m < TILES:
                                pe.wait_ge(qk_in[m // 4], 32)
                            if s >= 2:
                                pe.wait_ge(keep_ready, s - 1)
                                pe.wait_ge(beta_ready, s - 1)
                            bank = b_z[0:R, s % 2]
                            q0 = SROW if m == TILES else m * P
                            q = reg[half, QS + h // 2, q0:q0 + R]
                            if m == TILES:
                                pe.matmul(bank[:, 0:PAST], q, kcT[half, h // 2, :], start=True, stop=True)
                                last = pe.matmul(bank[:, PAST:nk], q, reg[half, KS + h // 2, SROW:SROW + NSAMP], start=True, stop=False,
                                                 skip_group_check=True)
                                last = pe.matmul(bank[:, PAST:nk], identb[0:R, 0:R], cb[0:R, M_B:M_B + NSAMP], start=False, stop=True,
                                                 skip_group_check=True)
                            else:
                                masks = ([(nk - P, M_B)] if first else []) + ([(0, M_PAD)] if last_ else [])
                                last = pe.matmul(bank[:, 0:nk], q, reg[half, KS + h // 2, k0:k0 + nk], start=True, stop=not masks,
                                                 skip_group_check=True)
                                for n, (at, mask) in enumerate(masks):
                                    last = pe.matmul(bank[:, at:at + P], identb, cb[:, mask:mask + P], start=False,
                                                     stop=(n == len(masks) - 1), skip_group_check=True)
                            last.then_inc(z_ready, 1)

                        def turn(s):
                            R = rows_of(steps[s][0])
                            pe.wait_ge(w_ready, s + 1)
                            if s >= 2:
                                pe.wait_ge(wt_kept, s - 1)
                            for t, (_, part, at) in enumerate(key_tiles(s)):
                                kn = part.stop - part.start
                                last = pe.transpose(b_w[0:kn, s % 2, t, 0:R], beta[0:R, s % 4, at:at + kn], ident[0:R, 0:R])
                            last.then_inc(wt_ready, 1)

                        def values(s):
                            m, h, k0, nk, first, last_ = steps[s]
                            R = rows_of(m)
                            pe.wait_ge(wt_kept, s + 1)
                            row = rowno[s]
                            pair = row // 2
                            if first and h % 2 == 0 and pair >= 2:
                                pe.wait_ge(o_kept, pair - 1)
                            tiles_ = key_tiles(s)
                            for t, (v, part, at) in enumerate(tiles_):
                                last = pe.matmul(b_o[(h % 2) * CH:(h % 2) * CH + CH, pair % 2, 0:R], v, wt[part, s % 2, t, 0:R],
                                                 start=(first and t == 0), stop=(last_ and t == len(tiles_) - 1))
                            last.then_inc(o_ready, 1)

                        for s in range(N + 4):
                            if s < N:
                                scores(s)
                                side.products(pe, side_piece(s), side_piece(s + 1) - side_piece(s))
                            if 3 <= s < N + 3:
                                turn(s - 3)
                            if s >= 4:
                                values(s - 4)

                    @block.scalar
                    def _(act):
                        def sigmoids(s):
                            m, h, k0, nk, first, last_ = steps[s]
                            R = rows_of(m)
                            act.wait_ge(z_ready, s + 1)
                            if s >= 3:
                                act.wait_ge(prod_ready, s - 2)
                            act.activation(keepb[0:R, s % 3, 0:nk], b_z[0:R, s % 2, 0:nk], ACT.Sigmoid, scale=-SCALE).then_inc(keep_ready, 1)
                            if s >= 4:
                                act.wait_ge(wt_ready, s - 3)
                            act.activation(beta[0:R, s % 4, 0:nk], b_z[0:R, s % 2, 0:nk], ACT.Sigmoid, scale=SCALE).then_inc(beta_ready, 1)

                        def keep(s):
                            keep_weights(act, s, lambda o, i: act.activation(o, i, ACT.Copy))

                        for s in range(N + 4):
                            if s >= 4 and s % 2:
                                keep(s - 4)
                            if s < N:
                                sigmoids(s)
                                for n in side_units(s):
                                    side.keep(act, n)

                    @block.gpsimd
                    def _(pool):
                        for s, (m, h, k0, nk, first, last_) in enumerate(steps):
                            R = rows_of(m)
                            pool.wait_ge(prod_ready, s + 1)
                            pool.wait_ge(beta_ready, s + 1)
                            w = beta[0:R, s % 4, 0:nk]
                            pool.tensor_tensor(w, w, prod[0:R, rowno[s] % 2, k0 + 1:k0 + nk + 1], ALU.mult).then_inc(w_ready, 1)

                    @block.vector
                    def _(dve):
                        dve.wait_ge(turned, 1)
                        dve.tensor_copy(kcT[:, :, :], b_w[:, 0, :, :].rearrange("p (a t) k -> p a (t k)", a=2)).then_inc(kct_kept, 1)

                        def scan(s):
                            m, h, k0, nk, first, last_ = steps[s]
                            R, row = rows_of(m), rowno[s]
                            if first:
                                if row >= 2:
                                    dve.wait_ge(w_ready, row_end[row - 2])
                                dve.memset(prod[0:R, row % 2, k0 + nk:k0 + nk + 1], 1.0).then_inc(one_ready, 1)
                                dve.wait_ge(one_ready, row + 1)
                            else:
                                dve.wait_ge(prod_ready, s)
                            dve.wait_ge(keep_ready, s + 1)
                            kv = keepb[0:R, s % 3, 0:nk][:, ::-1]
                            dve.tensor_tensor_scan(prod[0:R, row % 2, k0:k0 + nk][:, ::-1], kv, kv, prod[0:R, row % 2, k0 + nk:k0 + nk + 1],
                                                   ALU.mult, ALU.bypass).then_inc(prod_ready, 1)

                        def keep_out(pair):
                            m, a = pair // 2, pair % 2
                            q0, cnt = (SROW, NSAMP) if m == TILES else (m * P, SP0 if m == LAST else P)
                            dve.tensor_copy(reg[:, QS + a, q0:q0 + cnt], b_o[:, pair % 2, 0:cnt]).then_inc(o_kept, 1)

                        for s in range(N + 5):
                            if s >= 4 and s - 4 < N and s % 2 == 0:
                                keep_weights(dve, s - 4, lambda o, i: dve.tensor_copy(o, i))
                            if s < N:
                                scan(s)
                                for n in side_units(s):
                                    side.gate(dve, n)
                            if s >= 5:
                                e = s - 5
                                if steps[e][5] and steps[e][1] % 2:
                                    dve.wait_ge(o_ready, e + 1)
                                    keep_out(rowno[e] // 2)

        def output():
            with ExitStack() as st:
                MIX0 = D
                gpost = sb("gpost", [P, D], st=st)
                xres = sb("xres", [P, 3, D], st=st)
                ssq, lnv, rstd = (sb(n, [P, 3], st=st) for n in ("ssq", "lnv", "rstd"))
                yy = sb("yy", [P, 3, D], st=st)
                b_y = pb("b_y", [P, 3, D], st)
                wo_in = sem("wo_in", st)
                mix_in = [sem(f"mix_in{i}", st) for i in range(3)]
                spilled, gated = sem("spilled", st), sem("gated", st)
                zin = sb("zin", [P, 3, KT, P], st=st)
                x_in = [sem(f"x_in{i}", st) for i in range(3)]
                y_out = [sem(f"y_out{i}", st) for i in range(3)]
                y_ready, sq_done, ln_done, rstd_done, normed, summed = (sem(n, st) for n in
                                                                      ("y_ready", "sq_done", "ln_done", "rstd_done", "normed", "summed"))
                xp, wo = io["x_prompt"][0], io["w_out"][0]
                yp = io["y_prompt"][0]
                with nc.Block() as block:
                    def rows(ap, n, base):
                        return ap[bass.ds(n * P + base, P), :]

                    @block.sync
                    def _(sp):
                        for b, (c0, w) in enumerate(BLOCKS):
                            sp.dma_start(mix[4:6, :, c0:c0 + w].rearrange("k p t -> p k t"), reg[:, 0:2, c0:c0 + w]).then_inc(spilled, 16)
                        for g in range(AG):
                            for j in range(AKV):
                                sp.dma_start(hT[j * CH:(j + 1) * CH, g, 0:D], wo[(j * AG + g) * HD:(j * AG + g + 1) * HD, :]).then_inc(wo_in, 16)
                        sp.dma_start(hT[:, AG:KT, 0:D], wo[AH * HD:D, :].rearrange("(k p) n -> p k n", p=P)).then_inc(wo_in, 16)
                        sp.dma_start(gpost[:, :], io["norm_post"].to_broadcast([P, D])).then_inc(wo_in, 16)

                        def load(n, s):
                            if not isinstance(n, int) or n >= 3:
                                sp.wait_ge(y_ready, n - 2)
                            c = slice(n * P, (n + 1) * P) if isinstance(n, int) else bass.ds(n * P, P)
                            sp.dma_start(hT[:, :, MIX0 + s * P:MIX0 + (s + 1) * P], mix[:, :, c].rearrange("k p t -> p k t")).then_inc(mix_in[s], 16)
                            sp.dma_start(zin[:, s], sz[:, :, c].rearrange("k p t -> p k t")).then_inc(mix_in[s], 16)
                            if not isinstance(n, int) or n >= 3:
                                sp.wait_ge(summed, n - 2)
                            if isinstance(n, int) and n == 0:
                                sp.dma_start(xres[CH:P, s, :], xp[0:CH, :]).then_inc(x_in[s], 32)
                            elif isinstance(n, int) and n == LAST:
                                sp.dma_start(xres[0:SP0, s, :], xp[SEQ - SP0:SEQ, :]).then_inc(x_in[s], 16)
                                sp.dma_start(xres[SP0:SP0 + NSAMP, s, :], io["x_sample"][0]).then_inc(x_in[s], 16)
                            else:
                                sp.dma_start(xres[:, s, :], rows(xp, n, -CH)).then_inc(x_in[s], 32)

                        sp.wait_ge(spilled, 16 * NBLK)
                        load(0, 0)
                        load(1, 1)
                        load(2, 2)
                        with sp.Fori(0, (TILES - 5) // 3) as i:
                            for u in range(3):
                                load(3 * i + (u + 3), u)
                        for n in range(LAST - 1, TILES):
                            load(n, n % 3)

                    @block.tensor
                    def _(pe):
                        pe.wait_ge(wo_in, 160)

                        def step(n, s):
                            pe.wait_ge(gated, n + 1)
                            if not isinstance(n, int) or n >= 3:
                                pe.wait_ge(normed, n - 2)
                            for c in range(2):
                                for k in range(KT):
                                    last = pe.matmul(b_y[:, s, c * 512:(c + 1) * 512], hT[:, k, MIX0 + s * P:MIX0 + (s + 1) * P],
                                                     hT[:, k, c * 512:(c + 1) * 512], start=(k == 0), stop=(k == KT - 1))
                            last.then_inc(y_ready, 1)
                        for n in range(3):
                            step(n, n)
                        with pe.Fori(0, (TILES - 5) // 3) as i:
                            for u in range(3):
                                step(3 * i + (u + 3), u)
                        for n in range(LAST - 1, TILES):
                            step(n, n % 3)

                    @block.scalar
                    def _(act):
                        def step(n, s):
                            act.wait_ge(y_ready, n + 1)
                            if not isinstance(n, int) or n >= 3:
                                act.wait_ge(y_out[s], y_stored(n, s))
                            act.activation(yy[:, s], b_y[:, s, :], ACT.Square, accum_out=ssq[:, s:s + 1]).then_inc(sq_done, 1)
                            act.wait_ge(sq_done, n + 1)
                            act.activation(lnv[:, s:s + 1], ssq[:, s:s + 1], ACT.Ln, bias=eps, scale=1.0 / D).then_inc(ln_done, 1)
                            act.wait_ge(ln_done, n + 1)
                            act.activation(rstd[:, s:s + 1], lnv[:, s:s + 1], ACT.Exp, scale=-0.5).then_inc(rstd_done, 1)
                        it = {}

                        def y_stored(n, s):
                            return 32 * (n // 3) if isinstance(n, int) else it["i"] * 32 + 32

                        for n in range(3):
                            step(n, n)
                        with act.Fori(0, (TILES - 5) // 3) as i:
                            it["i"] = i
                            for u in range(3):
                                step(3 * i + (u + 3), u)
                        for n in range(LAST - 1, TILES):
                            step(n, n % 3)

                    @block.vector
                    def _(dve):
                        dve.wait_ge(wo_in, 160)

                        def gate(n, s, landed):
                            m_ = hT[:, :, MIX0 + s * P:MIX0 + (s + 1) * P]
                            dve.wait_ge(mix_in[s], landed)
                            dve.tensor_tensor(m_, m_, zin[:, s], ALU.mult).then_inc(gated, 1)

                        def norm(n, s):
                            dve.wait_ge(rstd_done, n + 1)
                            dve.scalar_tensor_tensor(out=yy[:, s], in0=b_y[:, s, :], scalar=rstd[:, s:s + 1], in1=gpost[:, :],
                                                     op0=ALU.mult, op1=ALU.mult).then_inc(normed, 1)

                        for n in range(3):
                            gate(n, n, 32)
                        norm(0, 0)
                        with dve.Fori(0, (TILES - 5) // 3) as i:
                            for u in range(3):
                                gate(3 * i + (u + 3), u, 32 * i + 64)
                                norm(3 * i + (u + 1), (u + 1) % 3)
                        for n in range(LAST - 1, TILES):
                            gate(n, n % 3, 32 * (n // 3 + 1))
                            norm(n - 2, (n - 2) % 3)
                        norm(LAST - 1, (LAST - 1) % 3)
                        norm(LAST, LAST % 3)

                    @block.gpsimd
                    def _(pool):
                        def step(n, s, landed, part):
                            pool.wait_ge(normed, n + 1)
                            pool.wait_ge(x_in[s], landed)
                            pool.tensor_tensor(yy[part, s], yy[part, s], xres[part, s, :], ALU.add).then_inc(summed, 1)
                            pool.wait_ge(summed, n + 1)

                        step(0, 0, 32, slice(CH, P))
                        pool.dma_start(yp[0:CH, :], yy[CH:P, 0]).then_inc(y_out[0], 32)
                        for n in (1, 2):
                            step(n, n, 32, slice(0, P))
                            pool.dma_start(yp[n * P - CH:(n + 1) * P - CH, :], yy[:, n]).then_inc(y_out[n], 32)
                        with pool.Fori(0, (TILES - 5) // 3) as i:
                            for u in range(3):
                                step(3 * i + (u + 3), u, 32 * i + 64, slice(0, P))
                                pool.dma_start(rows(yp, 3 * i + (u + 3), -CH), yy[:, u]).then_inc(y_out[u], 32)
                        n = LAST - 1
                        step(n, n % 3, 32 * (n // 3 + 1), slice(0, P))
                        pool.dma_start(yp[n * P - CH:(n + 1) * P - CH, :], yy[:, n % 3]).then_inc(y_out[n % 3], 32)
                        n = LAST
                        step(n, n % 3, 32 * (n // 3 + 1), slice(0, SP0 + NSAMP))
                        pool.dma_start(yp[SEQ - SP0:SEQ, :], yy[0:SP0, n % 3]).then_inc(y_out[n % 3], 16)
                        pool.dma_start(io["y_sample"][0], yy[SP0:SP0 + NSAMP, n % 3]).then_inc(y_out[n % 3], 16)
                        for s in range(3):
                            pool.wait_ge(y_out[s], 32 * len([n for n in range(TILES) if n % 3 == s]))

        def stage(work, *args, **kwargs):
            with nc.cleanup_on_exit():
                work(*args, **kwargs)

        stage(norm_and_transpose)
        with ExitStack() as st:
            cx = {n: sb("cx_" + n, [P, TILES, 4], st=st) for n in ("g", "ngc", "beta", "eg", "neg_eg", "ekd")}
            cx["gl"] = sb("cx_gl", [P, TILES, 2, 2], st=st)
            cx["S"] = sb("cx_S", [P, 2, 2, HD], st=st)
            stage(conv_and_gates, cx)
            pair = lambda c0, g: [(c0 + g * HD, HD), (c0 + (AG + g) * HD, HD)]
            tile = lambda c0: [(c0, P)]
            stage(delta_net, cx, [pair(QA, g) for g in range(AG)] + [tile(c) for c in (KA, QB, QB + P, KB, KB + P)])
        stage(window_attention)
        stage(key_rows, [4], 2, LAST - 1, a_key_stores)
        stage(stick_breaking, [pair(ZZ, g) for g in range(AG)] + [tile(ZZ + AH * HD + i * P) for i in range(4)])
        stage(key_rows, [4, 5], TILES, 0, b_key_stores)
        stage(output)


_INS = ["x_prompt", "x_sample", "cache_a_k", "cache_a_v", "cache_b_k", "cache_b_v", "state_c_conv", "state_c_ssm", "meta_tokens",
        "norm_pre", "norm_post", "w_in", "w_out", "sinks_a", "conv_c", "a_log_c", "dt_bias_c", "onorm_c"]
_OUTS = [("y_prompt", (1, SEQ, D)), ("y_sample", (1, NSAMP, D)),
         ("p_a_k", (1, 1, WIN, AKV, HD)), ("p_a_v", (1, 1, WIN, AKV, HD)),
         ("p_b_k", (1, 1, NMETA + SEQ, BH, HD)), ("p_b_v", (1, 1, NMETA + SEQ, BH, HD)),
         ("p_c_conv", (1, 1, 3, 768)), ("p_c_ssm", (1, 1, CHD, HD, HD)),
         ("s_a_k", (1, 1, WIN, AKV, HD)), ("s_a_v", (1, 1, WIN, AKV, HD)),
         ("s_b_k", (1, 1, NSAMP, BH, HD)), ("s_b_v", (1, 1, NSAMP, BH, HD)),
         ("s_c_conv", (1, 1, 3, 768)), ("s_c_ssm", (1, 1, CHD, HD, HD))]


def build(nc, arrays):
    io = {}
    for name, a in arrays.items():
        io[name] = nc.dram_tensor("in_" + name, a.shape, mybir.dt.from_np(a.dtype), kind="ExternalInput").ap()
    for name, shape in _OUTS:
        io[name] = nc.dram_tensor("out_" + name, shape, F32, kind="ExternalOutput").ap()
    for name, tiles in (("mix", KT), ("uT", 9), ("sz", KT)):
        io[name] = nc.dram_tensor(name + "_scratch", (tiles, P, T), F32, kind="Internal").ap()
    stream_layer(nc, io)


def kernel(**inputs):
    import concourse.bacc as bacc
    from concourse.bass_utils import run_bass_kernel_spmd as run
    arrays = {name: np.ascontiguousarray(inputs[name]) for name in _INS}
    arrays["cf"], arrays["cb"] = shape_constants()
    nc = bacc.Bacc("TRN2", target_bir_lowering=False, num_devices=1)
    build(nc, arrays)
    r = run(nc, [{"in_" + n: a for n, a in arrays.items()}], core_ids=[0])
    return tuple(r.results[0]["out_" + name] for name, _ in _OUTS)
```

```python
from contextlib import ExitStack

import numpy as np
import concourse.bass as bass
from concourse import mybir

F32 = mybir.dt.float32
F32R = mybir.dt.float32r
BF16 = mybir.dt.bfloat16
ALU = mybir.AluOpType
ACT = mybir.ActivationFunctionType
AX = mybir.AxisListType

P = 128
D = 1024
KT = D // P
SEQ, NMETA, NSAMP, PAST, WIN = 2048, 16, 32, 256, 128
CH = 64
HD = 64
PAD = CH - NMETA
ROW0 = CH
SROW = ROW0 + SEQ
TILES = -(-(SROW + NSAMP) // P)
T = TILES * P
LAST = TILES - 1
SP0 = SROW - LAST * P
AH, AKV, BH, CHD = 8, 2, 4, 4
AG = AH // AKV
QA, KA, VA, QB, KB, VB, XC = 0, 512, 640, 768, 1024, 1280, 1536
AB, ZZ = 2304, 2312
NIN = 3336
VAW, VBW, ABW = 128, 256, 8
RV = VAW + VBW + ABW
SCALE = HD ** -0.5
NEG = -1e30
LN_EXP = "natural_log_exp_and_others"
BLOCKS = [(512 * b, min(512, T - 512 * b)) for b in range(-(-T // 512))]
NBLK = len(BLOCKS)
SWAPPED = 3
RAWZ = 3
LEVELS = 6
C_ID, C_TRI, C_BLK, C_LO, C_HI, C_LVL = 0, 128, 256, 384, 512, 640
C_EPS = C_LVL + LEVELS * P
C_ONE = C_EPS + 1
NCF = C_EPS + 2
M_ID, M_DT, M_A0, M_A1, M_A, M_B, M_PAD = 0, 128, 256, 384, 640, 896, 1024
NCB = M_PAD + 128


def shape_constants():
    r = np.arange(P)
    same = r[:, None] // CH == r[None, :] // CH
    cf = np.zeros((P, NCF), np.float32)
    cf[:, C_ID:C_ID + P] = np.eye(P)
    cf[:, C_TRI:C_TRI + P] = same & (r[:, None] <= r[None, :])
    cf[:, C_BLK:C_BLK + P] = same
    cf[:, C_LO:C_LO + P] = (r < CH)[:, None]
    cf[:, C_HI:C_HI + P] = (r >= CH)[:, None]
    for lv in range(LEVELS):
        s = 1 << lv
        j, i = r[:, None], r[None, :]
        cf[:, C_LVL + lv * P:C_LVL + (lv + 1) * P] = (j // (2 * s) == i // (2 * s)) & (j % (2 * s) < s) & (i % (2 * s) >= s)
    cf[:, C_EPS] = 1e-6
    cf[:, C_ONE] = 1.0
    cb = np.zeros((P, NCB), np.float32)
    cb[:, M_ID:M_ID + P] = np.eye(P)
    cb[:, M_DT:M_DT + P] = np.where(same & (r[:, None] <= r[None, :]), 0, NEG)
    q, k = r[:, None], np.arange(2 * P)[None, :]
    win = np.where(q < CH, k < 3 * CH, k >= CH)
    cb[:, M_A:M_A + 2 * P] = np.where(win, 0, NEG)
    cb[:, M_A1:M_A1 + 2 * P] = np.where(win & (k >= PAD), 0, NEG)
    cb[:, M_A0:M_A0 + P] = np.where(win[:, P:] & (k[:, :P] >= PAD), 0, NEG)
    cb[:, M_B:M_B + P] = np.where(r[None, :] < r[:, None], 0, NEG)
    cb[:, M_PAD:M_PAD + P] = np.where(r[None, :] >= PAD, 0, NEG)
    return cf, cb


def stream_layer(nc, io):
    top = ExitStack()
    with top:
        top.enter_context(nc.allow_non_contiguous_dma(reason="short vectors turned onto the partitions"))
        scope = [0]

        def fresh(name):
            scope[0] += 1
            return f"{name}_{scope[0]}"

        def sb(name, shape, dt=F32, st=top):
            return st.enter_context(nc.sbuf_tensor(fresh(name), shape, dt))

        def pb(name, shape, st):
            return st.enter_context(nc.psum_tensor(fresh(name), shape, F32))

        def sem(name, st):
            return nc.alloc_semaphore(name=fresh(name))

        cf = sb("cf", [P, NCF])
        cb = sb("cb", [P, NCB], BF16)
        hT = sb("hT", [P, KT, T])
        mixers = top.enter_context(ExitStack())
        reg = sb("reg", [P, 6, T], st=mixers)
        vrow = sb("vrow", [P, TILES, RV], st=mixers)
        wslot = sb("wslot", [P, 2, KT, P], st=mixers)
        mix, uT, sz = io["mix"], io["uT"], io["sz"]
        ident = cf[:, C_ID:C_ID + P]
        identb = cb[:, M_ID:M_ID + P]
        eps = cf[:, C_EPS:C_EPS + 1]
        one = cf[:, C_ONE:C_ONE + 1]
        w_in = io["w_in"][0].rearrange("(k p) n -> p k n", p=P)

        def wide(ap, n, axis=1):
            a = ap.unsqueeze(axis)
            shape = list(a.shape)
            shape[axis] = n
            return a.to_broadcast(shape)


        def norm_and_transpose():
            with ExitStack() as st:
                xin = sb("xin", [P, 3, D], st=st)
                junk = sb("junk", [P, D], st=st)
                gpre = sb("gpre", [P, KT], st=st)
                ssq, lnv, rstd = (sb(n, [P, TILES], st=st) for n in ("ssq", "lnv", "rstd"))
                wv = sb("wv", [P, KT, RV], st=st)
                tp = pb("tp", [P, 3, KT, P], st)
                acc = pb("acc", [P, 2, 512], st)
                wv_in, row_ready, row_kept = (sem(n, st) for n in ("wv_in", "row_ready", "row_kept"))
                consts_in, zeroed, masks_cast = sem("consts_in", st), sem("zeroed", st), sem("masks_cast", st)
                x_in = [sem(f"x_in{i}", st) for i in range(3)]
                sq_done, ln_done, rstd_done = (sem(n, st) for n in ("sq_done", "ln_done", "rstd_done"))
                scaled, turned, kept = (sem(n, st) for n in ("scaled", "turned", "kept"))
                xp = io["x_prompt"][0]
                tile_of = lambda n: (0, LAST)[n] if n < 2 else n - 1
                with nc.Block() as block:
                    @block.sync
                    def _(sp):
                        sp.wait_ge(zeroed, 2)
                        sp.dma_start(xin[PAD:CH, 0, :], io["meta_tokens"]).then_inc(x_in[0], 16)
                        sp.dma_start(xin[CH:P, 0, :], xp[0:CH, :]).then_inc(x_in[0], 16)
                        sp.dma_start(xin[0:SP0, 1, :], xp[SEQ - SP0:SEQ, :]).then_inc(x_in[1], 16)
                        sp.dma_start(xin[SP0:SP0 + NSAMP, 1, :], io["x_sample"][0]).then_inc(x_in[1], 16)
                        sp.dma_start(xin[:, 2, :], xp[CH:CH + P, :]).then_inc(x_in[2], 32)
                        sp.dma_start(cf[:, :], io["cf"]).then_inc(consts_in, 16)
                        sp.dma_start(gpre[:, :], io["norm_pre"][0].rearrange("(k p) -> p k", p=P)).then_inc(consts_in, 16)
                        sp.dma_start(reg[:, 0, 0:NCB], io["cb"]).then_inc(consts_in, 16)
                        sp.dma_start(wv[:, :, 0:VAW], w_in[:, :, VA:VA + VAW]).then_inc(wv_in, 16)
                        sp.dma_start(wv[:, :, VAW:VAW + VBW], w_in[:, :, VB:VB + VBW]).then_inc(wv_in, 16)
                        sp.dma_start(wv[:, :, VAW + VBW:RV], w_in[:, :, AB:AB + ABW]).then_inc(wv_in, 16)
                        for n in range(3, 5):
                            sp.wait_ge(turned, n - 2)
                            sp.dma_start(xin[:, n % 3, :], xp[CH + P * (n - 2):CH + P * (n - 1), :]).then_inc(x_in[n % 3], 32)
                        with sp.Fori(0, (TILES - 5) // 3) as i:
                            for u in range(3):
                                sp.wait_ge(turned, 3 * i + (u + 3))
                                sp.dma_start(xin[:, (u + 2) % 3, :],
                                             xp[bass.ds(i * (3 * P) + (CH + P * (u + 3)), P), :]).then_inc(x_in[(u + 2) % 3], 32)

                    @block.gpsimd
                    def _(pool):
                        pool.memset(xin[0:CH, 0, :], 0.0).then_inc(zeroed, 1)
                        pool.memset(xin[SP0 + NSAMP:P, 1, :], 0.0).then_inc(zeroed, 1)

                    @block.scalar
                    def _(act):
                        def step(n, slot, col, landed):
                            act.wait_ge(x_in[slot], landed)
                            act.activation(junk[:, :], xin[:, slot, :], ACT.Square, accum_out=ssq[:, col]).then_inc(sq_done, 1)
                            act.wait_ge(sq_done, n + 1)
                            act.activation(lnv[:, col], ssq[:, col], ACT.Ln, bias=eps, scale=1.0 / D).then_inc(ln_done, 1)
                            act.wait_ge(ln_done, n + 1)
                            act.activation(rstd[:, col], lnv[:, col], ACT.Exp, scale=-0.5).then_inc(rstd_done, 1)

                        act.preload_act_table_set(LN_EXP)
                        act.wait_ge(consts_in, 48)
                        step(0, 0, slice(0, 1), 32)
                        step(1, 1, slice(LAST, TILES), 32)
                        with act.Fori(0, (TILES - 2) // 3) as i:
                            for u in range(3):
                                s = (u + 2) % 3
                                step(3 * i + (u + 2), s, bass.ds(3 * i + (u + 1), 1), 32 * i + (32 if s == 2 else 64))

                    @block.vector
                    def _(dve):
                        def scale(n, slot, col):
                            dve.wait_ge(rstd_done, n + 1)
                            dve.tensor_scalar(xin[:, slot, :], xin[:, slot, :], rstd[:, col], None, ALU.mult).then_inc(scaled, 1)

                        def keep(n, slot, cols):
                            dve.wait_ge(turned, n + 1)
                            for k in (0, KT // 2):
                                dve.tensor_tensor(hT[:, k:k + KT // 2, cols], tp[:, slot, k:k + KT // 2, :],
                                                  gpre[:, k:k + KT // 2].unsqueeze(2).to_broadcast([P, KT // 2, P]),
                                                  ALU.mult).then_inc(kept, 1)

                        def keep_row(n, tile):
                            dve.wait_ge(row_ready, n + 1)
                            dve.tensor_copy(vrow[:, tile, :], acc[:, n % 2, 0:RV]).then_inc(row_kept, 1)

                        dve.wait_ge(consts_in, 48)
                        dve.tensor_copy(cb[:, :], reg[:, 0, 0:NCB]).then_inc(masks_cast, 1)
                        scale(0, 0, slice(0, 1))
                        for n in range(TILES):
                            if n + 1 < TILES:
                                scale(n + 1, (n + 1) % 3, slice(tile_of(n + 1), tile_of(n + 1) + 1))
                            keep(n, n % 3, slice(P * tile_of(n), P * tile_of(n) + P))
                            if n:
                                keep_row(n - 1, tile_of(n - 1))
                        keep_row(TILES - 1, tile_of(TILES - 1))

                    @block.tensor
                    def _(pe):
                        def turn(n):
                            pe.wait_ge(scaled, n + 1)
                            if n >= 3:
                                pe.wait_ge(kept, 2 * (n - 2))
                            for k in range(KT):
                                last = pe.transpose(tp[:, n % 3, k, :], xin[:, n % 3, k * P:(k + 1) * P], ident)
                            last.then_inc(turned, 1)

                        def row(n):
                            m = tile_of(n)
                            pe.wait_ge(kept, 2 * (n + 1))
                            if n >= 2:
                                pe.wait_ge(row_kept, n - 1)
                            for k in range(KT):
                                last = pe.matmul(acc[:, n % 2, 0:RV], hT[:, k, m * P:(m + 1) * P], wv[:, k, :],
                                                 start=(k == 0), stop=(k == KT - 1))
                            last.then_inc(row_ready, 1)

                        pe.wait_ge(consts_in, 48)
                        turn(0)
                        for n in range(TILES):
                            if n + 1 < TILES:
                                turn(n + 1)
                            if n == 0:
                                pe.wait_ge(wv_in, 48)
                            row(n)

        class SideProjection:

            def __init__(self, st, kind, tiles):
                self.kind, self.tiles = kind, tiles
                self.units = NBLK * len(tiles)
                self.pieces = KT * self.units
                self.stage = sb("side_stage", [P, 2, 512], st=st)
                self.acc = pb("side_acc", [P, 2, 512], st)
                self.w_in_slot = [sem(f"side_w_in{i}", st) for i in range(2)]
                self.acc_ready, self.sig_ready, self.staged = (sem(n, st) for n in ("side_acc_ready", "side_sig_ready", "side_staged"))
                self.stored = [sem(f"side_stored{i}", st) for i in range(2)]

            def products(self, pe, first, count):
                for p in range(first, min(first + count, self.pieces)):
                    n, k = divmod(p, KT)
                    t, b = divmod(n, NBLK)
                    c0, width = BLOCKS[b]
                    if k == 0:
                        if b == 0:
                            pe.wait_ge(self.w_in_slot[t % 2], 32 * (t // 2 + 1))
                        if n >= 2:
                            pe.wait_ge(self.staged, n - 1)
                    last = pe.matmul(self.acc[:, n % 2, 0:width], wslot[:, t % 2, k, :], hT[:, k, c0:c0 + width],
                                     start=(k == 0), stop=(k == KT - 1))
                    if k == KT - 1:
                        last.then_inc(self.acc_ready, 1)

            def keep(self, act, n):
                width = BLOCKS[n % NBLK][1]
                act.wait_ge(self.acc_ready, n + 1)
                if n >= 2:
                    act.wait_ge(self.stored[n % 2], 16 * (n // 2))
                if self.kind == "copy":
                    act.activation(self.stage[:, n % 2, 0:width], self.acc[:, n % 2, 0:width], ACT.Copy).then_inc(self.staged, 1)
                else:
                    act.activation(self.stage[:, n % 2, 0:width], self.acc[:, n % 2, 0:width], ACT.Sigmoid).then_inc(self.sig_ready, 1)

            def gate(self, dve, n):
                width = BLOCKS[n % NBLK][1]
                dve.wait_ge(self.sig_ready, n + 1)
                dve.tensor_tensor(self.stage[:, n % 2, 0:width], self.acc[:, n % 2, 0:width], self.stage[:, n % 2, 0:width],
                                  ALU.mult).then_inc(self.staged, 1)

            def transfers(self, sp, between=None):
                def load(t):
                    at, segs = 0, self.tiles[t][0]
                    if t >= 2:
                        sp.wait_ge(self.acc_ready, NBLK * (t - 1))
                    for c0, width in segs:
                        sp.dma_start(wslot[:, t % 2, :, at:at + width], w_in[:, :, c0:c0 + width]).then_inc(self.w_in_slot[t % 2], 32 // len(segs))
                        at += width

                load(0)
                load(1)
                for n in range(self.units):
                    t, b = divmod(n, NBLK)
                    c0, width = BLOCKS[b]
                    sp.wait_ge(self.staged, n + 1)
                    sp.dma_start(self.tiles[t][1][:, c0:c0 + width], self.stage[:, n % 2, 0:width]).then_inc(self.stored[n % 2], 16)
                    if b == NBLK - 1 and t + 2 < len(self.tiles):
                        load(t + 2)
                    if between:
                        between(n)
                for i in range(2):
                    sp.wait_ge(self.stored[i], 16 * ((self.units + 1 - i) // 2))

        def conv_and_gates(cx):
            NC = 6
            with ExitStack() as st:
                y = sb("y", [P, 2, T], st=st)
                sq = sb("sq", [P, NBLK, 512], st=st)
                rn = sb("rn", [P, NBLK, 512], st=st)
                taps = sb("taps", [P, NC, 4], st=st)
                hist = sb("hist", [P, NC, 3 + NSAMP], st=st)
                tails = sb("tails", [P, NC, 2, 3], st=st)
                heads4 = sb("heads4", [P, 2, 4], st=st)
                ga = sb("ga", [P, 4, TILES, 4], st=st)
                ea = sb("ea", [P, 4], st=st)
                acc = pb("acc", [P, NBLK, 512], st)
                ss = pb("ss", [P, 2, 512], st)
                W4 = 4 * TILES
                gsum = pb("gsum", [P, 4, P], st)
                names = ("small_in copied tap sample_tap scaled conv_done sig_done silu_done gate_v gate_s sums out_done s0_in "
                         "acc_ready raw_kept sq_done ss_ready ln_done rn_done normed tail_kept").split()
                (small_in, copied, tap, sample_tap, scaled, conv_done, sig_done, silu_done, gate_v, gate_s, sums, out_done, s0_in,
                 acc_ready, raw_kept, sq_done, ss_ready, ln_done, rn_done, normed, tail_kept) = (sem(n, st) for n in names)
                w_in_slot = [sem(f"w_in_slot{i}", st) for i in range(2)]
                flat = lambda ap: ap.rearrange("p t h -> p (t h)")
                with nc.Block() as block:
                    @block.sync
                    def _(sp):
                        def load(c):
                            if c >= 2:
                                sp.wait_ge(acc_ready, NBLK * (c - 1))
                            sp.dma_start(wslot[:, c % 2], w_in[:, :, XC + c * P:XC + (c + 1) * P]).then_inc(w_in_slot[c % 2], 16)

                        load(0)
                        load(1)
                        for w in range(4):
                            sp.dma_start(taps[:, :, w], io["conv_c"][0, w].rearrange("(t p) -> p t", p=P)).then_inc(small_in, 16)
                        for w in range(3):
                            sp.dma_start(hist[:, :, w], io["state_c_conv"][0, 0, w].rearrange("(t p) -> p t", p=P)).then_inc(small_in, 16)
                        sp.dma_start(heads4[:, 0, :], io["dt_bias_c"].to_broadcast([P, 4])).then_inc(small_in, 16)
                        sp.dma_start(heads4[:, 1, :], io["a_log_c"].to_broadcast([P, 4])).then_inc(small_in, 16)
                        for par in range(2):
                            sp.dma_start(cx["S"][par * CH:par * CH + CH, 1],
                                         io["state_c_ssm"][0, 0].rearrange("(a b) k v -> b k a v", b=2)[par]).then_inc(s0_in, 16)
                        for c in range(2, NC):
                            load(c)
                        rows = lambda name: io[name][0, 0].rearrange("t h d -> t (h d)")
                        b0 = slice(VAW, VAW + VBW)
                        stores = [(rows("p_b_v")[0:NMETA, :], vrow[PAD:CH, 0, b0]),
                                  (rows("p_b_v")[NMETA:NMETA + CH, :], vrow[CH:P, 0, b0]),
                                  (rows("p_b_v")[NMETA + CH:NMETA + SEQ - SP0, :].rearrange("(t p) n -> p t n", p=P), vrow[:, 1:LAST, b0]),
                                  (rows("p_b_v")[NMETA + SEQ - SP0:NMETA + SEQ, :], vrow[0:SP0, LAST, b0]),
                                  (rows("s_b_v"), vrow[SP0:SP0 + NSAMP, LAST, b0]),
                                  (rows("p_a_v")[0:WIN - SP0, :], vrow[SP0:P, LAST - 1, 0:VAW]),
                                  (rows("p_a_v")[WIN - SP0:WIN, :], vrow[0:SP0, LAST, 0:VAW]),
                                  (rows("s_a_v")[WIN - NSAMP:WIN, :], vrow[SP0:SP0 + NSAMP, LAST, 0:VAW]),
                                  (rows("s_a_v")[0:WIN - NSAMP, :], rows("cache_a_v")[NSAMP:WIN, :]),
                                  (rows("s_a_k")[0:WIN - NSAMP, :], rows("cache_a_k")[NSAMP:WIN, :])]
                        for dst, src in stores:
                            sp.dma_start(dst, src).then_inc(out_done, 16)
                        sp.wait_ge(tail_kept, 2 * NC)
                        for a, name in enumerate(("p_c_conv", "s_c_conv")):
                            for w in range(3):
                                sp.dma_start(io[name][0, 0, w].rearrange("(t p) -> p t", p=P), tails[:, :, a, w]).then_inc(out_done, 16)
                        sp.wait_ge(out_done, 16 * (len(stores) + 6))
                        sp.wait_ge(s0_in, 32)

                    @block.tensor
                    def _(pe):
                        for c in range(NC):
                            pe.wait_ge(w_in_slot[c % 2], 16 * (c // 2 + 1))
                            for b, (c0, w) in enumerate(BLOCKS):
                                if c:
                                    pe.wait_ge(raw_kept, NBLK * (c - 1) + b + 1)
                                for k in range(KT):
                                    last = pe.matmul(acc[:, b, 0:w], wslot[:, c % 2, k, :], hT[:, k, c0:c0 + w],
                                                     start=(k == 0), stop=(k == KT - 1))
                                last.then_inc(acc_ready, 1)
                                if c >= 2:
                                    n = NBLK * (c - 2) + b
                                    pe.wait_ge(sq_done, n + 1)
                                    if n >= 2:
                                        pe.wait_ge(ln_done, n - 1)
                                    pe.matmul(ss[:, n % 2, 0:w], cf[:, C_BLK:C_BLK + P], sq[:, b, 0:w], start=True, stop=True).then_inc(ss_ready, 1)
                            if c == 0:
                                pe.wait_ge(gate_v, 8)
                                for n, c_ in enumerate((C_TRI, C_BLK, C_LO, C_HI)):
                                    last = pe.matmul(gsum[:, n, 0:W4], cf[:, c_:c_ + P], flat(cx["g"]), start=True, stop=True)
                                last.then_inc(sums, 1)

                    @block.scalar
                    def _(act):
                        act.preload_act_table_set(LN_EXP)
                        act.wait_ge(small_in, 144)
                        x, t, u, g = (ga[:, n] for n in range(4))
                        act.activation(ea[:, :], heads4[:, 1, :], ACT.Exp).then_inc(gate_s, 1)
                        act.activation(cx["beta"][:, :, :], vrow[:, :, VAW + VBW + 4:RV], ACT.Exp, scale=-1.0).then_inc(gate_s, 1)
                        act.wait_ge(gate_v, 2)
                        act.activation(t, t, ACT.Exp, scale=-1.0).then_inc(gate_s, 1)
                        act.wait_ge(gate_s, 3)
                        act.activation(t, t, ACT.Ln, bias=one).then_inc(gate_s, 1)

                        def gate_sums():
                            act.wait_ge(gate_v, 10)
                            act.activation(flat(cx["eg"]), gsum[:, 0, 0:W4], ACT.Exp).then_inc(gate_s, 1)
                            act.activation(flat(cx["ekd"]), flat(t), ACT.Exp).then_inc(gate_s, 1)
                            for c in range(2):
                                for par in range(2):
                                    half = slice(par * CH, par * CH + CH)
                                    act.activation(cx["gl"][half, :, c, :],
                                                   gsum[half, 2 + c, 0:W4].rearrange("p (t a b) -> p t a b", a=2, b=2)[:, :, :, par],
                                                   ACT.Exp).then_inc(gate_s, 1)

                        def last_tap(c):
                            act.wait_ge(raw_kept, NBLK * (c + 1))
                            if c >= 2:
                                act.wait_ge(silu_done, c - 1)
                            act.activation(y[:, c % 2, :], reg[:, c, :], ACT.Copy, scale=taps[:, c, 3:4]).then_inc(scaled, 1)

                        def sigmoid(c):
                            act.wait_ge(conv_done, c + 1)
                            act.activation(reg[:, c, :], y[:, c % 2, :], ACT.Sigmoid).then_inc(sig_done, 1)

                        for c in range(NC):
                            for b, (c0, w) in enumerate(BLOCKS):
                                act.wait_ge(acc_ready, NBLK * c + b + 1)
                                act.activation(reg[:, c, c0:c0 + w], acc[:, b, 0:w], ACT.Copy).then_inc(raw_kept, 1)
                                if c and b == 0:
                                    sigmoid(c - 1)
                                if c >= 2:
                                    n = NBLK * (c - 2) + b
                                    act.wait_ge(ss_ready, n + 1)
                                    if n >= NBLK:
                                        act.wait_ge(normed, n - NBLK + 1)
                                    act.activation(rn[:, b, 0:w], ss[:, n % 2, 0:w], ACT.Ln, bias=eps).then_inc(ln_done, 1)
                            last_tap(c)
                            if c == 0:
                                gate_sums()
                            if c >= 2:
                                for b, (c0, w) in enumerate(BLOCKS):
                                    act.wait_ge(ln_done, NBLK * (c - 2) + b + 1)
                                    act.activation(rn[:, b, 0:w], rn[:, b, 0:w], ACT.Exp, scale=-0.5).then_inc(rn_done, 1)
                        sigmoid(NC - 1)

                    @block.gpsimd
                    def _(pool):
                        for c in range(NC):
                            pool.wait_ge(sig_done, c + 1)
                            pool.tensor_tensor(reg[:, c, :], reg[:, c, :], y[:, c % 2, :], ALU.mult).then_inc(silu_done, 1)
                            if c < 4:
                                pool.wait_ge(silu_done, c + 1)
                                for b, (c0, w) in enumerate(BLOCKS):
                                    if c:
                                        pool.wait_ge(ss_ready, NBLK * (c - 1) + b + 1)
                                    r = reg[:, c, c0:c0 + w]
                                    pool.tensor_tensor(sq[:, b, 0:w], r, r, ALU.mult).then_inc(sq_done, 1)

                    @block.vector
                    def _(dve):
                        dve.memset(cx["S"][:, 0], 0.0).then_inc(copied, 1)
                        dve.wait_ge(small_in, 144)
                        x, t, u, g = (ga[:, n] for n in range(4))
                        dve.tensor_tensor(x, vrow[:, :, VAW + VBW:VAW + VBW + 4], wide(heads4[:, 0, :], TILES), ALU.add).then_inc(gate_v, 1)
                        dve.wait_ge(gate_v, 1)
                        dve.scalar_tensor_tensor(out=t, in0=x, scalar=-1.0, in1=x, op0=ALU.mult, op1=ALU.max).then_inc(gate_v, 1)
                        dve.wait_ge(gate_s, 4)
                        dve.scalar_tensor_tensor(out=u, in0=x, scalar=0.0, in1=t, op0=ALU.max, op1=ALU.add).then_inc(gate_v, 1)
                        dve.wait_ge(gate_v, 3)
                        dve.scalar_tensor_tensor(out=g, in0=u, scalar=-1.0, in1=wide(ea[:, :], TILES),
                                                 op0=ALU.mult, op1=ALU.mult).then_inc(gate_v, 1)
                        dve.tensor_scalar(cx["beta"][:, :, :], cx["beta"][:, :, :], 1.0, None, ALU.add).then_inc(gate_v, 1)
                        dve.wait_ge(gate_v, 5)
                        dve.reciprocal(cx["beta"][:, :, :], cx["beta"][:, :, :]).then_inc(gate_v, 1)
                        dve.memset(g[SP0 + NSAMP:P, LAST, :], 0.0).then_inc(gate_v, 1)
                        dve.wait_ge(gate_v, 7)
                        dve.tensor_copy(cx["g"][:, :, :], g).then_inc(gate_v, 1)
                        dve.wait_ge(sums, 1)
                        dve.tensor_scalar(flat(cx["ngc"]), gsum[:, 0, 0:W4], -1.0, None, ALU.mult).then_inc(gate_v, 1)
                        dve.wait_ge(gate_v, 9)
                        dve.tensor_tensor(flat(t), gsum[:, 1, 0:W4], flat(cx["ngc"]), ALU.add).then_inc(gate_v, 1)
                        dve.wait_ge(gate_s, 6)
                        dve.tensor_scalar(flat(cx["neg_eg"]), flat(cx["eg"]), -1.0, None, ALU.mult).then_inc(gate_v, 1)

                        def conv(c):
                            yc = y[:, c % 2, :]
                            dve.wait_ge(raw_kept, NBLK * (c + 1))
                            for a, c0 in enumerate((SROW - 3, SROW + NSAMP - 3)):
                                dve.tensor_copy(tails[:, c, a, :], reg[:, c, c0:c0 + 3]).then_inc(tail_kept, 1)
                            dve.tensor_copy(hist[:, c, 3:3 + NSAMP], reg[:, c, SROW:SROW + NSAMP]).then_inc(copied, 1)
                            dve.wait_ge(scaled, c + 1)
                            for w in range(3):
                                if w:
                                    dve.wait_ge(tap, 3 * c + w)
                                dve.scalar_tensor_tensor(out=yc[:, 3:T], in0=reg[:, c, w:T - 3 + w], scalar=taps[:, c, w:w + 1],
                                                         in1=yc[:, 3:T], op0=ALU.mult, op1=ALU.add).then_inc(tap, 1)
                            dve.wait_ge(tap, 3 * c + 3)
                            dve.wait_ge(copied, c + 2)
                            ys = yc[:, SROW:SROW + NSAMP]
                            dve.tensor_scalar(ys, hist[:, c, 3:3 + NSAMP], taps[:, c, 3:4], None, ALU.mult).then_inc(sample_tap, 1)
                            for w in range(3):
                                dve.wait_ge(sample_tap, 4 * c + w + 1)
                                dve.scalar_tensor_tensor(out=ys, in0=hist[:, c, w:w + NSAMP], scalar=taps[:, c, w:w + 1],
                                                         in1=ys, op0=ALU.mult, op1=ALU.add).then_inc(sample_tap, 1)
                            dve.wait_ge(sample_tap, 4 * c + 4)
                            dve.memset(yc[:, SROW + NSAMP:T], 0.0).then_inc(conv_done, 1)

                        def norm(c):
                            for b, (c0, w) in enumerate(BLOCKS):
                                n = NBLK * c + b
                                dve.wait_ge(rn_done, n + 1)
                                r = reg[:, c, c0:c0 + w]
                                dve.scalar_tensor_tensor(out=r, in0=r, scalar=SCALE if c < 2 else 1.0, in1=rn[:, b, 0:w],
                                                         op0=ALU.mult, op1=ALU.mult).then_inc(normed, 1)

                        for c in range(NC):
                            conv(c)
                            if c >= 2:
                                norm(c - 2)

        def delta_net(cx, side_tiles):
            with ExitStack() as st:
                tg = sb("tg", [P, 4, P], st=st)
                dec = sb("dec", [P, 4, P], st=st)
                at = sb("at", [P, 4, P], st=st)
                atl = sb("atl", [P, LEVELS, 4, P], st=st)
                qk = sb("qk", [P, 2, 4, P], st=st)
                xm = sb("xm", [P, 4, P], st=st)
                xt = sb("xt", [P, 2, 4, P], st=st)
                ym = sb("ym", [P, 4, P], st=st)
                kd = sb("kd", [P, 2, 4, HD], st=st)
                vr = sb("vr", [P, 2, 4, HD], st=st)
                rr = sb("rr", [P, 4, HD], st=st)
                vn = sb("vn", [P, 4, HD], st=st)
                oo = sb("oo", [P, 4, HD], st=st)
                osq = sb("osq", [P, 4, HD], st=st)
                oss, oln, ors = (sb(n, [P, 4], st=st) for n in ("oss", "oln", "ors"))
                onorm = sb("onorm", [P, HD], st=st)
                b_dr = pb("b_dr", [P, 4, P], st)
                b_kq = pb("b_kq", [P, 2, 2, 2, P], st)
                b_lv = b_kq[:, 0].rearrange("p a q i -> p (a q) i")
                b_lt = b_kq[:, 1].rearrange("p a q i -> p (a q) i")
                b_s = pb("b_s", [P, 2, 512], st)
                b_ds = b_s[:, 0, 4 * HD:6 * HD]
                b_ot = b_s[:, 1, 4 * HD:8 * HD]
                b_vn = pb("b_vn", [P, 2, 4, HD], st)
                side = SideProjection(st, "copy", side_tiles)
                names = ("tg_ready dec_ready dec_done rows_ready v_kept rows_kept kq_ready at_ready qk_ready kd_ready level "
                         "xt0_ready x_turned x_kept y_ready y_kept z_ready x_new ks_ready r_ready vn_ready vn_kept "
                         "ds_ready state_ready o_ready o_sum o_squared o_rss o_ln o_rstd o_scaled o_normed ot_ready ot_kept "
                         "onorm_in out_done o_part").split()
                (tg_ready, dec_ready, dec_done, rows_ready, v_kept, rows_kept, kq_ready, at_ready, qk_ready, kd_ready, level,
                 xt0_ready, x_turned, x_kept, y_ready, y_kept, z_ready, x_new, ks_ready, r_ready, vn_ready, vn_kept,
                 ds_ready, state_ready, o_ready, o_sum, o_squared, o_rss, o_ln, o_rstd, o_scaled, o_normed, ot_ready, ot_kept,
                 onorm_in, out_done, o_part) = (sem(n, st) for n in names)
                lvl = lambda l: cf[:, C_LVL + l * P:C_LVL + (l + 1) * P]
                cols = lambda m: slice(m * P, (m + 1) * P)
                NL = LEVELS - 1
                
                S = cx["S"]
                POINTS = [4, 2, 1, 1] + [2, 2, 1] * 4 + [1]
                FIRST = [[m * sum(POINTS) + sum(POINTS[:p]) for p in range(len(POINTS))] for m in range(TILES)]
                assert TILES * sum(POINTS) >= side.pieces
                SWAPS = [max(5 * NBLK + 3, sum(POINTS) * (4 * b + 6) // KT) for b in range(SWAPPED)]
                spilled, swapped = [sem(f"spilled{b}", st) for b in range(SWAPPED)], sem("swapped", st)

                def state(c):
                    return S[:, 1] if c == 2 * TILES - 1 else S[:, 0]

                with nc.Block() as block:
                    @block.sync
                    def _(sp):
                        def swap(n):
                            for b, at_unit in enumerate(SWAPS):
                                c0, w = BLOCKS[b]
                                if n == at_unit:
                                    sp.wait_ge(ot_kept, 4 * (b + 1))
                                    for i in range(2):
                                        sp.wait_ge(side.stored[i], 16 * ((5 * NBLK + 1 - i) // 2))
                                    sp.dma_start(mix[6:8, :, c0:c0 + w].rearrange("k p t -> p k t"), reg[:, 0:2, c0:c0 + w]).then_inc(spilled[b], 16)
                                    sp.dma_start(reg[:, 2:5, c0:c0 + w], uT[2:5, :, c0:c0 + w].rearrange("k p t -> p k t")).then_inc(swapped, 16)
                                elif n == at_unit + 3:
                                    sp.wait_ge(spilled[b], 16)
                                    sp.dma_start(reg[:, 0:2, c0:c0 + w], uT[0:2, :, c0:c0 + w].rearrange("k p t -> p k t")).then_inc(swapped, 16)

                        side.transfers(sp, swap)
                        sp.wait_ge(swapped, 32 * SWAPPED)

                    @block.gpsimd
                    def _(pool):
                        def triangle_gates(m):
                            if m:
                                pool.wait_ge(dec_ready, m)
                            pool.tensor_tensor(tg[:, :, :], wide(cf[:, C_TRI:C_TRI + P], 4),
                                               cx["g"][:, m, :].unsqueeze(2).to_broadcast([P, 4, P]), ALU.mult).then_inc(tg_ready, 1)

                        pool.dma_start(onorm[:, :], io["onorm_c"].to_broadcast([P, HD])).then_inc(onorm_in, 16)
                        triangle_gates(0)
                        for m in range(TILES + 1):
                            if m < TILES:
                                pool.wait_ge(at_ready, 4 * m + 4)
                                for l in range(LEVELS):
                                    if m and l:
                                        pool.wait_ge(y_ready, NL * (m - 1) + l)
                                    elif m:
                                        pool.wait_ge(xt0_ready, m)
                                    pool.tensor_tensor(atl[:, l], at[:, :, :], wide(lvl(l), 4), ALU.mult).then_inc(level, 1)
                                if m + 1 < TILES:
                                    triangle_gates(m + 1)
                            if m:
                                pool.wait_ge(o_rstd, m)
                                pool.tensor_tensor(osq[:, :, :], oo[:, :, :], ors[:, :].unsqueeze(2).to_broadcast([P, 4, HD]),
                                                   ALU.mult).then_inc(o_scaled, 1)
                                if m == 1:
                                    pool.wait_ge(onorm_in, 16)
                                else:
                                    pool.wait_ge(ot_ready, m - 1)
                                pool.wait_ge(o_scaled, m)
                                pool.tensor_tensor(oo[:, :, :], osq[:, :, :], wide(onorm[:, :], 4), ALU.mult).then_inc(o_normed, 1)
                        for a, name in enumerate(("p_c_ssm", "s_c_ssm")):
                            pool.wait_ge(state_ready, 2 * (2 * TILES - 1) + 2 * a)
                            for par in range(2):
                                pool.dma_start(io[name][0, 0].rearrange("(a b) k v -> b k a v", b=2)[par],
                                               S[par * CH:par * CH + CH, a]).then_inc(out_done, 16)
                        pool.wait_ge(out_done, 64)

                    @block.tensor
                    def _(pe):
                        def decay(m):
                            pe.wait_ge(tg_ready, m + 1)
                            if m:
                                pe.wait_ge(rows_kept, m)
                            pe.matmul(b_dr[:, :, :], identb, wide(cb[:, M_DT:M_DT + P], 4), start=True, stop=False)
                            pe.matmul(b_dr[:, :, :], cf[:, C_BLK:C_BLK + P], tg[:, :, :], start=False, stop=True).then_inc(dec_ready, 1)

                        def rows(m):
                            pe.wait_ge(dec_done, 4 * m + 4)
                            for a in range(4):
                                last = pe.transpose(b_dr[:, a, :], reg[:, 2 + a, cols(m)], ident)
                            last.then_inc(rows_ready, 1)

                        def kq(m):
                            if m:
                                pe.wait_ge(x_new, NL * m)
                            for h in range(4):
                                half = slice((h % 2) * CH, (h % 2) * CH + CH)
                                last = pe.matmul(b_kq[:, h % 2, h // 2], reg[half, 2 + h // 2, cols(m)],
                                                 reg[half, h // 2:h // 2 + 3:2, cols(m)], start=True, stop=True)
                            last.then_inc(kq_ready, 1)

                        def turn_x(m, l):
                            if l == 1:
                                pe.wait_ge(xt0_ready, m + 1)
                                pe.wait_ge(at_ready, 4 * m + 4)
                                pe.wait_ge(qk_ready, 2 * m + 2)
                            else:
                                pe.wait_ge(x_new, NL * m + l - 1)
                            for h in range(4):
                                last = pe.transpose(b_lv[:, h, :], xt[:, m % 2, h], ident)
                            last.then_inc(x_turned, 1)

                        def level_y(m, l):
                            pe.wait_ge(x_kept, NL * m + l)
                            pe.wait_ge(level, LEVELS * m + l + 1)
                            for h in range(4):
                                last = pe.matmul(b_lv[:, h, :], atl[:, l, h], xm[:, h], start=True, stop=True)
                            last.then_inc(y_ready, 1)

                        def level_z(m, l):
                            pe.wait_ge(y_kept, NL * m + l)
                            for h in range(4):
                                last = pe.matmul(b_lt[:, h, :], ym[:, h], xt[:, m % 2, h], start=True, stop=True)
                            last.then_inc(z_ready, 1)

                        def read_state(c):
                            m, at0 = c // 2, (c % 2) * CH
                            if c:
                                pe.wait_ge(state_ready, 2 * c)
                            if c >= 2 and c % 2 == 0:
                                pe.wait_ge(o_part, 2 * m)
                                pe.wait_ge(ot_kept, m)
                            tok = slice(m * P + at0, m * P + at0 + CH)
                            for h in range(4):
                                half = slice((h % 2) * CH, (h % 2) * CH + CH)
                                for a in range(2):
                                    o = a * 2 * HD + (h // 2) * HD
                                    last = pe.matmul(b_s[at0:at0 + CH, h % 2, o:o + HD], reg[half, 2 * a + h // 2, tok],
                                                     state(c)[half, h // 2], start=True, stop=True)
                            last.then_inc(ks_ready, 1)

                        def new_values(c):
                            m, at0 = c // 2, (c % 2) * CH
                            pe.wait_ge(r_ready, 4 * c + 4)
                            if c:
                                pe.wait_ge(vn_kept, c)
                            if m and c == 2 * m:
                                pe.wait_ge(o_sum, m)
                            half = slice(at0, at0 + CH)
                            for h in range(4):
                                last = pe.matmul(b_vn[half, 0, h], xt[half, m % 2, h, half], rr[half, h], start=True, stop=True)
                            last.then_inc(vn_ready, 1)

                        def update_state(c):
                            m, at0 = c // 2, (c % 2) * CH
                            half = slice(at0, at0 + CH)
                            pe.wait_ge(vn_kept, c + 1)
                            for h in range(4):
                                o = (h // 2) * HD
                                last = pe.matmul(b_ds[(h % 2) * CH:(h % 2) * CH + CH, o:o + HD], kd[half, m % 2, h], vn[half, h],
                                                 start=True, stop=True)
                            last.then_inc(ds_ready, 1)

                        def outputs(m):
                            pe.wait_ge(vn_kept, 2 * m + 2)
                            for h in range(4):
                                last = pe.matmul(b_vn[:, 1, h], qk[:, m % 2, h], vn[:, h], start=True, stop=True)
                            last.then_inc(o_ready, 1)

                        def outputs_transposed(m):
                            pe.wait_ge(o_normed, m + 1)
                            for a in range(2):
                                last = pe.transpose(b_ot[:, a * P:(a + 1) * P],
                                                    oo[:, 2 * a:2 * a + 2, :].rearrange("p h v -> p (h v)"), ident)
                            last.then_inc(ot_ready, 1)

                        def beside(m, point):
                            side.products(pe, FIRST[m][point], POINTS[point])

                        for m in range(TILES + 1):
                            new, old = m < TILES, m > 0
                            c = 2 * (m - 1)

                            def invert(l, after_turn=None, after_y=None, after_z=None):
                                if new:
                                    beside(m, 3 * l - 2)
                                    turn_x(m, l)
                                if old and after_turn:
                                    after_turn()
                                if new:
                                    beside(m, 3 * l - 1)
                                    level_y(m, l)
                                    beside(m, 3 * l)
                                if old and after_y:
                                    after_y()
                                if new:
                                    level_z(m, l)
                                if old and after_z:
                                    after_z()

                            if new:
                                decay(m)
                                kq(m)
                                beside(m, 0)
                                rows(m)
                            if old:
                                read_state(c)
                            invert(1, lambda: new_values(c), lambda: update_state(c), lambda: read_state(c + 1))
                            invert(2, None, lambda: new_values(c + 1), lambda: update_state(c + 1))
                            invert(3, None, lambda: outputs(m - 1))
                            invert(4, None, None, lambda: outputs_transposed(m - 1))
                            invert(5)
                            if new:
                                beside(m, 16)

                    @block.scalar
                    def _(act):
                        def keep_y(m, l):
                            keep_beside(m, (3 * l - 2,))
                            act.wait_ge(x_turned, NL * m + l)
                            act.activation(xm[:, :, :], b_lv, ACT.Copy).then_inc(x_kept, 1)
                            keep_beside(m, (3 * l - 1,))
                            act.wait_ge(y_ready, NL * m + l)
                            act.activation(ym[:, :, :], b_lv[:, :, :], ACT.Copy).then_inc(y_kept, 1)
                            keep_beside(m, (3 * l,))

                        def keep_beside(m, points):
                            for p in points:
                                for n in range(FIRST[m][p] // KT, min((FIRST[m][p] + POINTS[p]) // KT, side.units)):
                                    side.keep(act, n)

                        act.preload_act_table_set(LN_EXP)
                        for m in range(TILES + 1):
                            if m < TILES:
                                act.wait_ge(dec_ready, m + 1)
                                if m:
                                    act.wait_ge(at_ready, 4 * m)
                                    act.wait_ge(qk_ready, 2 * m)
                                for h in range(4):
                                    act.activation(dec[:, h, :], b_dr[:, h, :], ACT.Exp, bias=cx["ngc"][:, m, h:h + 1]).then_inc(dec_done, 1)
                                act.wait_ge(rows_ready, m + 1)
                                if m >= 2:
                                    act.wait_ge(r_ready, 8 * (m - 1))
                                act.activation(vr[:, m % 2], b_dr[:, 2:4, :].rearrange("p a (b v) -> p (a b) v", b=2), ACT.Copy).then_inc(v_kept, 1)
                                keep_beside(m, (0,))
                                for l in range(1, 5):
                                    keep_y(m, l)
                            if m:
                                act.wait_ge(o_rss, m)
                                act.activation(oln[:, :], oss[:, :], ACT.Ln, bias=eps, scale=1.0 / HD).then_inc(o_ln, 1)
                                act.wait_ge(o_ln, m)
                                act.activation(ors[:, :], oln[:, :], ACT.Exp, scale=-0.5).then_inc(o_rstd, 1)
                            if m < TILES:
                                keep_y(m, 5)
                            if m:
                                act.wait_ge(ot_ready, m)
                                act.activation(reg[:, 0:2, cols(m - 1)], b_ot.rearrange("p (a t) -> p a t", a=2),
                                               ACT.Copy).then_inc(ot_kept, 1)
                            if m < TILES:
                                keep_beside(m, (16,))

                    @block.vector
                    def _(dve):
                        def products(m):
                            dve.wait_ge(kq_ready, m + 1)
                            dve.wait_ge(dec_done, 4 * m + 4)
                            if m:
                                dve.wait_ge(level, LEVELS * m)
                            for h in range(4):
                                dve.scalar_tensor_tensor(out=at[:, h, :], in0=b_kq[:, h % 2, h // 2, 1], scalar=cx["beta"][:, m, h:h + 1],
                                                         in1=dec[:, h, :], op0=ALU.mult, op1=ALU.mult).then_inc(at_ready, 1)
                            if m >= 2:
                                dve.wait_ge(o_ready, m - 1)
                            for b in range(2):
                                dve.tensor_tensor(qk[:, m % 2, b::2, :], b_kq[:, b, :, 0, :], dec[:, b::2, :], ALU.mult).then_inc(qk_ready, 1)
                            dve.wait_ge(v_kept, m + 1)
                            if m >= 2:
                                dve.wait_ge(ds_ready, 2 * (m - 1))
                            dve.tensor_tensor(kd[:, m % 2], b_dr[:, 0:2, :].rearrange("p a (b v) -> p (a b) v", b=2),
                                              cx["ekd"][:, m, :].unsqueeze(2).to_broadcast([P, 4, HD]), ALU.mult).then_inc(rows_kept, 1)

                        def first_inverse(m):
                            dve.wait_ge(level, LEVELS * m + 1)
                            if m >= 2:
                                dve.wait_ge(vn_ready, 2 * (m - 1))
                            dve.tensor_tensor(xt[:, m % 2], wide(ident, 4), atl[:, 0], ALU.subtract).then_inc(xt0_ready, 1)

                        def level_sub(m, l):
                            dve.wait_ge(z_ready, NL * m + l)
                            dve.tensor_tensor(xt[:, m % 2], xt[:, m % 2], b_lt, ALU.subtract).then_inc(x_new, 1)

                        def residual(c):
                            m, at0 = c // 2, (c % 2) * CH
                            half = slice(at0, at0 + CH)
                            dve.wait_ge(ks_ready, c + 1)
                            dve.wait_ge(rows_kept, m + 1)
                            if c:
                                dve.wait_ge(vn_ready, c)
                            for h in range(4):
                                o = 2 * HD + (h // 2) * HD
                                dve.scalar_tensor_tensor(out=rr[half, h], in0=b_s[half, h % 2, o:o + HD], scalar=cx["neg_eg"][half, m, h:h + 1],
                                                         in1=vr[half, m % 2, h], op0=ALU.mult, op1=ALU.add).then_inc(r_ready, 1)

                        def values(c):
                            m, at0 = c // 2, (c % 2) * CH
                            half = slice(at0, at0 + CH)
                            dve.wait_ge(vn_ready, c + 1)
                            if c >= 2 and c % 2 == 0:
                                dve.wait_ge(o_ready, m)
                            dve.tensor_tensor(vn[half], b_vn[half, 0], cx["beta"][half, m, :].unsqueeze(2).to_broadcast([CH, 4, HD]),
                                              ALU.mult).then_inc(vn_kept, 1)

                        def new_state(c):
                            dve.wait_ge(ds_ready, c + 1)
                            for a in range(2):
                                s_ = state(c)[:, a]
                                dve.scalar_tensor_tensor(out=s_, in0=s_, scalar=cx["gl"][:, c // 2, c % 2, a:a + 1],
                                                         in1=b_ds[:, a * HD:(a + 1) * HD], op0=ALU.mult, op1=ALU.add).then_inc(state_ready, 1)

                        def finish(m):
                            dve.wait_ge(o_ready, m + 1)
                            if m:
                                dve.wait_ge(ot_ready, m)
                            for b in range(2):
                                dve.tensor_tensor(oo[:, b::2, :], b_s[:, b, 0:2 * HD].rearrange("p (a v) -> p a v", a=2),
                                                  cx["eg"][:, m, b::2].unsqueeze(2).to_broadcast([P, 2, HD]), ALU.mult).then_inc(o_part, 1)
                            dve.wait_ge(o_part, 2 * m + 2)
                            dve.tensor_tensor(oo[:, :, :], oo[:, :, :], b_vn[:, 1], ALU.add).then_inc(o_sum, 1)
                            dve.wait_ge(o_sum, m + 1)
                            dve.tensor_tensor(osq[:, :, :], oo[:, :, :], oo[:, :, :], ALU.mult).then_inc(o_squared, 1)
                            dve.wait_ge(o_squared, m + 1)
                            dve.tensor_reduce(oss[:, :], osq[:, :, :], AX.X, ALU.add).then_inc(o_rss, 1)

                        for m in range(TILES + 1):
                            new, old = m < TILES, m > 0
                            c = 2 * (m - 1)
                            if new:
                                products(m)
                            if old:
                                residual(c)
                            if new:
                                first_inverse(m)
                            if old:
                                values(c)
                                new_state(c)
                            if new:
                                level_sub(m, 1)
                            if old:
                                residual(c + 1)
                                values(c + 1)
                            if new:
                                level_sub(m, 2)
                            if old:
                                new_state(c + 1)
                            if new:
                                level_sub(m, 3)
                            if old:
                                finish(m - 1)
                            if new:
                                level_sub(m, 4)
                                level_sub(m, 5)

        def a_key_stores(m):
            pk = io["p_a_k"][0, 0].rearrange("t h d -> t (h d)")
            sk = io["s_a_k"][0, 0].rearrange("t h d -> t (h d)")
            if m == LAST - 1:
                return [(pk[0:WIN - SP0, :], slice(SP0, P))]
            return [(pk[WIN - SP0:WIN, :], slice(0, SP0)), (sk[WIN - NSAMP:WIN, :], slice(SP0, SP0 + NSAMP))]

        def b_key_stores(m):
            pk = io["p_b_k"][0, 0].rearrange("t h d -> t (h d)")
            sk = io["s_b_k"][0, 0].rearrange("t h d -> t (h d)")
            if m == 0:
                return [(pk[0:P - PAD, :], slice(PAD, P))]
            if m == LAST:
                return [(pk[m * P - PAD:m * P - PAD + SP0, :], slice(0, SP0)), (sk, slice(SP0, SP0 + NSAMP))]
            return [(pk[m * P - PAD:(m + 1) * P - PAD, :], slice(0, P))]

        def window_attention():
            with ExitStack() as st:
                kc = sb("kc", [P, P], st=st)
                vc = sb("vc", [P, P], st=st)
                kcT = sb("kcT", [P, P], st=st)
                nsink = sb("nsink", [P, AH], st=st)
                sink = sb("sink", [P, AH], st=st)
                krow = sb("krow", [P, 2, P], st=st)
                pr = sb("pr", [P, 2, AG, 2 * P], st=st)
                pt = sb("pt", [P, 2, 2, AG, P], st=st)
                mx, nm, den, se, rd = (sb(n, [P, 2, AG], st=st) for n in ("mx", "nm", "den", "se", "rd"))
                b_sc = pb("b_sc", [P, 2, AG, 2 * P], st)
                b_pt = pb("b_pt", [P, 2, AG, P], st)
                b_o = pb("b_o", [P, 2, AG, P], st)
                names = ("cache_in sink_in turned kct_kept nsink_ready scores_ready max_ready bias_ready exp_done sink_biased sink_exp "
                         "den_ready recip_ready normed pt_ready pt_kept_act pt_kept_dve o_ready o_kept "
                         "swapped krow_turned krow_kept krow_out").split()
                (cache_in, sink_in, turned, kct_kept, nsink_ready, scores_ready, max_ready, bias_ready, exp_done, sink_biased, sink_exp,
                 den_ready, recip_ready, normed, pt_ready, pt_kept_act, pt_kept_dve, o_ready, o_kept,
                 swapped, krow_turned, krow_kept, krow_out) = (sem(n, st) for n in names)
                spilled = [sem(f"spilled{b}", st) for b in range(NBLK)]
                qk_in = [sem(f"qk_in{b}", st) for b in range(NBLK)]
                vA = vrow
                units = [(m, j) for m in range(TILES + 1) for j in range(AKV)]
                N = len(units)

                def keys(m):
                    return P if m == 0 else (WIN + NSAMP if m == TILES else 2 * P)

                def rows_of(m):
                    return NSAMP if m == TILES else P

                def key_tiles(m, j):
                    d = slice(j * HD, (j + 1) * HD)
                    if m == 0:
                        return [(vA[:, 0, d], slice(0, P), 0)]
                    if m == TILES:
                        new = slice(SP0, SP0 + NSAMP)
                        return [(vc[:, d], slice(0, P), 0), (vA[new, LAST, d], new, WIN)]
                    return [(vA[:, m - 1, d], slice(0, P), 0), (vA[:, m, d], slice(0, P), P)]

                with nc.Block() as block:
                    @block.sync
                    def _(sp):
                        sp.dma_start(kc[:, :], io["cache_a_k"][0, 0].rearrange("t h d -> t (h d)")).then_inc(cache_in, 16)
                        sp.dma_start(vc[:, :], io["cache_a_v"][0, 0].rearrange("t h d -> t (h d)")).then_inc(cache_in, 16)
                        sp.dma_start(sink[:, :], io["sinks_a"].to_broadcast([P, AH])).then_inc(sink_in, 16)
                        for b in range(SWAPPED, NBLK):
                            c0, w = BLOCKS[b]
                            sp.dma_start(mix[6:8, :, c0:c0 + w].rearrange("k p t -> p k t"), reg[:, 0:2, c0:c0 + w]).then_inc(spilled[b], 16)
                            sp.dma_start(reg[:, 2:5, c0:c0 + w], uT[2:5, :, c0:c0 + w].rearrange("k p t -> p k t")).then_inc(qk_in[b], 16)
                        for b in range(SWAPPED, NBLK):
                            c0, w = BLOCKS[b]
                            sp.wait_ge(spilled[b], 16)
                            sp.dma_start(reg[:, 0:2, c0:c0 + w], uT[0:2, :, c0:c0 + w].rearrange("k p t -> p k t")).then_inc(qk_in[b], 16)
                        for b in range(SWAPPED):
                            c0, w = BLOCKS[b]
                            sp.wait_ge(o_kept, 4 * b + 5)
                            sp.dma_start(mix[0:4, :, c0:c0 + w].rearrange("k p t -> p k t"), reg[:, 0:4, c0:c0 + w]).then_inc(spilled[b], 16)
                            sp.dma_start(reg[:, 4:6, c0:c0 + w], uT[7:9, :, c0:c0 + w].rearrange("k p t -> p k t")).then_inc(swapped, 16)
                            sp.wait_ge(spilled[b], 16)
                            sp.dma_start(reg[:, 0:2, c0:c0 + w], uT[5:7, :, c0:c0 + w].rearrange("k p t -> p k t")).then_inc(swapped, 16)
                        sp.wait_ge(swapped, 32 * SWAPPED)
                        sp.wait_ge(krow_kept, 1)
                        for n, m in enumerate((LAST - 1, LAST)):
                            for dst, part in a_key_stores(m):
                                sp.dma_start(dst, krow[part, n, :]).then_inc(krow_out, 16)
                        sp.wait_ge(krow_out, 48)

                    @block.tensor
                    def _(pe):
                        def scores(n):
                            m, j = units[n]
                            R, K = rows_of(m), keys(m)
                            if j == 0 and m % 4 == 0 and SWAPPED <= m // 4 < NBLK:
                                pe.wait_ge(qk_in[m // 4], 32)
                            if n >= 2:
                                pe.wait_ge(exp_done, AG * (n - 1))
                            half = slice(j * CH, (j + 1) * CH)
                            q0 = SROW if m == TILES else m * P
                            for a in range(0, AG, 2):
                                if m < TILES:
                                    at = M_A0 if m == 0 else (M_A1 if m == 1 else M_A)
                                    pe.matmul(b_sc[:, n % 2, a:a + 2, 0:K], identb, wide(cb[:, at:at + K], 2), start=True, stop=False,
                                              skip_group_check=True)
                            for g in range(AG):
                                qh = reg[half, g, q0:q0 + R]
                                if m < TILES:
                                    k0 = max(m - 1, 0) * P
                                    last = pe.matmul(b_sc[0:R, n % 2, g, 0:K], qh, reg[half, 4, k0:k0 + K], start=False, stop=True,
                                                     skip_group_check=True)
                                else:
                                    pe.matmul(b_sc[0:R, n % 2, g, 0:WIN], qh, kcT[half, :], start=True, stop=True)
                                    last = pe.matmul(b_sc[0:R, n % 2, g, WIN:K], qh, reg[half, 4, SROW:SROW + NSAMP], start=True, stop=True)
                            last.then_inc(scores_ready, 1)

                        def turn(n):
                            m, j = units[n]
                            R = rows_of(m)
                            pe.wait_ge(normed, AG * (n + 1))
                            if n:
                                pe.wait_ge(pt_kept_act, n)
                                pe.wait_ge(pt_kept_dve, n)
                            for t, (_, part, k0) in enumerate(key_tiles(m, j)):
                                kn = part.stop - part.start
                                for g in range(AG):
                                    last = pe.transpose(b_pt[0:kn, t, g, 0:R], pr[0:R, n % 2, g, k0:k0 + kn], ident[0:R, 0:R])
                            last.then_inc(pt_ready, 1)

                        def values(n):
                            m, j = units[n]
                            R = rows_of(m)
                            pe.wait_ge(pt_kept_act, n + 1)
                            pe.wait_ge(pt_kept_dve, n + 1)
                            if n >= 4 and j == 0:
                                pe.wait_ge(o_kept, n // 2 - 1)
                            tiles_ = key_tiles(m, j)
                            for t, (v, part, k0) in enumerate(tiles_):
                                last = pe.matmul(b_o[j * CH:(j + 1) * CH, m % 2, :, 0:R], v, pt[part, n % 2, t, :, 0:R],
                                                 start=(t == 0), stop=(t == len(tiles_) - 1))
                            last.then_inc(o_ready, 1)

                        for n in range(N + 3):
                            if n < N:
                                scores(n)
                            if n == 1:
                                pe.wait_ge(cache_in, 32)
                                pe.transpose(b_pt[:, 0, 0, :], kc[:, :], ident).then_inc(turned, 1)
                            if n == 2:
                                pe.wait_ge(kct_kept, 1)
                            if 2 <= n < N + 2:
                                turn(n - 2)
                            if n >= 3:
                                values(n - 3)
                        for n, m in enumerate((LAST - 1, LAST)):
                            last = pe.transpose(b_pt[:, 0, n, :], reg[:, 4, m * P:(m + 1) * P], ident)
                        last.then_inc(krow_turned, 1)

                    @block.scalar
                    def _(act):
                        def exps(n):
                            m, j = units[n]
                            R, K = rows_of(m), keys(m)
                            act.wait_ge(bias_ready, n + 1)
                            if n >= 2:
                                act.wait_ge(pt_ready, n - 1)
                            for g in range(AG):
                                act.activation(pr[0:R, n % 2, g, 0:K], b_sc[0:R, n % 2, g, 0:K], ACT.Exp, bias=nm[0:R, n % 2, g:g + 1],
                                               scale=SCALE, accum_out=den[0:R, n % 2, g:g + 1]).then_inc(exp_done, 1)
                            act.wait_ge(sink_biased, n + 1)
                            act.activation(se[0:R, n % 2, :], se[0:R, n % 2, :], ACT.Exp).then_inc(sink_exp, 1)

                        def keep(n):
                            m, j = units[n]
                            R = rows_of(m)
                            act.wait_ge(pt_ready, n + 1)
                            if n >= 2:
                                act.wait_ge(o_ready, n - 1)
                            act.activation(pt[:, n % 2, 0, :, 0:R], b_pt[:, 0, :, 0:R], ACT.Copy).then_inc(pt_kept_act, 1)

                        for n in range(N + 2):
                            if n < N:
                                exps(n)
                            if n >= 2:
                                keep(n - 2)

                    @block.vector
                    def _(dve):
                        dve.wait_ge(sink_in, 16)
                        dve.tensor_scalar(nsink[:, :], sink[:, :], -1.0, None, ALU.mult).then_inc(nsink_ready, 1)
                        dve.wait_ge(nsink_ready, 1)

                        def bias(n):
                            m, j = units[n]
                            R, K = rows_of(m), keys(m)
                            hs = slice(j * AG, (j + 1) * AG)
                            dve.wait_ge(scores_ready, n + 1)
                            dve.tensor_reduce(mx[0:R, n % 2, :], b_sc[0:R, n % 2, :, 0:K], AX.X, ALU.max).then_inc(max_ready, 1)
                            dve.wait_ge(max_ready, n + 1)
                            if n >= 2:
                                dve.wait_ge(exp_done, AG * (n - 1))
                            dve.scalar_tensor_tensor(out=nm[0:R, n % 2, :], in0=mx[0:R, n % 2, :], scalar=-SCALE, in1=nsink[0:R, hs],
                                                     op0=ALU.mult, op1=ALU.min).then_inc(bias_ready, 1)
                            dve.wait_ge(bias_ready, n + 1)
                            dve.tensor_tensor(se[0:R, n % 2, :], sink[0:R, hs], nm[0:R, n % 2, :], ALU.add).then_inc(sink_biased, 1)

                        def norm(n):
                            m, j = units[n]
                            R, K = rows_of(m), keys(m)
                            dve.wait_ge(sink_exp, n + 1)
                            dve.wait_ge(exp_done, AG * (n + 1))
                            dve.tensor_tensor(den[0:R, n % 2, :], den[0:R, n % 2, :], se[0:R, n % 2, :], ALU.add).then_inc(den_ready, 1)
                            dve.wait_ge(den_ready, n + 1)
                            dve.reciprocal(rd[0:R, n % 2, :], den[0:R, n % 2, :]).then_inc(recip_ready, 1)
                            dve.wait_ge(recip_ready, n + 1)
                            for g in range(AG):
                                x = pr[0:R, n % 2, g, 0:K]
                                dve.tensor_scalar(x, x, rd[0:R, n % 2, g:g + 1], None, ALU.mult).then_inc(normed, 1)

                        def keep(n):
                            m, j = units[n]
                            R = rows_of(m)
                            dve.wait_ge(pt_ready, n + 1)
                            if n >= 2:
                                dve.wait_ge(o_ready, n - 1)
                            part = key_tiles(m, j)[-1][1]
                            if m == 0:
                                dve.memset(pt[:, n % 2, 1, :, :], 0.0).then_inc(pt_kept_dve, 1)
                            else:
                                dve.tensor_copy(pt[part, n % 2, 1, :, 0:R], b_pt[0:part.stop - part.start, 1, :, 0:R]).then_inc(pt_kept_dve, 1)

                        def keep_out(m):
                            dve.wait_ge(o_ready, 2 * m + 2)
                            q0, cnt = (SROW, NSAMP) if m == TILES else (m * P, SP0 if m == LAST else P)
                            dve.tensor_copy(reg[:, 0:AG, q0:q0 + cnt], b_o[:, m % 2, :, 0:cnt]).then_inc(o_kept, 1)

                        for n in range(N + 4):
                            if n < N:
                                bias(n)
                            if 1 <= n <= N:
                                norm(n - 1)
                            if n == 1:
                                dve.wait_ge(turned, 1)
                                dve.tensor_copy(kcT[:, :], b_pt[:, 0, 0, :]).then_inc(kct_kept, 1)
                            if 2 <= n < N + 2:
                                keep(n - 2)
                            if n >= 4 and n % 2:
                                keep_out((n - 4) // 2)
                        dve.wait_ge(krow_turned, 1)
                        dve.tensor_copy(krow[:, :, :], b_pt[:, 0, 0:2, :]).then_inc(krow_kept, 1)

        def stick_breaking(side_tiles):
            KC = 512
            TAIL = 16
            QS, KS = 0, 4
            with ExitStack() as st:
                kc = sb("kc", [P, 2, VBW], st=st)
                vc = sb("vc", [P, 2, VBW], st=st)
                kcT = sb("kcT", [P, 2, PAST], st=st)
                keepb = sb("keepb", [P, 3, KC], st=st)
                beta = sb("beta", [P, 4, KC], st=st)
                prod = sb("prod", [P, 2, T + 1], st=st)
                wt = sb("wt", [P, 2, 4, P], st=st)
                b_z = pb("b_z", [P, 2, KC], st)
                b_w = pb("b_w", [P, 2, 4, P], st)
                b_o = pb("b_o", [P, 2, 512], st)
                side = SideProjection(st, "silu", side_tiles)
                spilled = [sem(f"spilled{b}", st) for b in range(NBLK)]
                qk_in = [sem(f"qk_in{b}", st) for b in range(NBLK)]
                names = ("cache_in turned kct_kept z_ready keep_ready beta_ready one_ready prod_ready w_ready wt_ready wt_kept o_ready o_kept part_kept wo_in o_stored").split()
                (cache_in, turned, kct_kept, z_ready, keep_ready, beta_ready, one_ready, prod_ready, w_ready, wt_ready, wt_kept, o_ready,
                 o_kept, part_kept, wo_in, o_stored) = (sem(n, st) for n in names)
                new = slice(SP0, SP0 + NSAMP)

                def side_piece(s):
                    return side.pieces * min(s, N - TAIL) // (N - TAIL)

                def side_units(s):
                    return range(side_piece(s) // KT, min(side_piece(s + 1) // KT, side.units))
                steps = []
                for m in range(TILES + 1):
                    for h in range(BH):
                        if m == TILES:
                            steps.append((m, h, 0, PAST + NSAMP, True, True))
                            continue
                        L = (m + 1) * P
                        for k0 in range((L - 1) // KC * KC, -1, -KC):
                            steps.append((m, h, k0, min(KC, L - k0), k0 + KC >= L, k0 == 0))
                N = len(steps)
                rowno = []
                for s_ in steps:
                    rowno.append((rowno[-1] if rowno else -1) + s_[4])
                row_end = [s + 1 for s, s_ in enumerate(steps) if s_[5]]

                GROUPS = -(-TILES // 2)
                krow_turned, krow_kept, krow_out = sem("krow_turned", st), sem("krow_kept", st), [sem(f"krow_out{i}", st) for i in range(2)]
                assert GROUPS <= TAIL

                def key_group(g):
                    return range(2 * g, min(2 * g + 2, TILES))

                def krow_transfers(parity, g):
                    return 16 * sum(len(b_key_stores(m)) for i in range(parity, g, 2) for m in key_group(i))

                def rows_of(m):
                    return NSAMP if m == TILES else P

                def key_tiles(s):
                    m, h, k0, nk = steps[s][:4]
                    d = slice(VAW + h * HD, VAW + (h + 1) * HD)
                    if m == TILES:
                        dc = slice(h * HD, (h + 1) * HD)
                        return [(vc[:, 0, dc], slice(0, P), 0), (vc[:, 1, dc], slice(0, P), P), (vrow[new, LAST, d], new, PAST)]
                    return [(vrow[:, k0 // P + t, d], slice(0, P), t * P) for t in range(nk // P)]

                def keep_weights(eng, s, copy):
                    eng.wait_ge(wt_ready, s + 1)
                    if s >= 2:
                        eng.wait_ge(o_ready, s - 1)
                    if s >= 1:
                        eng.wait_ge(wt_kept, s)
                    R = rows_of(steps[s][0])
                    tiles_ = key_tiles(s)
                    full = [t for t, x in enumerate(tiles_) if x[1].stop - x[1].start == P]
                    if len(full) == len(tiles_):
                        copy(wt[:, s % 2, 0:len(full), 0:R], b_w[:, s % 2, 0:len(full), 0:R]).then_inc(wt_kept, 1)
                    else:
                        copy(wt[:, s % 2, 0:len(full), 0:R], b_w[:, s % 2, 0:len(full), 0:R]).then_inc(part_kept, 1)
                        eng.wait_ge(part_kept, steps[s][1] + 1)
                        copy(wt[new, s % 2, len(full), 0:R], b_w[0:NSAMP, s % 2, len(full), 0:R]).then_inc(wt_kept, 1)

                with nc.Block() as block:
                    @block.sync
                    def _(sp):
                        for name, dst in (("cache_b_k", kc), ("cache_b_v", vc)):
                            sp.dma_start(dst[:, :, :], io[name][0, 0].rearrange("(t p) h d -> p t (h d)", p=P)).then_inc(cache_in, 16)

                        def swap(n):
                            if n % 2 == 0 and SWAPPED <= n // 2 < NBLK:
                                b = n // 2
                                c0, w = BLOCKS[b]
                                sp.dma_start(mix[0:4, :, c0:c0 + w].rearrange("k p t -> p k t"), reg[:, 0:4, c0:c0 + w]).then_inc(spilled[b], 16)
                                sp.dma_start(reg[:, KS:KS + 2, c0:c0 + w], uT[7:9, :, c0:c0 + w].rearrange("k p t -> p k t")).then_inc(qk_in[b], 16)
                                sp.wait_ge(spilled[b], 16)
                                sp.dma_start(reg[:, QS:QS + 2, c0:c0 + w], uT[5:7, :, c0:c0 + w].rearrange("k p t -> p k t")).then_inc(qk_in[b], 16)

                        side.transfers(sp, swap)
                        sp.wait_ge(side.acc_ready, side.units)
                        wo = io["w_out"][0]
                        for g in range(AG):
                            for j in range(AKV):
                                sp.dma_start(hT[j * CH:(j + 1) * CH, g, 0:D], wo[(j * AG + g) * HD:(j * AG + g + 1) * HD, :]).then_inc(wo_in, 16)
                        sp.dma_start(hT[:, AG:KT, 0:D], wo[AH * HD:D, :].rearrange("(k p) n -> p k n", p=P)).then_inc(wo_in, 16)
                        for g in range(GROUPS):
                            sp.wait_ge(krow_kept, g + 1)
                            for m in key_group(g):
                                for dst, part in b_key_stores(m):
                                    sp.dma_start(dst, side.stage[part, g % 2, (m % 2) * VBW:(m % 2 + 1) * VBW]).then_inc(krow_out[g % 2], 16)
                        for i in range(2):
                            sp.wait_ge(krow_out[i], krow_transfers(i, GROUPS))
                        sp.wait_ge(wo_in, 16 * (AH + 1))

                    @block.tensor
                    def _(pe):
                        def scores(s):
                            m, h, k0, nk, first, last_ = steps[s]
                            R = rows_of(m)
                            half = slice((h % 2) * CH, (h % 2) * CH + CH)
                            if first and h == 0 and m % 4 == 0 and SWAPPED <= m // 4 < NBLK:
                                pe.wait_ge(qk_in[m // 4], 32)
                            if s >= 2:
                                pe.wait_ge(keep_ready, s - 1)
                                pe.wait_ge(beta_ready, s - 1)
                            bank = b_z[0:R, s % 2]
                            q0 = SROW if m == TILES else m * P
                            q = reg[half, QS + h // 2, q0:q0 + R]
                            if m == TILES:
                                pe.matmul(bank[:, 0:PAST], q, kcT[half, h // 2, :], start=True, stop=True)
                                last = pe.matmul(bank[:, PAST:nk], q, reg[half, KS + h // 2, SROW:SROW + NSAMP], start=True, stop=False,
                                                 skip_group_check=True)
                                last = pe.matmul(bank[:, PAST:nk], identb[0:R, 0:R], cb[0:R, M_B:M_B + NSAMP], start=False, stop=True,
                                                 skip_group_check=True)
                            else:
                                masks = ([(nk - P, M_B)] if first else []) + ([(0, M_PAD)] if last_ else [])
                                last = pe.matmul(bank[:, 0:nk], q, reg[half, KS + h // 2, k0:k0 + nk], start=True, stop=not masks,
                                                 skip_group_check=True)
                                for n, (at, mask) in enumerate(masks):
                                    last = pe.matmul(bank[:, at:at + P], identb, cb[:, mask:mask + P], start=False,
                                                     stop=(n == len(masks) - 1), skip_group_check=True)
                            last.then_inc(z_ready, 1)

                        def turn(s):
                            R = rows_of(steps[s][0])
                            pe.wait_ge(w_ready, s + 1)
                            if s >= 2:
                                pe.wait_ge(wt_kept, s - 1)
                            for t, (_, part, at) in enumerate(key_tiles(s)):
                                kn = part.stop - part.start
                                last = pe.transpose(b_w[0:kn, s % 2, t, 0:R], beta[0:R, s % 4, at:at + kn], ident[0:R, 0:R])
                            last.then_inc(wt_ready, 1)

                        def values(s):
                            m, h, k0, nk, first, last_ = steps[s]
                            R = rows_of(m)
                            pe.wait_ge(wt_kept, s + 1)
                            row = rowno[s]
                            pair = row // 2
                            if first and h % 2 == 0 and pair >= 2:
                                pe.wait_ge(o_kept, pair - 1)
                            tiles_ = key_tiles(s)
                            for t, (v, part, at) in enumerate(tiles_):
                                last = pe.matmul(b_o[(h % 2) * CH:(h % 2) * CH + CH, pair % 2, 0:R], v, wt[part, s % 2, t, 0:R],
                                                 start=(first and t == 0), stop=(last_ and t == len(tiles_) - 1))
                            last.then_inc(o_ready, 1)

                        def turn_keys(g):
                            if g < 2:
                                pe.wait_ge(side.staged, side.units)
                            else:
                                pe.wait_ge(krow_kept, g - 1)
                            for m in key_group(g):
                                for a in range(2):
                                    at = (m % 2) * VBW + a * P
                                    last = pe.transpose(side.acc[:, g % 2, at:at + P], reg[:, KS + a, m * P:(m + 1) * P], ident)
                            last.then_inc(krow_turned, 1)

                        for s in range(N + 4):
                            if s < N:
                                scores(s)
                                side.products(pe, side_piece(s), side_piece(s + 1) - side_piece(s))
                                if 0 <= s - (N - TAIL) < GROUPS:
                                    turn_keys(s - (N - TAIL))
                            if s == 1:
                                pe.wait_ge(cache_in, 32)
                                for a in range(2):
                                    for t in range(2):
                                        last = pe.transpose(b_w[:, 0, 2 * a + t, :], kc[:, t, a * P:(a + 1) * P], ident)
                                last.then_inc(turned, 1)
                            if s == 3:
                                pe.wait_ge(kct_kept, 1)
                            if 3 <= s < N + 3:
                                turn(s - 3)
                            if s >= 4:
                                values(s - 4)

                    @block.scalar
                    def _(act):
                        def sigmoids(s):
                            m, h, k0, nk, first, last_ = steps[s]
                            R = rows_of(m)
                            act.wait_ge(z_ready, s + 1)
                            if s >= 3:
                                act.wait_ge(prod_ready, s - 2)
                            act.activation(keepb[0:R, s % 3, 0:nk], b_z[0:R, s % 2, 0:nk], ACT.Sigmoid, scale=-SCALE).then_inc(keep_ready, 1)
                            if s >= 4:
                                act.wait_ge(wt_ready, s - 3)
                            act.activation(beta[0:R, s % 4, 0:nk], b_z[0:R, s % 2, 0:nk], ACT.Sigmoid, scale=SCALE).then_inc(beta_ready, 1)

                        def keep(s):
                            keep_weights(act, s, lambda o, i: act.activation(o, i, ACT.Copy))

                        def keep_keys(g):
                            act.wait_ge(krow_turned, g + 1)
                            if g < 2:
                                act.wait_ge(side.stored[g], 16 * ((side.units + 1 - g) // 2))
                            else:
                                act.wait_ge(krow_out[g % 2], krow_transfers(g % 2, g))
                            width = VBW * len(key_group(g))
                            act.activation(side.stage[:, g % 2, 0:width], side.acc[:, g % 2, 0:width], ACT.Copy).then_inc(krow_kept, 1)

                        for s in range(N + 4):
                            if s >= 4 and s % 2:
                                keep(s - 4)
                            if s < N:
                                sigmoids(s)
                                for n in side_units(s):
                                    side.keep(act, n)
                                if 0 <= s - (N - TAIL) < GROUPS:
                                    keep_keys(s - (N - TAIL))

                    @block.gpsimd
                    def _(pool):
                        def store_outputs(b, tiles_done):
                            c0, w = BLOCKS[b]
                            pool.wait_ge(o_kept, 2 * tiles_done)
                            pool.dma_start(mix[4:6, :, c0:c0 + w].rearrange("k p t -> p k t"), reg[:, QS:QS + 2, c0:c0 + w]).then_inc(o_stored, 16)

                        for s, (m, h, k0, nk, first, last_) in enumerate(steps):
                            if first and h == 0 and m > 1 and m % 4 == 1:
                                store_outputs(m // 4 - 1, m - 1)
                            R = rows_of(m)
                            pool.wait_ge(prod_ready, s + 1)
                            pool.wait_ge(beta_ready, s + 1)
                            w = beta[0:R, s % 4, 0:nk]
                            pool.tensor_tensor(w, w, prod[0:R, rowno[s] % 2, k0 + 1:k0 + nk + 1], ALU.mult).then_inc(w_ready, 1)
                        store_outputs(NBLK - 1, TILES + 1)
                        pool.wait_ge(o_stored, 16 * NBLK)

                    @block.vector
                    def _(dve):
                        def scan(s):
                            m, h, k0, nk, first, last_ = steps[s]
                            R, row = rows_of(m), rowno[s]
                            if first:
                                if row >= 2:
                                    dve.wait_ge(w_ready, row_end[row - 2])
                                dve.memset(prod[0:R, row % 2, k0 + nk:k0 + nk + 1], 1.0).then_inc(one_ready, 1)
                                dve.wait_ge(one_ready, row + 1)
                            else:
                                dve.wait_ge(prod_ready, s)
                            dve.wait_ge(keep_ready, s + 1)
                            kv = keepb[0:R, s % 3, 0:nk][:, ::-1]
                            dve.tensor_tensor_scan(prod[0:R, row % 2, k0:k0 + nk][:, ::-1], kv, kv, prod[0:R, row % 2, k0 + nk:k0 + nk + 1],
                                                   ALU.mult, ALU.bypass).then_inc(prod_ready, 1)

                        def keep_out(pair):
                            m, a = pair // 2, pair % 2
                            q0, cnt = (SROW, NSAMP) if m == TILES else (m * P, SP0 if m == LAST else P)
                            dve.tensor_copy(reg[:, QS + a, q0:q0 + cnt], b_o[:, pair % 2, 0:cnt]).then_inc(o_kept, 1)

                        for s in range(N + 5):
                            if s == 2:
                                dve.wait_ge(turned, 1)
                                dve.tensor_copy(kcT[:, :, :], b_w[:, 0, :, :].rearrange("p (a t) k -> p a (t k)", a=2)).then_inc(kct_kept, 1)
                            if s >= 4 and s - 4 < N and s % 2 == 0:
                                keep_weights(dve, s - 4, lambda o, i: dve.tensor_copy(o, i))
                            if s < N:
                                scan(s)
                                for n in side_units(s):
                                    side.gate(dve, n)
                            if s >= 5:
                                e = s - 5
                                if steps[e][5] and steps[e][1] % 2:
                                    dve.wait_ge(o_ready, e + 1)
                                    keep_out(rowno[e] // 2)

        def output():
            MIX0, Z0 = D, D + 3 * P
            with ExitStack() as st:
                whi, wlo = (sb(n, [P, KT, D], F32R, st=st) for n in ("whi", "wlo"))
                mhi, mlo = (sb(n, [P, 3, KT, P], F32R, st=st) for n in ("mhi", "mlo"))
                zsig = sb("zsig", [P, 3, RAWZ, P], st=st)
                gpost = sb("gpost", [P, D], st=st)
                xres = sb("xres", [P, 3, D], st=st)
                ssq, lnv, rstd = (sb(n, [P, 3], st=st) for n in ("ssq", "lnv", "rstd"))
                yy = sb("yy", [P, 3, D], st=st)
                b_y = pb("b_y", [P, 3, D], st)
                mix_in, x_in, y_out = ([sem(f"{n}{i}", st) for i in range(3)] for n in ("mix_in", "x_in", "y_out"))
                names = "gpost_in w_hi w_lo z_sig z_gated gated m_hi m_lo y_ready sq_done ln_done rstd_done normed summed".split()
                (gpost_in, w_hi, w_lo, z_sig, z_gated, gated, m_hi, m_lo, y_ready, sq_done, ln_done, rstd_done, normed,
                 summed) = (sem(n, st) for n in names)
                xp, yp = io["x_prompt"][0], io["y_prompt"][0]
                LOOPS = (TILES - 8) // 3
                SPLIT0 = 5
                mtile = lambda s: hT[:, :, MIX0 + s * P:MIX0 + (s + 1) * P]
                ztile = lambda s, k: hT[:, 0:k, Z0 + s * P:Z0 + (s + 1) * P]
                exact = lambda n: isinstance(n, int)

                def rows(ap, n, base):
                    return ap[bass.ds(n * P + base, P), :]

                def steps(eng, step):
                    def written_out(n):
                        step(lambda d: (n + d, (n + d) % 3, (n + d) // 3), lambda d: n + d < TILES)

                    for n in range(3):
                        written_out(n)
                    with eng.Fori(0, LOOPS) as i:
                        for u in range(3):
                            step(lambda d: (3 * i + (u + 3 + d), (u + d) % 3, i + (1 + (u + d) // 3)), lambda d: True)
                    for n in range(3 * LOOPS + 3, TILES):
                        written_out(n)

                def reuse(eng, semaphore, n):
                    if not exact(n) or n >= 3:
                        eng.wait_ge(semaphore, n - 2)

                with nc.Block() as block:
                    @block.sync
                    def _(sp):
                        def load(n, s, q):
                            c = slice(n * P, (n + 1) * P) if exact(n) else bass.ds(n * P, P)
                            reuse(sp, m_lo, n)
                            sp.dma_start(mtile(s), mix[:, :, c].rearrange("k p t -> p k t")).then_inc(mix_in[s], 16)
                            sp.dma_start(ztile(s, KT), sz[:, :, c].rearrange("k p t -> p k t")).then_inc(mix_in[s], 16)
                            reuse(sp, summed, n)
                            if exact(n) and n == 0:
                                sp.dma_start(xres[CH:P, s, :], xp[0:CH, :]).then_inc(x_in[s], 32)
                            elif exact(n) and n == LAST:
                                sp.dma_start(xres[0:SP0, s, :], xp[SEQ - SP0:SEQ, :]).then_inc(x_in[s], 16)
                                sp.dma_start(xres[SP0:SP0 + NSAMP, s, :], io["x_sample"][0]).then_inc(x_in[s], 16)
                            else:
                                sp.dma_start(xres[:, s, :], rows(xp, n, -CH)).then_inc(x_in[s], 32)

                        def step(ahead, has):
                            n, s, q = ahead(0)
                            if exact(n) and n == 1:
                                sp.dma_start(gpost[:, :], io["norm_post"].to_broadcast([P, D])).then_inc(gpost_in, 16)
                            load(n, s, q)

                        steps(sp, step)

                    @block.tensor
                    def _(pe):
                        def step(ahead, has):
                            n, s, q = ahead(0)
                            pe.wait_ge(m_lo, n + 1)
                            reuse(pe, normed, n)
                            for c in range(2):
                                cols = slice(c * 512, (c + 1) * 512)
                                for k in range(KT):
                                    if exact(n) and n == 0 and c == 0:
                                        pe.wait_ge(w_lo, k + 1)
                                    for p, (m_, w_) in enumerate(((mhi, whi), (mhi, wlo), (mlo, whi))):
                                        last = pe.matmul(b_y[:, s, cols], m_[:, s, k, :], w_[:, k, cols],
                                                         start=(k == 0 and p == 0), stop=(k == KT - 1 and p == 2))
                            last.then_inc(y_ready, 1)

                        steps(pe, step)

                    @block.scalar
                    def _(act):
                        def z_sigmoid(n, s, q):
                            act.wait_ge(mix_in[s], 32 * q + 32)
                            reuse(act, z_gated, n)
                            act.activation(zsig[:, s], ztile(s, RAWZ), ACT.Sigmoid).then_inc(z_sig, 1)

                        def high(n, s, q):
                            act.wait_ge(gated, n + 1)
                            reuse(act, y_ready, n)
                            act.activation(mhi[:, s], mtile(s), ACT.Copy).then_inc(m_hi, 1)

                        def inverse_rms(n, s, q):
                            act.wait_ge(y_ready, n + 1)
                            if not exact(n) or n >= 3:
                                act.wait_ge(y_out[s], 32 * q)
                            act.activation(yy[:, s], b_y[:, s, :], ACT.Square, accum_out=ssq[:, s:s + 1]).then_inc(sq_done, 1)
                            act.wait_ge(sq_done, n + 1)
                            act.activation(lnv[:, s:s + 1], ssq[:, s:s + 1], ACT.Ln, bias=eps, scale=1.0 / D).then_inc(ln_done, 1)
                            act.wait_ge(ln_done, n + 1)
                            act.activation(rstd[:, s:s + 1], lnv[:, s:s + 1], ACT.Exp, scale=-0.5).then_inc(rstd_done, 1)

                        def step(ahead, has):
                            if has(2):
                                z_sigmoid(*ahead(2))
                            if has(1):
                                high(*ahead(1))
                            inverse_rms(*ahead(0))

                        for k in range(KT):
                            act.activation(whi[:, k, :], hT[:, k, 0:D], ACT.Copy).then_inc(w_hi, 1)
                            if k == SPLIT0 - 1:
                                z_sigmoid(0, 0, 0)
                            if k == SPLIT0:
                                high(0, 0, 0)
                        z_sigmoid(1, 1, 0)
                        steps(act, step)

                    @block.vector
                    def _(dve):
                        def gate(n, s, q):
                            dve.wait_ge(mix_in[s], 32 * q + 32)
                            dve.wait_ge(z_gated, n + 1)
                            dve.tensor_tensor(mtile(s), mtile(s), ztile(s, KT), ALU.mult).then_inc(gated, 1)

                        def low(n, s, q):
                            dve.wait_ge(m_hi, n + 1)
                            dve.tensor_tensor(mlo[:, s], mtile(s), mhi[:, s].bitcast(F32), ALU.subtract).then_inc(m_lo, 1)

                        def norm(n, s, q):
                            dve.wait_ge(rstd_done, n + 1)
                            dve.scalar_tensor_tensor(out=yy[:, s], in0=b_y[:, s, :], scalar=rstd[:, s:s + 1], in1=gpost[:, :],
                                                     op0=ALU.mult, op1=ALU.mult).then_inc(normed, 1)

                        def step(ahead, has):
                            if has(1):
                                gate(*ahead(1))
                                low(*ahead(1))
                            norm(*ahead(0))

                        for k in range(KT):
                            dve.wait_ge(w_hi, k + 1)
                            dve.tensor_tensor(wlo[:, k, :], hT[:, k, 0:D], whi[:, k, :].bitcast(F32), ALU.subtract).then_inc(w_lo, 1)
                            if k == SPLIT0 - 1:
                                gate(0, 0, 0)
                            if k == SPLIT0:
                                low(0, 0, 0)
                        dve.wait_ge(gpost_in, 16)
                        steps(dve, step)

                    @block.gpsimd
                    def _(pool):
                        def z_gate(n, s, q):
                            pool.wait_ge(z_sig, n + 1)
                            pool.tensor_tensor(ztile(s, RAWZ), ztile(s, RAWZ), zsig[:, s], ALU.mult).then_inc(z_gated, 1)

                        def result(n, s, q):
                            part = slice(CH, P) if exact(n) and n == 0 else slice(0, SP0 + NSAMP if exact(n) and n == LAST else P)
                            if exact(n) and n == 0:
                                pool.wait_ge(z_gated, 3)
                            pool.wait_ge(normed, n + 1)
                            pool.wait_ge(x_in[s], 32 * q + 32)
                            pool.tensor_tensor(yy[part, s], yy[part, s], xres[part, s, :], ALU.add).then_inc(summed, 1)
                            pool.wait_ge(summed, n + 1)
                            if exact(n) and n == 0:
                                pool.dma_start(yp[0:CH, :], yy[CH:P, 0]).then_inc(y_out[s], 32)
                            elif exact(n) and n == LAST:
                                pool.dma_start(yp[SEQ - SP0:SEQ, :], yy[0:SP0, s]).then_inc(y_out[s], 16)
                                pool.dma_start(io["y_sample"][0], yy[SP0:SP0 + NSAMP, s]).then_inc(y_out[s], 16)
                            else:
                                pool.dma_start(rows(yp, n, -CH), yy[:, s]).then_inc(y_out[s], 32)

                        def step(ahead, has):
                            if has(2):
                                z_gate(*ahead(2))
                            result(*ahead(0))

                        z_gate(0, 0, 0)
                        z_gate(1, 1, 0)
                        steps(pool, step)
                        for s in range(3):
                            pool.wait_ge(y_out[s], 32 * len([n for n in range(TILES) if n % 3 == s]))

        def stage(work, *args, **kwargs):
            with nc.cleanup_on_exit():
                work(*args, **kwargs)

        stage(norm_and_transpose)
        with ExitStack() as st:
            cx = {n: sb("cx_" + n, [P, TILES, 4], st=st) for n in ("g", "ngc", "beta", "eg", "neg_eg", "ekd")}
            cx["gl"] = sb("cx_gl", [P, TILES, 2, 2], st=st)
            cx["S"] = sb("cx_S", [P, 2, 2, HD], st=st)
            stage(conv_and_gates, cx)
            pair = lambda c0, g: [(c0 + g * HD, HD), (c0 + (AG + g) * HD, HD)]
            tile = lambda c0: [(c0, P)]
            qk_tiles = [pair(QA, g) for g in range(AG)] + [tile(c) for c in (KA, QB, QB + P, KB, KB + P)]
            z_tiles = [(segs, sz[n]) for n, segs in enumerate([pair(ZZ, g) for g in range(AG)] + [tile(ZZ + AH * HD + i * P) for i in range(4)])]
            stage(delta_net, cx, [(segs, uT[n]) for n, segs in enumerate(qk_tiles)] + z_tiles[0:RAWZ])
        stage(window_attention)
        stage(stick_breaking, z_tiles[RAWZ:])
        mixers.close()
        stage(output)


_INS = ["x_prompt", "x_sample", "cache_a_k", "cache_a_v", "cache_b_k", "cache_b_v", "state_c_conv", "state_c_ssm", "meta_tokens",
        "norm_pre", "norm_post", "w_in", "w_out", "sinks_a", "conv_c", "a_log_c", "dt_bias_c", "onorm_c"]
_OUTS = [("y_prompt", (1, SEQ, D)), ("y_sample", (1, NSAMP, D)),
         ("p_a_k", (1, 1, WIN, AKV, HD)), ("p_a_v", (1, 1, WIN, AKV, HD)),
         ("p_b_k", (1, 1, NMETA + SEQ, BH, HD)), ("p_b_v", (1, 1, NMETA + SEQ, BH, HD)),
         ("p_c_conv", (1, 1, 3, 768)), ("p_c_ssm", (1, 1, CHD, HD, HD)),
         ("s_a_k", (1, 1, WIN, AKV, HD)), ("s_a_v", (1, 1, WIN, AKV, HD)),
         ("s_b_k", (1, 1, NSAMP, BH, HD)), ("s_b_v", (1, 1, NSAMP, BH, HD)),
         ("s_c_conv", (1, 1, 3, 768)), ("s_c_ssm", (1, 1, CHD, HD, HD))]


def build(nc, arrays):
    io = {}
    for name, a in arrays.items():
        io[name] = nc.dram_tensor("in_" + name, a.shape, mybir.dt.from_np(a.dtype), kind="ExternalInput").ap()
    for name, shape in _OUTS:
        io[name] = nc.dram_tensor("out_" + name, shape, F32, kind="ExternalOutput").ap()
    for name, tiles in (("mix", KT), ("uT", 9), ("sz", KT)):
        io[name] = nc.dram_tensor(name + "_scratch", (tiles, P, T), F32, kind="Internal").ap()
    stream_layer(nc, io)


def kernel(**inputs):
    import concourse.bacc as bacc
    from concourse.bass_utils import run_bass_kernel_spmd as run
    arrays = {name: np.ascontiguousarray(inputs[name]) for name in _INS}
    arrays["cf"], arrays["cb"] = shape_constants()
    nc = bacc.Bacc("TRN2", target_bir_lowering=False, num_devices=1)
    build(nc, arrays)
    r = run(nc, [{"in_" + n: a for n, a in arrays.items()}], core_ids=[0])
    return tuple(r.results[0]["out_" + name] for name, _ in _OUTS)
```
